# Optimizing a Trainium2 kernel written in Bass

```python
import jax, jax.numpy as jnp
from jax import lax
import numpy as np
import jax
import jax.numpy as jnp

D_MODEL = 1024
BATCH = 1
SEQ = 512
DEPTH = 2

CHUNK = 64
N_MIXERS = 2
POOL_WINDOWS = (2, 4, 8, 16)
N_POOL_GROUPS = len(POOL_WINDOWS)
POOL_GROUP_DIM = D_MODEL // N_POOL_GROUPS
CONV_WIDTH = 3
D_FF = ((8 * D_MODEL // 3 + 255) // 256) * 256
N_SUB = 3
N_MOD = 3
RMS_EPS = 1e-6
N_POOL_LAYERS = (DEPTH + 1) // 2
N_CONV_LAYERS = DEPTH // 2


def rms_norm(x, g):
    xf = x.astype(jnp.float32)
    y = xf * lax.rsqrt(jnp.mean(xf * xf, axis=-1, keepdims=True) + RMS_EPS)
    return (y * g.astype(jnp.float32)).astype(x.dtype)

def modulate(h, shift, scale):
    return h * (1 + scale[:, None, :]) + shift[:, None, :]

def swiglu(h, w_in, w_out):
    a, b = jnp.split(h @ w_in, 2, axis=-1)
    return (jax.nn.silu(a) * b) @ w_out

def pool_mixer(h, w_grp, scale):
    B, T, D = h.shape
    hg = h.reshape(B, T, N_POOL_GROUPS, POOL_GROUP_DIM)
    cs = jnp.cumsum(hg.astype(jnp.float32), axis=1)
    pos = jnp.arange(1, T + 1, dtype=jnp.float32)
    pooled = []
    for g, w in enumerate(POOL_WINDOWS):
        csg = cs[:, :, g]
        lag = jnp.pad(csg, ((0, 0), (w, 0), (0, 0)))[:, :T]
        cnt = jnp.minimum(pos, float(w))[None, :, None]
        pooled.append((csg - lag) / cnt)
    pooled = jnp.stack(pooled, axis=2).astype(h.dtype)
    mixed = pooled - hg
    y = jnp.einsum('btgc,gcd->btgd', mixed, w_grp).reshape(B, T, D)
    return y * scale

def conv_mixer(h, w_in, w_conv, w_out):
    D = h.shape[-1]
    b_gate, c_gate, v = jnp.split(h @ w_in, 3, axis=-1)
    u = c_gate * v
    conv = lax.conv_general_dilated(
        u, w_conv[:, None, :].astype(u.dtype),
        window_strides=(1,),
        padding=[(CONV_WIDTH - 1, 0)],
        dimension_numbers=('NWC', 'WIO', 'NWC'),
        feature_group_count=D)
    return (b_gate * conv) @ w_out

def first_inputs(seed: int = 0) -> dict:
    key = jax.random.key(seed)
    ks = jax.random.split(key, 14)
    f32 = jnp.float32
    x = jax.random.normal(ks[0], (BATCH, SEQ, D_MODEL), f32)
    c = jax.random.normal(ks[1], (BATCH, D_MODEL), f32)
    ada_w = jax.random.normal(ks[2], (DEPTH, D_MODEL, N_SUB * N_MOD * D_MODEL), f32) * D_MODEL ** -0.5
    ada_b = 0.01 * jax.random.normal(ks[3], (DEPTH, N_SUB * N_MOD * D_MODEL), f32)
    norm_g = 1.0 + 0.1 * jax.random.normal(ks[4], (DEPTH, N_SUB, D_MODEL), f32)
    ffn_w_in = jax.random.normal(ks[5], (DEPTH, 2, D_MODEL, 2 * D_FF), f32) * D_MODEL ** -0.5
    ffn_w_out = jax.random.normal(ks[6], (DEPTH, 2, D_FF, D_MODEL), f32) * D_FF ** -0.5
    pool_w = jax.random.normal(ks[7], (N_POOL_LAYERS, N_POOL_GROUPS, POOL_GROUP_DIM, POOL_GROUP_DIM), f32) * POOL_GROUP_DIM ** -0.5
    pool_scale = 1.0 + 0.1 * jax.random.normal(ks[8], (N_POOL_LAYERS, D_MODEL), f32)
    conv_w_in = jax.random.normal(ks[9], (N_CONV_LAYERS, D_MODEL, 3 * D_MODEL), f32) * D_MODEL ** -0.5
    conv_w = jax.random.normal(ks[10], (N_CONV_LAYERS, CONV_WIDTH, D_MODEL), f32) * CONV_WIDTH ** -0.5
    conv_w_out = jax.random.normal(ks[11], (N_CONV_LAYERS, D_MODEL, D_MODEL), f32) * D_MODEL ** -0.5
    final_g = 1.0 + 0.1 * jax.random.normal(ks[12], (D_MODEL,), f32)
    return {"x": x, "c": c, "ada_w": ada_w, "ada_b": ada_b, "norm_g": norm_g,
            "ffn_w_in": ffn_w_in, "ffn_w_out": ffn_w_out,
            "pool_w": pool_w, "pool_scale": pool_scale,
            "conv_w_in": conv_w_in, "conv_w": conv_w, "conv_w_out": conv_w_out,
            "final_g": final_g}

def first_block(x, c, ada_w, ada_b, norm_g, ffn_w_in, ffn_w_out, pool_w, pool_scale,
              conv_w_in, conv_w, conv_w_out, final_g):
    B = x.shape[0]
    cond = jax.nn.silu(c)
    for i in range(DEPTH):
        mod = (cond @ ada_w[i] + ada_b[i]).reshape(B, N_SUB, N_MOD, D_MODEL)
        shift, scale, gate = mod[:, :, 0], mod[:, :, 1], mod[:, :, 2]

        h = modulate(rms_norm(x, norm_g[i, 0]), shift[:, 0], scale[:, 0])
        x = x + 0.5 * gate[:, 0, None, :] * swiglu(h, ffn_w_in[i, 0], ffn_w_out[i, 0])

        h = modulate(rms_norm(x, norm_g[i, 1]), shift[:, 1], scale[:, 1])
        j = i // N_MIXERS
        if i % N_MIXERS == 0:
            y = pool_mixer(h, pool_w[j], pool_scale[j])
        else:
            y = conv_mixer(h, conv_w_in[j], conv_w[j], conv_w_out[j])
        x = x + gate[:, 1, None, :] * y

        h = modulate(rms_norm(x, norm_g[i, 2]), shift[:, 2], scale[:, 2])
        x = x + 0.5 * gate[:, 2, None, :] * swiglu(h, ffn_w_in[i, 1], ffn_w_out[i, 1])
    return rms_norm(x, final_g)


DEPTH_2 = 1

GRID_W = 64
CTX_LEN = 256
HEAD_DIM = 128
N_Q_HEADS = 8
N_KV_HEADS = 2
Q_PER_KV = N_Q_HEADS // N_KV_HEADS
Q_BLOCK = 128
ROPE_THETA = 10000.0
GLA_HEADS = 4
GLA_DK = D_MODEL // (2 * GLA_HEADS)
GLA_DV = D_MODEL // GLA_HEADS
GLA_GATE_RANK = 16
GLA_GATE_NORM = 16.0
GLA_CHUNK = 64
D_FF_2 = 4 * D_MODEL
EPS = 1e-6

IN_SIZES = (
    N_KV_HEADS * HEAD_DIM,
    N_KV_HEADS * HEAD_DIM,
    GLA_HEADS * GLA_DK,
    GLA_HEADS * GLA_DV,
    GLA_GATE_RANK,
    GLA_GATE_RANK,
    N_Q_HEADS * HEAD_DIM,
    GLA_HEADS * GLA_DK,
    GLA_HEADS * GLA_DV,
    D_MODEL,
    D_MODEL,
)
N_CTX_GROUPS = 6
D_IN = int(sum(IN_SIZES))
IN_OFFSETS = tuple(int(o) for o in np.cumsum(IN_SIZES)[:-1])
CTX_COLS = int(sum(IN_SIZES[:N_CTX_GROUPS]))


def rms_norm_2(x, g):
    xf = x.astype(jnp.float32)
    y = xf * lax.rsqrt(jnp.mean(xf * xf, axis=-1, keepdims=True) + EPS)
    return (y * g.astype(jnp.float32)).astype(x.dtype)

def modulate_2(h, shift, scale):
    return h * (1 + scale[..., None, :]) + shift[..., None, :]

def split_heads(a, n_heads, d):
    return a.reshape(*a.shape[:-1], n_heads, d)

def axial_rope_tables(n_rows):
    rows = jnp.repeat(jnp.arange(n_rows), GRID_W).astype(jnp.float32)
    cols = jnp.tile(jnp.arange(GRID_W), n_rows).astype(jnp.float32)
    half = HEAD_DIM // 2
    freqs = ROPE_THETA ** (-jnp.arange(0, half, 2, dtype=jnp.float32) / half)
    ang = jnp.stack([rows[:, None] * freqs, cols[:, None] * freqs], axis=1)
    return jnp.cos(ang)[None, :, None], jnp.sin(ang)[None, :, None]

def apply_rope(x, cos, sin):
    xf = x.astype(jnp.float32).reshape(*x.shape[:-1], 2, 2, HEAD_DIM // 4)
    a, b = xf[..., 0, :], xf[..., 1, :]
    out = jnp.stack([a * cos - b * sin, b * cos + a * sin], axis=-2)
    return out.reshape(x.shape).astype(x.dtype)

def gqa_attention(q, k, v):
    b, t = q.shape[:2]
    qb = jnp.moveaxis(q.reshape(b, t // Q_BLOCK, Q_BLOCK, N_KV_HEADS, Q_PER_KV, HEAD_DIM), 1, 0)

    def one_block(q_blk):
        s = jnp.einsum('bqhgd,bkhd->bhgqk', q_blk, k, preferred_element_type=jnp.float32) * (HEAD_DIM ** -0.5)
        p = jax.nn.softmax(s, axis=-1).astype(v.dtype)
        return jnp.einsum('bhgqk,bkhd->bqhgd', p, v)

    o = lax.map(one_block, qb)
    return jnp.moveaxis(o, 0, 1).reshape(b, t, N_Q_HEADS * HEAD_DIM)

def gla_heads(a, d):
    return jnp.moveaxis(split_heads(a.astype(jnp.float32), GLA_HEADS, d), 2, 1)

def gla_log_decay(lowrank, w_gk, b_gk):
    g = jax.nn.log_sigmoid((lowrank @ w_gk + b_gk).astype(jnp.float32)) / GLA_GATE_NORM
    return gla_heads(g, GLA_DK)

def flip_t(a):
    return a[:, :, ::-1]

def gla_chunked(q, k, v, g, s0):
    b_, h_, t, _ = q.shape
    n = t // GLA_CHUNK

    def to_chunks(a):
        return jnp.moveaxis(a.reshape(b_, h_, n, GLA_CHUNK, a.shape[-1]), 2, 0)

    mask = jnp.tril(jnp.ones((GLA_CHUNK, GLA_CHUNK), dtype=bool))[:, :, None]

    def step(state, inp):
        qc, kc, vc, gc = inp
        b = jnp.cumsum(gc, axis=2)
        o_inter = jnp.einsum('bhid,bhde->bhie', qc * jnp.exp(b), state)
        diff = jnp.where(mask, b[:, :, :, None, :] - b[:, :, None, :, :], -jnp.inf)
        a = jnp.einsum('bhid,bhjd,bhijd->bhij', qc, kc, jnp.exp(diff))
        o = o_inter + jnp.einsum('bhij,bhje->bhie', a, vc)
        b_last = b[:, :, -1:, :]
        state = jnp.exp(b_last[:, :, 0, :])[..., None] * state + jnp.einsum('bhjd,bhje->bhde', kc * jnp.exp(b_last - b), vc)
        return state, o

    s_fin, o = lax.scan(step, s0, (to_chunks(q), to_chunks(k), to_chunks(v), to_chunks(g)))
    o = jnp.moveaxis(o, 0, 2).reshape(b_, h_, t, v.shape[-1])
    return o, s_fin

def gla_final_state(k, v, g):
    b = jnp.cumsum(g, axis=2)
    return jnp.einsum('bhtd,bhte->bhde', k * jnp.exp(b[:, :, -1:] - b), v)

def gla_output(o, gate, g_norm):
    o = jnp.moveaxis(o, 1, 2)
    y = rms_norm_2(o, g_norm) * jax.nn.silu(split_heads(gate, GLA_HEADS, GLA_DV).astype(jnp.float32))
    return y.reshape(*y.shape[:2], GLA_HEADS * GLA_DV).astype(gate.dtype)

def branch_merge(attn, gla, gate_a, gate_g, w_br_attn, w_br_gla, w_out):
    y = jax.nn.sigmoid(gate_a) * (attn @ w_br_attn) + jax.nn.sigmoid(gate_g) * (gla @ w_br_gla)
    return y @ w_out

def sq_relu_mlp(h, w1, w2):
    return jnp.square(jax.nn.relu(h @ w1)) @ w2

def hybrid_layer(x, ctx, mod_x, mod_c, rope, norm1, w_in, q_norm, k_norm, w_gk_fwd, b_gk_fwd,
                 w_gk_bwd, b_gk_bwd, gla_norm, w_br_attn, w_br_gla, w_out, norm2, w_mlp1, w_mlp2,
                 update_ctx):
    cos, sin = rope
    sh1, sc1, gt1, sh2, sc2, gt2 = mod_x
    bsz = x.shape[0]
    hx = modulate_2(rms_norm_2(x, norm1), sh1, sc1)
    hc = modulate_2(rms_norm_2(ctx, norm1), mod_c[0], mod_c[1])
    ak, av, gk, gv, lrf, lrb, aq, gq, go, ga, gg = jnp.split(hx @ w_in, IN_OFFSETS, axis=-1)
    if update_ctx:
        ak_c, av_c, gk_c, gv_c, lrf_c, lrb_c, aq_c, gq_c, go_c, ga_c, gg_c = jnp.split(hc @ w_in, IN_OFFSETS, axis=-1)
    else:
        ak_c, av_c, gk_c, gv_c, lrf_c, lrb_c = jnp.split(hc @ w_in[:, :CTX_COLS], IN_OFFSETS[:N_CTX_GROUPS - 1], axis=-1)

    qx = apply_rope(rms_norm_2(split_heads(aq, N_Q_HEADS, HEAD_DIM), q_norm), cos, sin)
    kx = apply_rope(rms_norm_2(split_heads(ak, N_KV_HEADS, HEAD_DIM), k_norm), cos, sin)
    vx = split_heads(av, N_KV_HEADS, HEAD_DIM)
    kc = rms_norm_2(split_heads(ak_c, N_KV_HEADS, HEAD_DIM), k_norm)
    vc = split_heads(av_c, N_KV_HEADS, HEAD_DIM)
    attn_x = gqa_attention(qx, jnp.concatenate([kx, kc], axis=1), jnp.concatenate([vx, vc], axis=1))

    kgc, vgc = gla_heads(gk_c, GLA_DK), gla_heads(gv_c, GLA_DV)
    gfc = gla_log_decay(lrf_c, w_gk_fwd, b_gk_fwd)
    gbc = gla_log_decay(lrb_c, w_gk_bwd, b_gk_bwd)
    if update_ctx:
        zeros = jnp.zeros((bsz, GLA_HEADS, GLA_DK, GLA_DV), jnp.float32)
        qgc = gla_heads(gq_c, GLA_DK) * (GLA_DK ** -0.5)
        oc_f, s_f = gla_chunked(qgc, kgc, vgc, gfc, zeros)
        oc_b, s_b = gla_chunked(flip_t(qgc), flip_t(kgc), flip_t(vgc), flip_t(gbc), zeros)
    else:
        s_f = gla_final_state(kgc, vgc, gfc)
        s_b = gla_final_state(flip_t(kgc), flip_t(vgc), flip_t(gbc))
    qgx = gla_heads(gq, GLA_DK) * (GLA_DK ** -0.5)
    kgx, vgx = gla_heads(gk, GLA_DK), gla_heads(gv, GLA_DV)
    gfx = gla_log_decay(lrf, w_gk_fwd, b_gk_fwd)
    gbx = gla_log_decay(lrb, w_gk_bwd, b_gk_bwd)
    ox_f, _ = gla_chunked(qgx, kgx, vgx, gfx, s_f)
    ox_b, _ = gla_chunked(flip_t(qgx), flip_t(kgx), flip_t(vgx), flip_t(gbx), s_b)
    gla_x = gla_output(ox_f + flip_t(ox_b), go, gla_norm)

    x = x + gt1[..., None, :] * branch_merge(attn_x, gla_x, ga, gg, w_br_attn, w_br_gla, w_out)
    x = x + gt2[..., None, :] * sq_relu_mlp(modulate_2(rms_norm_2(x, norm2), sh2, sc2), w_mlp1, w_mlp2)

    if update_ctx:
        _, _, gt1c, sh2c, sc2c, gt2c = mod_c
        qc = rms_norm_2(split_heads(aq_c, N_Q_HEADS, HEAD_DIM), q_norm)
        attn_c = gqa_attention(qc, kc, vc)
        gla_c = gla_output(oc_f + flip_t(oc_b), go_c, gla_norm)
        ctx = ctx + gt1c[..., None, :] * branch_merge(attn_c, gla_c, ga_c, gg_c, w_br_attn, w_br_gla, w_out)
        ctx = ctx + gt2c[..., None, :] * sq_relu_mlp(modulate_2(rms_norm_2(ctx, norm2), sh2c, sc2c), w_mlp1, w_mlp2)
    return x, ctx

def second_inputs(seed: int = 0) -> dict:
    key = jax.random.key(seed)
    ks = jax.random.split(key, 24)
    f32 = jnp.float32

    def nrm(k, shape, scale=1.0):
        return jax.random.normal(k, shape, f32) * scale

    L, D = DEPTH_2, D_MODEL
    return {
        'x': nrm(ks[0], (BATCH, SEQ, D)),
        'c': nrm(ks[1], (BATCH, D)),
        'ctx': nrm(ks[2], (BATCH, CTX_LEN, D)),
        'c_ctx': nrm(ks[3], (D,)),
        'w_ada': nrm(ks[4], (L, D, 6 * D), 0.5 * D ** -0.5),
        'b_ada': nrm(ks[5], (L, 6 * D), 0.02),
        'norm1': 1.0 + nrm(ks[6], (L, D), 0.02),
        'w_in': nrm(ks[7], (L, D, D_IN), D ** -0.5),
        'q_norm': 1.0 + nrm(ks[8], (L, HEAD_DIM), 0.02),
        'k_norm': 1.0 + nrm(ks[9], (L, HEAD_DIM), 0.02),
        'w_gk_fwd': nrm(ks[10], (L, GLA_GATE_RANK, GLA_HEADS * GLA_DK), GLA_GATE_RANK ** -0.5),
        'b_gk_fwd': nrm(ks[11], (L, GLA_HEADS * GLA_DK), 0.1),
        'w_gk_bwd': nrm(ks[12], (L, GLA_GATE_RANK, GLA_HEADS * GLA_DK), GLA_GATE_RANK ** -0.5),
        'b_gk_bwd': nrm(ks[13], (L, GLA_HEADS * GLA_DK), 0.1),
        'gla_norm': 1.0 + nrm(ks[14], (L, GLA_DV), 0.02),
        'w_br_attn': nrm(ks[15], (L, N_Q_HEADS * HEAD_DIM, D), (N_Q_HEADS * HEAD_DIM) ** -0.5),
        'w_br_gla': nrm(ks[16], (L, GLA_HEADS * GLA_DV, D), (GLA_HEADS * GLA_DV) ** -0.5),
        'w_out': nrm(ks[17], (L, D, D), D ** -0.5),
        'norm2': 1.0 + nrm(ks[18], (L, D), 0.02),
        'w_mlp1': nrm(ks[19], (L, D, D_FF_2), D ** -0.5),
        'w_mlp2': nrm(ks[20], (L, D_FF_2, D), D_FF_2 ** -0.5),
    }

def second_block(x, c, ctx, c_ctx, w_ada, b_ada, norm1, w_in, q_norm, k_norm, w_gk_fwd, b_gk_fwd,
              w_gk_bwd, b_gk_bwd, gla_norm, w_br_attn, w_br_gla, w_out, norm2, w_mlp1, w_mlp2):
    ROWS = x.shape[1] // GRID_W
    rope = axial_rope_tables(ROWS)
    for l in range(DEPTH_2):
        update_ctx = l < DEPTH_2 - 1
        n_mod = 6 if update_ctx else 2
        mod_x = jnp.split(jax.nn.silu(c) @ w_ada[l] + b_ada[l], 6, axis=-1)
        mod_c = jnp.split(jax.nn.silu(c_ctx) @ w_ada[l][:, :n_mod * D_MODEL] + b_ada[l][:n_mod * D_MODEL], n_mod, axis=-1)
        x, ctx = hybrid_layer(x, ctx, mod_x, mod_c, rope, norm1[l], w_in[l], q_norm[l], k_norm[l],
                              w_gk_fwd[l], b_gk_fwd[l], w_gk_bwd[l], b_gk_bwd[l], gla_norm[l],
                              w_br_attn[l], w_br_gla[l], w_out[l], norm2[l], w_mlp1[l], w_mlp2[l],
                              update_ctx)
    return x


def setup_inputs(seed=0):
    out = dict(first_inputs(seed))
    for name, value in second_inputs(seed + 1).items():
        if name != "x":
            out[name + "_2"] = value
    return out


def reference(
    x, c, ada_w, ada_b, norm_g, ffn_w_in, ffn_w_out, pool_w, pool_scale, conv_w_in, conv_w,
    conv_w_out, final_g, c_2, ctx_2, c_ctx_2, w_ada_2, b_ada_2, norm1_2, w_in_2, q_norm_2,
    k_norm_2, w_gk_fwd_2, b_gk_fwd_2, w_gk_bwd_2, b_gk_bwd_2, gla_norm_2, w_br_attn_2,
    w_br_gla_2, w_out_2, norm2_2, w_mlp1_2, w_mlp2_2,
):
    x = first_block(
        x, c, ada_w, ada_b, norm_g, ffn_w_in, ffn_w_out, pool_w, pool_scale, conv_w_in, conv_w,
        conv_w_out, final_g,
    )
    return second_block(
        x, c_2, ctx_2, c_ctx_2, w_ada_2, b_ada_2, norm1_2, w_in_2, q_norm_2, k_norm_2,
        w_gk_fwd_2, b_gk_fwd_2, w_gk_bwd_2, b_gk_bwd_2, gla_norm_2, w_br_attn_2, w_br_gla_2,
        w_out_2, norm2_2, w_mlp1_2, w_mlp2_2,
    )


_drawn_inputs = setup_inputs


def setup_inputs(seed=0):
    import zlib

    import numpy as np

    out = dict(_drawn_inputs(seed))
    spreads = {}
    factors = {'ctx_2': 3.956,
     'c_ctx_2': 3.236,
     'norm1_2': 8.0,
     'q_norm_2': 8.0,
     'k_norm_2': 8.0,
     'w_gk_fwd_2': 5.098,
     'b_gk_fwd_2': 22.434,
     'w_gk_bwd_2': 4.707,
     'b_gk_bwd_2': 21.472,
     'gla_norm_2': 23.188,
     'norm2_2': 16.267}
    for name, (base, spread) in spreads.items():
        noise = np.random.default_rng([zlib.crc32(name.encode()), seed]).standard_normal(out[name].shape)
        drawn = base * np.exp(spread * noise) if base else spread * noise
        out[name] = jnp.asarray(drawn.astype(out[name].dtype))
    for name, factor in factors.items():
        out[name] = (out[name] * factor).astype(out[name].dtype)
    return out
```

```python
from contextlib import ExitStack

import numpy as np

import concourse.bass as bass
from concourse import mybir

P = 128
D = 1024
KD = D // P
T = 512
TC = 256
TA = T + TC
F = 2816
FH = F // P // 2
EPS = 1e-6
POOL_WINDOWS = (2, 4, 8, 16)
CONV_WIDTH = 3
HD = 128
NQ = 8
NKV = 2
GH_ = 4
DK = 128
DV = 256
RANK = 16
CH = 128
NC_ = T // CH
GRID_W = 64
F2 = 4096
LEVELS = (1, 2, 4, 8, 16, 32, 64)

ALU = mybir.AluOpType
ACT = mybir.ActivationFunctionType
F32 = mybir.dt.float32
F32R = mybir.dt.float32r
I32 = mybir.dt.int32
AX = mybir.AxisListType

IN_SIZES = (NKV * HD, NKV * HD, GH_ * DK, GH_ * DV, RANK, RANK, NQ * HD, GH_ * DK, GH_ * DV, D, D)
(C_AK, C_AV, C_GK, C_GV, C_LR, _, C_AQ, C_GQ, C_GO, C_GA, C_GG) = (
    int(x) for x in np.cumsum((0,) + IN_SIZES)[:-1])

VEC_ROWS = {}
_at = 0
for _name, _rows in (("c", 8), ("c_2", 8), ("c_ctx_2", 8), ("ada_b", 144), ("norm_g", 48),
                     ("pool_scale", 8), ("conv_w", 24), ("final_g", 8), ("b_ada_2", 48),
                     ("norm1_2", 8), ("norm2_2", 8), ("q_norm_2", 1), ("k_norm_2", 1),
                     ("b_gk_fwd_2", 4), ("b_gk_bwd_2", 4), ("gla_norm_2", 2)):
    VEC_ROWS[_name] = (_at, _rows)
    _at += _rows
NVEC = _at
NVT = -(-NVEC // P)
N_VEC_DMAS = sum((a + n - 1) // P - a // P + 1 for a, n in VEC_ROWS.values())

IN_UNITS = FH
OUT_UNITS = KD
FFN_UNITS = 2 * (IN_UNITS + OUT_UNITS)
U_FFN = [0, FFN_UNITS + 1, 2 * FFN_UNITS + 1, 3 * FFN_UNITS + 1 + 16]
U_POOL = FFN_UNITS
U_CONV = 3 * FFN_UNITS + 1
U_B2 = 4 * FFN_UNITS + 1 + 16
U_LR = U_B2
U_G = U_LR + 1
U_K, U_V, U_Q = U_G + 3 * GH_, U_G + 3 * GH_ + 1, U_G + 3 * GH_ + 2
U_D = U_Q + NQ // 2
U_WO = U_D + 16
U_MLP = U_WO + 4
N_UNITS = U_MLP + 32
FULL = 2048
OUT_SIZE = FH * P


def unit_size(n):
    for u in U_FFN:
        for h in range(2):
            o = u + h * (IN_UNITS + OUT_UNITS) + IN_UNITS
            if o <= n < o + OUT_UNITS:
                return OUT_SIZE
    return KD * 2 * RANK if n == U_LR else FULL


def host_tables():
    ident = np.eye(P, dtype=np.float32)
    half = HD // 2
    freqs = (10000.0 ** (-np.arange(0, half, 2, dtype=np.float32) / half)).astype(np.float32)
    t = np.arange(T)
    ang = np.stack([(t // GRID_W)[:, None].astype(np.float32) * freqs,
                    (t % GRID_W)[:, None].astype(np.float32) * freqs], axis=1)
    cos = np.zeros((HD, T), np.float32)
    sin = np.zeros((HD, T), np.float32)
    perm = np.zeros((HD, HD), np.float32)
    for d in range(HD):
        ax, ab, f = d // 64, (d // 32) % 2, d % 32
        cos[d] = np.cos(ang[:, ax, f])
        sin[d] = np.sin(ang[:, ax, f]) * (1 if ab else -1)
        perm[d, d ^ 32] = 1
    masks = np.zeros((P, 2 * len(LEVELS), P), np.int32)
    j, i = np.arange(P)[:, None], np.arange(P)[None, :]
    for n, s in enumerate(LEVELS):
        same = j // (2 * s) == i // (2 * s)
        masks[:, n] = same & (j % (2 * s) < s) & (i % (2 * s) >= s)
        masks[:, len(LEVELS) + n] = same & (j % (2 * s) >= s) & (i % (2 * s) < s)
    keep = np.ones((P, T), np.float32)
    keep[:, ::CH] = 0
    pos = np.arange(16, dtype=np.float32) + 1
    edge = np.stack([np.where(pos < w, np.float32(w) / pos, 1) for w in POOL_WINDOWS])
    edge = np.broadcast_to(edge.astype(np.float32), (P, 4, 16))
    return {"t_ident": ident, "t_perm": perm, "t_cos": cos, "t_sin": sin, "t_masks": masks,
            "t_keep": keep, "t_edge": np.ascontiguousarray(edge)}


class At:

    def __init__(self, base, i=None, stride=0):
        self.base, self.i, self.stride = base, i, stride

    def __add__(self, n):
        return At(self.base + n, self.i, self.stride)

    def __sub__(self, n):
        return At(self.base - n, self.i, self.stride)

    @property
    def v(self):
        return self.base if self.i is None else self.i * self.stride + self.base

    def times(self, n):
        return At(self.base * n, self.i, self.stride * n)

    def half(self):
        return At(self.base // 2, self.i, self.stride // 2)

    @property
    def slot(self):
        return self.base % 2


def wait(eng, sem, at):
    assert at.base > 0 or at.i is None
    if at.base > 0:
        eng.wait_ge(sem, at.v)


def at(n):
    return At(n)


def spans(count, pre, post):
    out = [(n, 0) for n in range(pre)]
    pairs = (count - pre - post) // 2
    out.append((pre, pairs))
    out += [(n, 0) for n in range(pre + 2 * pairs, count)]
    return out


def each(eng, count, pre, post, step):
    for n, pairs in spans(count, pre, post):
        if pairs:
            with eng.Fori(0, pairs) as i:
                for s in range(2):
                    step(At(n + s, i, 2))
        else:
            step(At(n))


def build(nc, ins, out):
    ctx_ = ExitStack()
    with ctx_:
        def sb(name, shape, dt=F32):
            return ctx_.enter_context(nc.sbuf_tensor(name, shape, dt))

        def psum(name, shape):
            return ctx_.enter_context(nc.psum_tensor(name, shape, F32))

        def sem(name):
            return ctx_.enter_context(nc.semaphore(name))

        W_RAW = [sb(f"w_raw{s}", [P, FULL]) for s in range(2)]
        W_HI = [sb(f"w_hi{s}", [P, FULL], F32R) for s in range(2)]
        W_LO = [sb(f"w_lo{s}", [P, FULL], F32R) for s in range(2)]
        X = sb("x_res", [P, KD, T])
        H_HI = sb("h_hi", [P, KD, TA], F32R)
        H_LO = sb("h_lo", [P, KD, TA], F32R)
        IDENT = sb("ident", [P, P])
        ONES_D = sb("ones_d", [P, 2])
        ONES = sb("ones", [P, P])
        ONES_HD = sb("ones_hd", [P, 1])
        EPS_C = sb("eps_c", [P, 1])
        VECS = sb("vecs", [P, NVT * P])
        COND = sb("cond", [P, 24])
        MODS = sb("mods", [P, 8 * 24 + 16])
        GAIN = sb("gain", [P, 9 * KD])
        GATE = sb("gate", [P, 8 * KD])
        RSTD4 = sb("rstd4", [P, 8])
        DIAG = sb("diag", [P, 4, P])
        SSQ = sb("ssq", [P, T])
        FLEX_KB = 84
        FLEX = sb("flex", [P, FLEX_KB * 256])
        FLEX0 = nc.sbuf_base - FLEX_KB * 1024

        def view(name, kb, shape, dt=F32):
            return nc.alloc_sbuf_tensor_at(name, shape, dt, offset=FLEX0 + int(kb * 1024))

        G_HI = view("g_hi", 0, [P, FH, T], F32R)
        G_LO = view("g_lo", 22, [P, FH, T], F32R)
        ADA = [view(f"ada{h}", 44 + 6 * h, [P, 1536]) for h in range(2)]
        ACC = view("ada_acc", 56, [P, 3 * D])
        SA = [view(f"silu_a{s}", 68 + 2 * s, [P, T]) for s in range(2)]
        GT = [view(f"g_t{s}", 72 + 2 * s, [P, T]) for s in range(2)]
        ACC_C = view("ada_acc_ctx", 76, [P, 2 * D])
        X_ROWS = view("x_rows", 0, [P, 4, D])
        V_ROWS = view("vec_rows", 16, [P, NVT, P])
        PH = view("pool_h", 0, [P, KD, T])
        PS_A = view("pool_a", 16, [P, 2, T])
        PS_B = view("pool_b", 20, [P, 2, T])
        EDGE = view("pool_edge", 24, [P, 4, 16])
        U_T = [view(f"conv_u{s}", 32 + 3 * s, [P, T + 2]) for s in range(2)]
        C_T = [view(f"conv_c{s}", 38 + 2 * s, [P, T]) for s in range(2)]
        CV = view("conv_out", 16, [P, KD, T])
        Z_HI = view("z_hi", 0, [P, KD, T], F32R)
        Z_LO = view("z_lo", 16, [P, KD, T], F32R)

        C_ROWS = view("ctx_rows", 0, [P, 2, D])
        C_X = view("ctx_t", 8, [P, KD, TC])
        O_T = view("gla_out", 0, [P, KD, T])
        MASKS = view("masks", 16, [P, 2 * len(LEVELS), P], I32)
        KEEP = view("keep", 23, [P, T])
        LRT = view("low_rank", 25, [P, TA])
        W_GK = view("w_gk", 28, [P, 2, P])
        KT = view("gla_k", 29, [P, TA])
        QT = view("gla_q", 32, [P, T])
        V = view("gla_v", 34, [P, TA // P, DV])
        B = view("gla_b", 40, [P, TA])
        T1 = view("gla_t1", 43, [P, TA])
        T2 = view("gla_t2", 46, [P, TA])
        QB = [view(f"gla_qb{d}", 49 + 2 * d, [P, T]) for d in range(2)]
        KDT = view("gla_kdt", 53, [P, TA // P, P])
        ST = [view(f"gla_state{d}", 56 + 4 * d, [P, NC_, DV]) for d in range(2)]
        AM = view("gla_a", 64, [P, T])
        QL = [view(f"gla_ql{n}", 66 + 2 * n, [P, T]) for n in range(2)]
        KL = [view(f"gla_kl{n}", 70 + 2 * n, [P, T]) for n in range(2)]
        EL = [view(f"gla_el{n}", 74 + 2 * n, [P, T]) for n in range(2)]
        SG = [view(f"gla_sg{n}", 78 + 2 * n, [P, T]) for n in range(2)]
        AT_T = view("attn_out", 16, [P, KD, T])
        KR = view("attn_k", 32, [P, NKV, TA])
        VA = view("attn_v", 38, [P, TA // P, NKV * HD])
        K_RAW = view("attn_k_raw", 44, [P, NKV, TA])
        K_X = view("attn_k_x", 50, [P, NKV, TA])
        K_SQ = view("attn_k_sq", 56, [P, NKV, TA])
        DIAG_K = view("attn_diag", 66, [P, 12, P])
        PT = view("attn_pt", 44, [P, TA // P, T])
        PP = [view(f"attn_p{n}", 56 + 3 * n, [P, TA]) for n in range(2)]
        QX = [view(f"attn_qx{n}", 62 + 2 * n, [P, T]) for n in range(2)]
        Q_SQ = [view(f"attn_qsq{n}", 66 + 2 * n, [P, T]) for n in range(2)]
        QR = [view(f"attn_qr{n}", 66 + 2 * n, [P, T]) for n in range(2)]
        VS = view("attn_vs", 70, [P, TA // P, HD])
        COS = view("cos", 74, [P, T])
        SIN = view("sin", 76, [P, T])
        PERM = view("perm", 78, [P, P])
        TQ = [view(f"attn_tq{n}", 80 + 2 * n, [P, T]) for n in range(2)]
        A_HI = view("a_hi", 32, [P, KD, T], F32R)
        A_LO = view("a_lo", 48, [P, KD, T], F32R)
        L_HI = view("l_hi", 64, [P, KD, T], F32R)
        L_LO = view("l_lo", 16, [P, KD, T], F32R)
        Y = view("merged", 0, [P, KD, T])
        SGB = [view(f"branch_gate{n}", 80 + 2 * n, [P, T]) for n in range(2)]
        STAT = sb("stat", [P, 64])

        PS = psum("ps", [P, 8 * T])
        BANK = [PS[:, b * T:(b + 1) * T] for b in range(8)]
        WIDE = {b: PS[:, b * T:b * T + TA] for b in (0, 2, 4, 6)}

        landed = [sem(f"w_landed{s}") for s in range(2)]
        hi_done = sem("hi_done")
        lo_done = sem("lo_done")
        pe_done = sem("pe_done")
        evac_done = sem("evac_done")
        silu_made = sem("silu_made")
        g_hi_made = sem("g_hi_made")
        g_ready = sem("g_ready")
        ada_landed = [sem(f"ada_landed{h}") for h in range(2)]
        ada_used = [sem(f"ada_used{h}") for h in range(2)]
        acc_cleared = sem("acc_cleared")
        mod_summed = sem("mod_summed")
        mod_read = sem("mod_read")
        mod_done = sem("mod_done")
        const_ready = sem("const_ready")
        in_landed = sem("in_landed")
        vec_landed = sem("vec_landed")
        tab_landed = sem("tab_landed")
        vec_turned = sem("vec_turned")
        vec_ready = sem("vec_ready")
        cond_ready = sem("cond_ready")
        x_turned = sem("x_turned")
        x_made = sem("x_made")
        sq_made = sem("sq_made")
        sq_summed = sem("sq_summed")
        ms_made = sem("ms_made")
        rt_made = sem("rt_made")
        rs_made = sem("rs_made")
        diag_made = sem("diag_made")
        rb_made = sem("rb_made")
        rstd_made = sem("rstd_made")
        xr_made = sem("xr_made")
        h_made = sem("h_made")
        h_hi_made = sem("h_hi_made")
        h_ready = sem("h_ready")
        fin_made = sem("fin_made")
        pool_step = sem("pool_step")
        pool_mixed = sem("pool_mixed")
        pool_mm = sem("pool_mm")
        pool_added = sem("pool_added")
        cv_zero = sem("cv_zero")
        p_hi_made = sem("p_hi_made")
        p_ready = sem("p_ready")
        cv_c = sem("cv_c")
        cv_u = sem("cv_u")
        cv_1 = sem("cv_1")
        cv_2 = sem("cv_2")
        cv_3 = sem("cv_3")
        cz_made = sem("cz_made")
        z_hi_made = sem("z_hi_made")
        z_ready = sem("z_ready")
        (c_landed, c_turned, c_made, csq_made, csq_summed, cms_made, crt_made, crs_made, cdiag_made, crb_made, cxr_made, ch_made, tab2_landed, wgk_zero, wgk_landed, lr_made, z_made, z_out, z_min, z_exp, z_ln, g_made, b_made, kd_arg, kd_e, eb_made, kd_made, qb_made, kdt_t, kdt_made, sp_made, st_made, lv_d, lv_abs, lv_e, lv_q, lv_k, lv_mm, lv_cp, dg_mm, dg_made, o_mm, o_cp, o_sq, o_ms, o_rt, o_rs, o_diag, o_rb, o_xr, o_done, sg_made, tab3_landed, k_raw, k_sq, k_ms, k_rt, k_rs, k_diag, k_rb, k_x, k_rot, k_cos, k_sin, k_made, vs_made, q_sq, q_rot, q_rt, q_rs, q_sc, q_cos, q_sin, q_made, sc_made, mx_made, nb_made, p_exp, p_rr, p_norm, p_t, pt_made, pv_made, at_made, a_hi_made, a_ready, sig_made, y_a, y_g, y_hi_made, y_ready, relu_made, m_hi_made, m_ready, row_t) = (sem(n) for n in ("c_landed", "c_turned", "c_made", "csq_made", "csq_summed", "cms_made", "crt_made", "crs_made", "cdiag_made", "crb_made", "cxr_made", "ch_made", "tab2_landed", "wgk_zero", "wgk_landed", "lr_made", "z_made", "z_out", "z_min", "z_exp", "z_ln", "g_made", "b_made", "kd_arg", "kd_e", "eb_made", "kd_made", "qb_made", "kdt_t", "kdt_made", "sp_made", "st_made", "lv_d", "lv_abs", "lv_e", "lv_q", "lv_k", "lv_mm", "lv_cp", "dg_mm", "dg_made", "o_mm", "o_cp", "o_sq", "o_ms", "o_rt", "o_rs", "o_diag", "o_rb", "o_xr", "o_done", "sg_made", "tab3_landed", "k_raw", "k_sq", "k_ms", "k_rt", "k_rs", "k_diag", "k_rb", "k_x", "k_rot", "k_cos", "k_sin", "k_made", "vs_made", "q_sq", "q_rot", "q_rt", "q_rs", "q_sc", "q_cos", "q_sin", "q_made", "sc_made", "mx_made", "nb_made", "p_exp", "p_rr", "p_norm", "p_t", "pt_made", "pv_made", "at_made", "a_hi_made", "a_ready", "sig_made", "y_a", "y_g", "y_hi_made", "y_ready", "relu_made", "m_hi_made", "m_ready", "row_t"))
        out_made = sem("out_made")
        out_sem = sem("out_written")

        def vec(name, n=0):
            return VECS[:, VEC_ROWS[name][0] + n:VEC_ROWS[name][0] + n + 1]

        def vecs(name, a, b):
            return VECS[:, VEC_ROWS[name][0] + a:VEC_ROWS[name][0] + b]

        def ada_view(g):
            w = ins["ada_w"][g // 3] if g < 6 else ins["w_ada_2"][0]
            return w.rearrange("(k p) m -> p k m", p=P), 3 * D * (g % 3)

        FFN_GROUPS = [(1, 2), (3, 4), (5, 6), (7, None)]
        FFN_NORM = [0, 2, 3, 5]
        H_BASE = {0: 0, 2: 8, 3: 16, 4: 24, 5: 32, 7: 40, 8: 56}
        MOD_READ = {g: g + 1 for g in range(6)} | {6: 8, 7: 9}
        MOD_DONE = {g: 2 * g + 2 for g in range(6)} | {6: 15, 7: 17}

        block = ctx_.enter_context(nc.Block())

        @block.sync
        def _(sp):
            sp.dma_start(X_ROWS[:], ins["x"][0].rearrange("(c p) d -> p c d", p=P)).then_inc(in_landed, 16)
            for name, (row, rows) in VEC_ROWS.items():
                flat = ins[name]
                while len(flat.shape) > 1:
                    flat = flat.rearrange("a b c -> (a b) c") if len(flat.shape) == 3 else flat.rearrange("a b -> (a b)")
                src = flat.rearrange("(r q) -> r q", q=P)
                done = 0
                while done < rows:
                    r = row + done
                    n = min(rows - done, P - r % P)
                    sp.dma_start(V_ROWS[r % P:r % P + n, r // P, :], src[done:done + n, :]).then_inc(vec_landed, 16)
                    done += n
            sp.dma_start(IDENT[:], ins["t_ident"]).then_inc(tab_landed, 16)

            def unit(u, kt, width, *src):
                wait(sp, lo_done, u - 1)
                dst = W_RAW[u.slot][:, 0:kt * width * len(src)]
                if len(src) == 2:
                    dst = dst.rearrange("p (k g m) -> p k g m", k=kt, g=2)
                    for g in range(2):
                        sp.dma_start(dst[:, :, g, :], src[g]).then_inc(landed[u.slot], 16)
                else:
                    dst = dst.rearrange("p (k m) -> p k m", k=kt)
                    for rows in (slice(0, kt // 2), slice(kt // 2, kt)):
                        sp.dma_start(dst[:, rows, :], src[0][:, rows, :]).then_inc(landed[u.slot], 16)

            def ada(g, k):
                w, col = ada_view(g)
                for h in range(2):
                    wait(sp, ada_used[h], k + 8 * g)
                    sp.dma_start(ADA[h][:], w[:, bass.ds(k.v, 1), col + 1536 * h:col + 1536 * (h + 1)]
                                 .rearrange("p a m -> p (a m)")).then_inc(ada_landed[h], 16)

            def ffn(f):
                layer, s = f // 2, f % 2
                w_in = ins["ffn_w_in"][layer, s].rearrange("(k p) (g m) -> p k g m", p=P, g=2)
                w_out = ins["ffn_w_out"][layer, s].rearrange("(k p) m -> p k m", p=P)
                for half in range(2):
                    g = FFN_GROUPS[f][half]
                    base = U_FFN[f] + half * (IN_UNITS + OUT_UNITS)

                    def in_unit(j):
                        if j.base >= 2 or base > 0:
                            c = (j + half * FH).times(P).v
                            unit(j + base, KD, P, w_in[:, :, 0, bass.ds(c, P)], w_in[:, :, 1, bass.ds(c, P)])
                        if g is not None and (j.base % 2 == 1):
                            ada(g, (j - 1).half())
                        if g is not None and j.base == IN_UNITS - 1:
                            ada(g, at(5))

                    each(sp, IN_UNITS, 0 if base else 2, 1, in_unit)

                    def out_unit(m):
                        unit(m + (base + IN_UNITS), FH, P,
                             w_out[:, half * FH:(half + 1) * FH, bass.ds(m.times(P).v, P)])
                        if g is not None and m.i is None and m.base < 2:
                            ada(g, at(6 + m.base))

                    each(sp, OUT_UNITS, 2, 2, out_unit)

            w_in0 = ins["ffn_w_in"][0, 0].rearrange("(k p) (g m) -> p k g m", p=P, g=2)
            unit(at(0), KD, P, w_in0[:, :, 0, 0:P], w_in0[:, :, 1, 0:P])
            ada(0, at(0))
            with sp.Fori(0, 7) as i:
                ada(0, At(1, i, 1))
            unit(at(1), KD, P, w_in0[:, :, 0, P:2 * P], w_in0[:, :, 1, P:2 * P])
            ffn(0)
            unit(at(U_POOL), KD, 2 * P, ins["pool_w"][0].rearrange("g (k p) m -> p (g k) m", p=P))
            sp.wait_ge(evac_done, U_POOL)
            sp.dma_start(EDGE[:], ins["t_edge"]).then_inc(tab_landed, 16)
            ffn(1)
            ffn(2)
            w_cin = ins["conv_w_in"][0].rearrange("(k p) (g m) -> p k g m", p=P, g=3)
            w_cout = ins["conv_w_out"][0].rearrange("(k p) m -> p k m", p=P)
            each(sp, 8, 0, 0, lambda j: unit(
                j + U_CONV, KD, P, w_cin[:, :, 1, bass.ds(j.times(P).v, P)], w_cin[:, :, 2, bass.ds(j.times(P).v, P)]))
            each(sp, 4, 0, 0, lambda j: unit(
                j + (U_CONV + 8), KD, 2 * P, w_cin[:, :, 0, bass.ds(j.times(2 * P).v, 2 * P)]))
            each(sp, 4, 0, 2, lambda j: unit(
                j + (U_CONV + 12), KD, 2 * P, w_cout[:, :, bass.ds(j.times(2 * P).v, 2 * P)]))
            ffn(3)
            w2 = ins["w_in_2"][0].rearrange("(k p) m -> p k m", p=P)
            unit(at(U_LR), KD, 2 * RANK, w2[:, :, C_LR:C_LR + 2 * RANK])
            sp.wait_ge(evac_done, U_LR)
            sp.dma_start(C_ROWS[:], ins["ctx_2"][0].rearrange("(c p) d -> p c d", p=P)).then_inc(c_landed, 16)
            sp.dma_start(MASKS[:], ins["t_masks"]).then_inc(tab2_landed, 16)
            sp.dma_start(KEEP[:], ins["t_keep"]).then_inc(tab2_landed, 16)
            with sp.Fori(1, GH_ // 2 + 1) as i:
                for s in range(2):
                    hd, u = At(s - 2, i, 2), At(U_G + 3 * s - 6, i, 6)
                    unit(u, KD, P, w2[:, :, bass.ds((hd.times(DK) + C_GK).v, DK)],
                         w2[:, :, bass.ds((hd.times(DK) + C_GQ).v, DK)])
                    unit(u + 1, KD, DV, w2[:, :, bass.ds((hd.times(DV) + C_GV).v, DV)])
                    if s == 0:
                        sp.wait_ge(wgk_zero, 1)
                    head_cols = bass.ds(hd.times(DK).v, DK)
                    sp.wait_ge(pe_done, (u + 1).v)
                    sp.dma_start(W_GK[0:RANK, 0, :], ins["w_gk_fwd_2"][0][:, head_cols]).then_inc(wgk_landed, 16)
                    sp.dma_start(W_GK[RANK:2 * RANK, 1, :], ins["w_gk_bwd_2"][0][:, head_cols]).then_inc(wgk_landed, 16)
                    unit(u + 2, KD, DV, w2[:, :, bass.ds((hd.times(DV) + C_GO).v, DV)])
            unit(at(U_K), KD, 2 * P, w2[:, :, C_AK:C_AK + 2 * P])
            unit(at(U_V), KD, 2 * P, w2[:, :, C_AV:C_AV + 2 * P])
            sp.wait_ge(o_done, 2 * GH_)
            sp.dma_start(COS[:], ins["t_cos"]).then_inc(tab3_landed, 16)
            sp.dma_start(SIN[:], ins["t_sin"]).then_inc(tab3_landed, 16)
            sp.dma_start(PERM[:], ins["t_perm"]).then_inc(tab3_landed, 16)
            each(sp, NQ // 2, 0, 0, lambda j: unit(j + U_Q, KD, 2 * P, w2[:, :, bass.ds((j.times(2 * P) + C_AQ).v, 2 * P)]))
            w_bra = ins["w_br_attn_2"][0].rearrange("(k p) m -> p k m", p=P)
            w_brg = ins["w_br_gla_2"][0].rearrange("(k p) m -> p k m", p=P)
            with sp.Fori(1, KD + 1) as i:
                col = lambda c0: bass.ds(At(c0 - P, i, P).v, P)
                unit(At(U_D - 2, i, 2), KD, P, w2[:, :, col(C_GA)], w2[:, :, col(C_GG)])
                unit(At(U_D - 1, i, 2), KD, P, w_bra[:, :, col(0)], w_brg[:, :, col(0)])
            w_o = ins["w_out_2"][0].rearrange("(k p) m -> p k m", p=P)
            each(sp, 4, 0, 2, lambda j: unit(j + U_WO, KD, 2 * P, w_o[:, :, bass.ds(j.times(2 * P).v, 2 * P)]))
            w_m1 = ins["w_mlp1_2"][0].rearrange("(k p) m -> p k m", p=P)
            w_m2 = ins["w_mlp2_2"][0].rearrange("(k p) m -> p k m", p=P)

            def quarter(q):
                for j in range(4):
                    unit(q.times(8) + (U_MLP + j), KD, 2 * P, w_m1[:, :, bass.ds((q.times(D) + 2 * P * j).v, 2 * P)])
                for j in range(4):
                    unit(q.times(8) + (U_MLP + 4 + j), KD, 2 * P,
                         w_m2[:, bass.ds(q.times(KD).v, KD), 2 * P * j:2 * P * (j + 1)])

            with sp.Fori(0, 3) as i:
                quarter(At(0, i, 1))
            quarter(at(3))
            for c in range(4):
                sp.wait_ge(out_made, c + 1)
                sp.dma_start(out[c * P:(c + 1) * P, :], X_ROWS[:, c, :]).then_inc(out_sem, 16)
            sp.wait_ge(out_sem, 64)

        @block.gpsimd
        def _(pool):
            nc.gpsimd.memset(ONES[:], 1.0).then_inc(const_ready, 1)
            nc.gpsimd.memset(ONES_D[:, 0:1], 1.0 / D)
            nc.gpsimd.memset(ONES_D[:, 1:2], 1.0 / DV)
            nc.gpsimd.memset(ONES_HD[:], 1.0 / HD).then_inc(const_ready, 1)
            nc.gpsimd.memset(EPS_C[:], EPS).then_inc(const_ready, 1)
            nc.gpsimd.memset(ACC[:], 0.0).then_inc(acc_cleared, 1)
            for g in range(1, 8):
                pool.wait_ge(mod_summed, g)
                if g == 6:
                    nc.gpsimd.memset(ACC_C[:], 0.0).then_inc(acc_cleared, 1)
                nc.gpsimd.memset(ACC[:], 0.0).then_inc(acc_cleared, 1)

            pool.wait_ge(evac_done, U_LR)
            nc.gpsimd.memset(W_GK[0:2 * RANK], 0.0).then_inc(wgk_zero, 1)

        @block.scalar
        def _(act):
            def split_hi(u):
                act.wait_ge(landed[u.slot], (u.half().times(32) + 32).v)
                wait(act, pe_done, u - 1)
                n = unit_size(u.base)
                nc.scalar.copy(W_HI[u.slot][:, 0:n], W_RAW[u.slot][:, 0:n]).then_inc(hi_done, 1)

            def squares(r, ready):
                for k in range(KD):
                    ready(k)
                    wait(act, sq_summed, at(KD * r + k - 1))
                    nc.scalar.activation((SA if r == 7 else GT)[k % 2][:], X[:, k, :], ACT.Square).then_inc(sq_made, 1)

            def root(r):
                act.wait_ge(ms_made, r + 1)
                nc.scalar.activation(RSTD4[:, 4:8], BANK[6][:, 0:4], ACT.Sqrt, bias=EPS_C[:]).then_inc(rt_made, 1)

            def h_hi(r):
                for k in range(KD):
                    act.wait_ge(h_made, KD * r + k + 1)
                    nc.scalar.copy(H_HI[:, k, 0:T], SA[k % 2][:]).then_inc(h_hi_made, 1)

            def ffn(f):
                for half in range(2):
                    base = U_FFN[f] + half * (IN_UNITS + OUT_UNITS)

                    def in_unit(j):
                        u = j + base
                        split_hi(u + 1)
                        act.wait_ge(pe_done, (u + 1).v)
                        wait(act, evac_done, u - 1)
                        nc.scalar.activation(SA[u.slot][:], BANK[2 * u.slot][:], ACT.Silu).then_inc(silu_made, 1)

                    each(act, IN_UNITS, 0 if base else 2, 1, in_unit)
                    each(act, OUT_UNITS, 2, 2, lambda m: split_hi(m + (base + IN_UNITS + 1)))

            act.wait_ge(vec_ready, 1)
            nc.scalar.activation(COND[:], VECS[:, 0:24], ACT.Silu).then_inc(cond_ready, 1)
            for k in range(KD):
                act.wait_ge(x_turned, k + 1)
                nc.scalar.copy(X[:, k, :], BANK[k % 4][:]).then_inc(x_made, 1)
            act.wait_ge(const_ready, 3)
            squares(0, lambda k: act.wait_ge(x_made, k + 1))
            root(0)
            split_hi(at(0))
            h_hi(0)

            def after_ffn(f):
                return lambda k: act.wait_ge(evac_done, U_FFN[f] + FFN_UNITS - OUT_UNITS + k + 1)

            ffn(0)
            squares(1, after_ffn(0))
            root(1)
            for k in range(KD):
                act.wait_ge(pool_mixed, k + 1)
                nc.scalar.copy(H_HI[:, k, 0:T], PH[:, k, :]).then_inc(p_hi_made, 1)
            split_hi(at(U_POOL + 1))
            squares(2, lambda k: act.wait_ge(pool_added, k // 2 + 1) if k < 6 else
                    act.wait_ge(evac_done, U_POOL + 1))
            root(2)
            h_hi(2)
            ffn(1)
            squares(3, after_ffn(1))
            root(3)
            h_hi(3)
            ffn(2)
            squares(4, after_ffn(2))
            root(4)
            h_hi(4)

            def cv_unit(j):
                u = j + U_CONV
                split_hi(u + 1)
                act.wait_ge(pe_done, (u + 1).v)
                wait(act, evac_done, u - 1)
                nc.scalar.copy(C_T[u.slot][:], BANK[2 * u.slot][:]).then_inc(cv_c, 1)

            each(act, 8, 0, 0, cv_unit)
            each(act, 4, 0, 0, lambda j: split_hi(j + (U_CONV + 9)))
            each(act, 4, 0, 2, lambda j: split_hi(j + (U_CONV + 13)))
            squares(5, lambda k: act.wait_ge(evac_done, U_CONV + 12 + k // 2 + 1))
            root(5)
            h_hi(5)
            ffn(3)
            squares(6, after_ffn(3))
            root(6)
            squares(7, lambda k: act.wait_ge(h_made, KD * 6 + k + 1))
            root(7)
            h_hi(7)
            for k in range(KD):
                act.wait_ge(c_turned, 2 * (k // 2) + 2)
                nc.scalar.copy(C_X[:, k, :], BANK[k // 2][:, TC * (k % 2):TC * (k % 2 + 1)]).then_inc(c_made, 1)
            for k in range(KD):
                act.wait_ge(c_made, k + 1)
                wait(act, csq_summed, at(k - 1))
                nc.scalar.activation(SG[k % 2][:, 0:TC], C_X[:, k, :], ACT.Square).then_inc(csq_made, 1)
            act.wait_ge(cms_made, 1)
            nc.scalar.activation(STAT[:, 0:2], BANK[7][:, 0:2], ACT.Sqrt, bias=EPS_C[:]).then_inc(crt_made, 1)
            for k in range(KD):
                act.wait_ge(ch_made, k + 1)
                nc.scalar.copy(H_HI[:, k, T:TA], SG[k % 2][:, 0:TC]).then_inc(h_hi_made, 1)
            split_hi(at(U_LR + 1))

            def gla_levels(hd, d):
                for n in range(len(LEVELS)):
                    lv = hd.times(14) + (7 * d + n + 1)
                    e = EL[(7 * d + n) % 2]
                    act.wait_ge(lv_d, lv.v)
                    nc.scalar.activation(e[:], e[:], ACT.Abs).then_inc(lv_abs, 1)
                    act.wait_ge(lv_abs, lv.v)
                    nc.scalar.activation(e[:], e[:], ACT.Exp, scale=-1.0 / 16).then_inc(lv_e, 1)

            with act.Fori(0, GH_ // 2) as i:
                for s in range(2):
                    hd, u = At(s, i, 2), At(U_G + 3 * s, i, 6)
                    split_hi(u + 1)
                    split_hi(u + 2)
                    for d in range(2):
                        zd = hd.times(2) + (d + 1)
                        bias = VECS[:, bass.ds((hd + VEC_ROWS[("b_gk_fwd_2", "b_gk_bwd_2")[d]][0]).v, 1)]
                        act.wait_ge(z_made, zd.v)
                        nc.scalar.activation(T1[:], WIDE[6], ACT.Identity, bias=bias).then_inc(z_out, 1)
                        act.wait_ge(z_min, zd.v)
                        nc.scalar.activation(T2[:], T2[:], ACT.Exp).then_inc(z_exp, 1)
                        act.wait_ge(z_exp, zd.v)
                        nc.scalar.activation(T2[:], T2[:], ACT.Ln, bias=1.0).then_inc(z_ln, 1)
                        act.wait_ge(b_made, zd.v)
                        nc.scalar.activation(T1[:, 0:T], B[:, 0:T], ACT.Exp, scale=1.0 / 16).then_inc(eb_made, 1)
                        act.wait_ge(kd_arg, zd.v)
                        nc.scalar.activation(T2[:], T2[:], ACT.Exp, scale=1.0 / 16).then_inc(kd_e, 1)
                        act.wait_ge(kdt_t, zd.v)
                        nc.scalar.copy(KDT[:].rearrange("p c t -> p (c t)"), WIDE[6]).then_inc(kdt_made, 1)
                        if d == 0:
                            split_hi(u + 3)
                        gla_levels(hd, d)
                    act.wait_ge(evac_done, (u + 3).v)
                    for e in range(2):
                        nc.scalar.activation(SG[e][:], SG[e][:], ACT.Silu).then_inc(sg_made, 1)
                    pb = 2 * ((s + 1) % 2)
                    act.wait_ge(o_mm, (hd + 1).v)
                    for e in range(2):
                        nc.scalar.copy(KL[e][:], BANK[pb + e][:]).then_inc(o_cp, 1)
                    for e in range(2):
                        nc.scalar.activation(QL[e][:], BANK[pb + e][:], ACT.Square).then_inc(o_sq, 1)
                    act.wait_ge(o_ms, (hd + 1).v)
                    nc.scalar.activation(STAT[:, 0:4], BANK[6][:, 0:4], ACT.Sqrt, bias=EPS_C[:]).then_inc(o_rt, 1)
            split_hi(at(U_K + 1))
            act.wait_ge(k_raw, 1)
            for h in range(NKV):
                nc.scalar.activation(K_SQ[:, h, :], K_RAW[:, h, :], ACT.Square).then_inc(k_sq, 1)
            act.wait_ge(k_ms, 1)
            nc.scalar.activation(STAT[:, 0:12], BANK[6][:, 0:12], ACT.Sqrt, bias=EPS_C[:]).then_inc(k_rt, 1)
            split_hi(at(U_V + 1))
            with act.Fori(0, NKV) as kv:
                for ui in range(2):
                    qi, u = At(ui, kv, 2), At(U_Q + ui, kv, 2)
                    pb = 2 * u.slot
                    act.wait_ge(pe_done, (u + 1).v)
                    if ui == 0:
                        act.wait_ge(vs_made, At(1, kv, 1).v)
                    for m in range(2):
                        if ui == 1:
                            act.wait_ge(at_made, At(2, kv, 4).v)
                        nc.scalar.activation(Q_SQ[m][:], BANK[pb + m][:], ACT.Square).then_inc(q_sq, 1)
                    split_hi(u + 1)
                    act.wait_ge(q_rot, (qi + 1).v)
                    nc.scalar.activation(STAT[:, 0:8], BANK[6][:, 0:8], ACT.Sqrt, bias=EPS_C[:]).then_inc(q_rt, 1)
                    for m in range(2):
                        a = At(2 * ui + m, kv, 4)

                        def exp_p(c):
                            act.wait_ge(nb_made, (a.times(4) + (c + 1)).v)
                            nc.scalar.activation(PP[c % 2][:], WIDE[4 + 2 * (c % 2)], ACT.Exp, bias=STAT[:, 34 + c % 2:35 + c % 2],
                                                 scale=STAT[:, 16 + 4 * m + c:17 + 4 * m + c],
                                                 accum_out=STAT[:, 36 + c % 2:37 + c % 2]).then_inc(p_exp, 1)

                        def copy_pt(c):
                            act.wait_ge(p_t, (a.times(4) + (c + 1)).v)
                            nc.scalar.copy(PT[:, :, c * P:(c + 1) * P],
                                           WIDE[2 * (c % 2)].rearrange("p (k q) -> p k q", k=6)).then_inc(pt_made, 1)

                        exp_p(0)
                        for c in range(1, 4):
                            exp_p(c)
                            copy_pt(c - 1)
                        copy_pt(3)
            act.wait_ge(at_made, NQ)
            for k in range(KD):
                nc.scalar.copy(A_HI[:, k, :], AT_T[:, k, :]).then_inc(a_hi_made, 1)
            for k in range(KD):
                nc.scalar.copy(L_HI[:, k, :], O_T[:, k, :]).then_inc(a_hi_made, 1)
            with act.Fori(0, KD) as i:
                u = At(U_D, i, 2)
                split_hi(u + 1)
                act.wait_ge(pe_done, (u + 1).v)
                act.wait_ge(evac_done, u.v)
                nc.scalar.activation(SGB[0][:], BANK[0][:], ACT.Sigmoid).then_inc(sig_made, 1)
                nc.scalar.activation(SGB[1][:], BANK[1][:], ACT.Sigmoid).then_inc(evac_done, 1)
                split_hi(u + 2)
            act.wait_ge(evac_done, U_WO)
            for k in range(KD):
                nc.scalar.copy(H_HI[:, k, 0:T], Y[:, k, :]).then_inc(y_hi_made, 1)
            each(act, 4, 0, 2, lambda j: split_hi(j + (U_WO + 1)))
            squares(8, lambda k: act.wait_ge(evac_done, U_WO + k // 2 + 1))
            root(8)
            h_hi(8)

            def quarter(q, last=False):
                for j in range(4):
                    u = q.times(8) + (U_MLP + j)
                    split_hi(u + 1)
                    act.wait_ge(pe_done, (u + 1).v)
                    act.wait_ge(evac_done, u.v)
                    for m in range(2):
                        nc.scalar.activation(SA[m][:], BANK[2 * u.slot + m][:], ACT.Relu).then_inc(relu_made, 1)
                for j in range(4):
                    if not (last and j == 3):
                        split_hi(q.times(8) + (U_MLP + 5 + j))

            with act.Fori(0, 3) as i:
                quarter(At(0, i, 1))
            quarter(at(3), True)
            for c in range(4):
                act.wait_ge(row_t, c + 1)
                nc.scalar.copy(X_ROWS[:, c, :], PS[:, 2 * T * (c % 2):2 * T * (c % 2 + 1)]).then_inc(out_made, 1)

        @block.vector
        def _(dve):
            def split_lo(u):
                dve.wait_ge(hi_done, (u + 1).v)
                n = unit_size(u.base)
                nc.vector.tensor_tensor(W_LO[u.slot][:, 0:n], W_RAW[u.slot][:, 0:n],
                                        W_HI[u.slot][:, 0:n].bitcast(F32), ALU.subtract).then_inc(lo_done, 1)

            def ada(g, k):
                for h in range(2):
                    dve.wait_ge(ada_landed[h], ((k + (8 * g + 1)).times(16)).v)
                    if h == 0 and k.base == 0:
                        dve.wait_ge(acc_cleared, g + 1 + (g >= 6))
                    wait(dve, ada_used[h], k + 8 * g)
                    acc = ACC[:, 1536 * h:1536 * (h + 1)]
                    cond = 0 if g < 6 else 8
                    if g == 6:
                        n = 1536 if h == 0 else 512
                        acc_c = ACC_C[:, 1536 * h:1536 * h + n]
                        nc.vector.scalar_tensor_tensor(acc_c, ADA[h][:, 0:n], COND[:, bass.ds((k + 16).v, 1)],
                                                       acc_c, ALU.mult, ALU.add)
                    nc.vector.scalar_tensor_tensor(acc, ADA[h][:], COND[:, bass.ds((k + cond).v, 1)],
                                                   acc, ALU.mult, ALU.add).then_inc(ada_used[h], 1)

            def modulation(g):
                bias = vecs("ada_b", 24 * g, 24 * g + 24) if g < 6 else vecs("b_ada_2", 24 * (g - 6), 24 * (g - 6) + 24)
                gain = vecs("norm_g", 8 * g, 8 * g + 8) if g < 6 else vecs(("norm1_2", "norm2_2")[g - 6], 0, 8)
                dve.wait_ge(mod_summed, g + 1)
                m = MODS[:, 24 * g:24 * g + 24]
                nc.vector.tensor_tensor(m, BANK[7][:, 0:24], bias, ALU.add).then_inc(mod_read, 1)
                if g == 6:
                    nc.vector.tensor_tensor(MODS[:, 192:208], BANK[7][:, 24:40], bias[:, 0:16], ALU.add).then_inc(mod_read, 1)
                dve.wait_ge(mod_read, MOD_READ[g])
                nc.vector.scalar_tensor_tensor(GAIN[:, 8 * g:8 * g + 8], m[:, 8:16], 1.0, gain, ALU.add, ALU.mult).then_inc(mod_done, 1)
                gate = GATE[:, 8 * g:8 * g + 8]
                if g in FFN_NORM:
                    nc.vector.tensor_scalar(gate, m[:, 16:24], 0.5, None, ALU.mult).then_inc(mod_done, 1)
                elif g == 1:
                    nc.vector.tensor_tensor(gate, m[:, 16:24], vecs("pool_scale", 0, 8), ALU.mult).then_inc(mod_done, 1)
                else:
                    nc.vector.tensor_copy(gate, m[:, 16:24]).then_inc(mod_done, 1)
                if g == 6:
                    nc.vector.scalar_tensor_tensor(GAIN[:, 64:72], MODS[:, 200:208], 1.0, gain, ALU.add, ALU.mult).then_inc(mod_done, 1)

            def square_sums(r):
                sq = SA if r == 7 else GT
                for k in range(KD):
                    dve.wait_ge(sq_made, KD * r + k + 1)
                    if k == 0:
                        nc.vector.tensor_copy(SSQ[:], sq[0][:]).then_inc(sq_summed, 1)
                    else:
                        dve.wait_ge(sq_summed, KD * r + k)
                        nc.vector.tensor_tensor(SSQ[:], SSQ[:], sq[k % 2][:], ALU.add).then_inc(sq_summed, 1)

            def rstd_diag(r):
                dve.wait_ge(rt_made, r + 1)
                nc.vector.reciprocal(RSTD4[:, 0:4], RSTD4[:, 4:8]).then_inc(rs_made, 1)
                dve.wait_ge(rs_made, r + 1)
                for c in range(4):
                    nc.vector.tensor_scalar(DIAG[:, c, :], IDENT[:], RSTD4[:, c:c + 1], None, ALU.mult).then_inc(diag_made, 1)

            def normed(r, k, dst, gain, shift=None):
                if k == 0:
                    dve.wait_ge(rb_made, r + 1)
                nc.vector.tensor_tensor(GT[k % 2][:], X[:, k, :], BANK[5][:], ALU.mult).then_inc(xr_made, 1)
                dve.wait_ge(xr_made, KD * r + k + 1)
                if shift is None:
                    nc.vector.tensor_scalar(dst, GT[k % 2][:], gain, None, ALU.mult).then_inc(h_made, 1)
                else:
                    nc.vector.tensor_scalar(dst, GT[k % 2][:], gain, shift, ALU.mult, ALU.add).then_inc(h_made, 1)

            def norm_split(r, g):
                def lo(k):
                    dve.wait_ge(h_hi_made, H_BASE[r] + k + 1)
                    nc.vector.tensor_tensor(H_LO[:, k, 0:T], SA[k % 2][:], H_HI[:, k, 0:T].bitcast(F32),
                                            ALU.subtract).then_inc(h_ready, 1)
                square_sums(r)
                rstd_diag(r)
                dve.wait_ge(mod_done, MOD_DONE[g])
                for k in range(KD):
                    normed(r, k, SA[k % 2][:], GAIN[:, 8 * g + k:8 * g + k + 1], MODS[:, 24 * g + k:24 * g + k + 1])
                    if k >= 1:
                        lo(k - 1)
                lo(KD - 1)

            def add_branch(m, bank, gate):
                mm = bass.ds(m.v, 1)
                x = X[:, mm, :].rearrange("p a t -> p (a t)")
                return nc.vector.scalar_tensor_tensor(x, bank[:], GATE[:, bass.ds((m + 8 * gate).v, 1)], x, ALU.mult, ALU.add)

            def ffn(f):
                for half in range(2):
                    g = FFN_GROUPS[f][half]
                    base = U_FFN[f] + half * (IN_UNITS + OUT_UNITS)
                    q0 = (2 * f + half) * FH

                    def in_unit(j):
                        u, q = j + base, j + q0
                        split_lo(u + 1)
                        dve.wait_ge(silu_made, (q + 1).v)
                        nc.vector.tensor_tensor(GT[u.slot][:], SA[u.slot][:], BANK[2 * u.slot + 1][:], ALU.mult).then_inc(evac_done, 1)
                        dve.wait_ge(evac_done, (u + 1).v)
                        tile = lambda b: b[:, bass.ds(j.v, 1), :].rearrange("p a t -> p (a t)")
                        nc.vector.tensor_copy(tile(G_HI), GT[u.slot][:]).then_inc(g_hi_made, 1)
                        dve.wait_ge(g_hi_made, (q + 1).v)
                        nc.vector.tensor_tensor(tile(G_LO), GT[u.slot][:], tile(G_HI).bitcast(F32), ALU.subtract).then_inc(g_ready, 1)
                        if g is not None and (j.base % 2 == 1):
                            ada(g, (j - 1).half())
                        if g is not None and j.base == IN_UNITS - 1:
                            ada(g, at(5))

                    each(dve, IN_UNITS, 0 if base else 2, 1, in_unit)

                    def out_unit(m):
                        u = m + (base + IN_UNITS)
                        split_lo(u + 1)
                        dve.wait_ge(pe_done, (u + 1).v)
                        add_branch(m, BANK[2 * u.slot], FFN_NORM[f]).then_inc(evac_done, 1)
                        if g is not None and m.i is None and m.base < 2:
                            ada(g, at(6 + m.base))
                        if g is not None and m.i is None and m.base == 6:
                            modulation(g)

                    each(dve, OUT_UNITS, 2, 2, out_unit)

            dve.wait_ge(vec_turned, 1)
            nc.vector.tensor_copy(VECS[:, 0:NVEC], BANK[6][:, 0:NVEC]).then_inc(vec_ready, 1)
            square_sums(0)
            rstd_diag(0)
            split_lo(at(0))
            dve.wait_ge(cond_ready, 1)
            ada(0, at(0))
            with dve.Fori(0, 7) as i:
                ada(0, At(1, i, 1))
            modulation(0)

            def h_first():
                def lo(k):
                    dve.wait_ge(h_hi_made, k + 1)
                    nc.vector.tensor_tensor(H_LO[:, k, 0:T], SA[k % 2][:], H_HI[:, k, 0:T].bitcast(F32),
                                            ALU.subtract).then_inc(h_ready, 1)
                dve.wait_ge(mod_done, MOD_DONE[0])
                for k in range(KD):
                    normed(0, k, SA[k % 2][:], GAIN[:, k:k + 1], MODS[:, k:k + 1])
                    if k >= 1:
                        lo(k - 1)
                lo(KD - 1)

            h_first()
            ffn(0)
            square_sums(1)
            rstd_diag(1)
            dve.wait_ge(mod_done, MOD_DONE[1])
            for k in range(KD):
                normed(1, k, PH[:, k, :], GAIN[:, 8 + k:9 + k], MODS[:, 24 + k:25 + k])
            dve.wait_ge(tab_landed, 32)
            steps = 0
            for gi, w in enumerate(POOL_WINDOWS):
                h = PH[:, 2 * gi:2 * gi + 2, :]
                dve.wait_ge(h_made, KD + 2 * gi + 2)
                src, dst, s = h, PS_A, 1
                while s < w:
                    nc.vector.tensor_tensor(dst[:, :, s:T], src[:, :, s:T], src[:, :, 0:T - s], ALU.add)
                    nc.vector.tensor_copy(dst[:, :, 0:s], src[:, :, 0:s]).then_inc(pool_step, 1)
                    steps += 1
                    dve.wait_ge(pool_step, steps)
                    src, dst = dst, (PS_B if dst is PS_A else PS_A)
                    s *= 2
                for a in range(2):
                    nc.vector.tensor_tensor(src[:, a, 0:w], src[:, a, 0:w], EDGE[:, gi, 0:w], ALU.mult).then_inc(pool_step, 1)
                steps += 2
                dve.wait_ge(pool_step, steps)
                for a in range(2):
                    nc.vector.scalar_tensor_tensor(PH[:, 2 * gi + a, :], src[:, a, :], 1.0 / w, PH[:, 2 * gi + a, :],
                                                   ALU.mult, ALU.subtract).then_inc(pool_mixed, 1)
                for k in (2 * gi, 2 * gi + 1):
                    dve.wait_ge(p_hi_made, k + 1)
                    nc.vector.tensor_tensor(H_LO[:, k, 0:T], PH[:, k, :], H_HI[:, k, 0:T].bitcast(F32),
                                            ALU.subtract).then_inc(p_ready, 1)
            split_lo(at(U_POOL + 1))
            for gi in range(4):
                if gi < 3:
                    dve.wait_ge(pool_mm, gi + 1)
                else:
                    dve.wait_ge(pe_done, U_POOL + 1)
                for a in range(2):
                    last = add_branch(at(2 * gi + a), BANK[2 * (gi % 2) + a], 1)
                last.then_inc(pool_added if gi < 3 else evac_done, 1)
            norm_split(2, 2)
            ffn(1)
            norm_split(3, 3)
            ffn(2)
            norm_split(4, 4)
            for s in range(2):
                nc.vector.memset(U_T[s][:, 0:2], 0.0).then_inc(cv_zero, 1)

            def cv_unit(j):
                u = j + U_CONV
                uu = U_T[u.slot]
                split_lo(u + 1)
                dve.wait_ge(cv_c, (j + 1).v)
                dve.wait_ge(cv_zero, 2)
                nc.vector.tensor_tensor(uu[:, 2:T + 2], C_T[u.slot][:], BANK[2 * u.slot + 1][:], ALU.mult).then_inc(evac_done, 1)
                dve.wait_ge(evac_done, (u + 1).v)
                cv = CV[:, bass.ds(j.v, 1), :].rearrange("p a t -> p (a t)")
                tap = lambda n: VECS[:, bass.ds((j + (VEC_ROWS["conv_w"][0] + 8 * n)).v, 1)]
                nc.vector.tensor_scalar(cv, uu[:, 0:T], tap(0), None, ALU.mult).then_inc(cv_1, 1)
                dve.wait_ge(cv_1, (j + 1).v)
                nc.vector.scalar_tensor_tensor(cv, uu[:, 1:T + 1], tap(1), cv, ALU.mult, ALU.add).then_inc(cv_2, 1)
                dve.wait_ge(cv_2, (j + 1).v)
                nc.vector.scalar_tensor_tensor(cv, uu[:, 2:T + 2], tap(2), cv, ALU.mult, ALU.add).then_inc(cv_3, 1)

            each(dve, 8, 0, 0, cv_unit)
            dve.wait_ge(cv_3, 8)

            def b_unit(j):
                u = j + (U_CONV + 8)
                split_lo(u + 1)
                dve.wait_ge(pe_done, (u + 1).v)
                for a in range(2):
                    m = j.times(2) + a
                    tile = lambda b: b[:, bass.ds(m.v, 1), :].rearrange("p a t -> p (a t)")
                    mul = nc.vector.tensor_tensor(GT[a][:], BANK[2 * u.slot + a][:], tile(CV), ALU.mult)
                    mul.then_inc(cz_made, 1)
                    dve.wait_ge(cz_made, (m + 1).v)
                    if a == 1:
                        nc.vector.tensor_copy(tile(Z_HI), GT[a][:]).then_inc(evac_done, 1)
                        dve.wait_ge(evac_done, (u + 1).v)
                    else:
                        nc.vector.tensor_copy(tile(Z_HI), GT[a][:]).then_inc(z_hi_made, 1)
                        dve.wait_ge(z_hi_made, (j + 1).v)
                    nc.vector.tensor_tensor(tile(Z_LO), GT[a][:], tile(Z_HI).bitcast(F32), ALU.subtract).then_inc(z_ready, 1)

            each(dve, 4, 0, 0, b_unit)

            def out_pair(j):
                u = j + (U_CONV + 12)
                split_lo(u + 1)
                dve.wait_ge(pe_done, (u + 1).v)
                for a in range(2):
                    last = add_branch(j.times(2) + a, BANK[2 * u.slot + a], 4)
                last.then_inc(evac_done, 1)

            each(dve, 4, 0, 2, out_pair)
            norm_split(5, 5)
            ffn(3)
            square_sums(6)
            rstd_diag(6)
            for k in range(KD):
                normed(6, k, X[:, k, :], vec("final_g", k))
            norm_split(7, 6)
            for k in range(KD):
                dve.wait_ge(csq_made, k + 1)
                if k == 0:
                    nc.vector.tensor_copy(SSQ[:, 0:TC], SG[0][:, 0:TC]).then_inc(csq_summed, 1)
                else:
                    dve.wait_ge(csq_summed, k)
                    nc.vector.tensor_tensor(SSQ[:, 0:TC], SSQ[:, 0:TC], SG[k % 2][:, 0:TC], ALU.add).then_inc(csq_summed, 1)
            dve.wait_ge(crt_made, 1)
            nc.vector.reciprocal(STAT[:, 2:4], STAT[:, 0:2]).then_inc(crs_made, 1)
            dve.wait_ge(crs_made, 1)
            for c in range(2):
                nc.vector.tensor_scalar(DIAG[:, c, :], IDENT[:], STAT[:, 2 + c:3 + c], None, ALU.mult).then_inc(cdiag_made, 1)
            dve.wait_ge(crb_made, 1)

            def ctx_lo(k):
                dve.wait_ge(h_hi_made, H_BASE[7] + KD + k + 1)
                nc.vector.tensor_tensor(H_LO[:, k, T:TA], SG[k % 2][:, 0:TC], H_HI[:, k, T:TA].bitcast(F32),
                                        ALU.subtract).then_inc(h_ready, 1)

            for k in range(KD):
                nc.vector.tensor_tensor(GT[k % 2][:, 0:TC], C_X[:, k, :], BANK[6][:, 0:TC], ALU.mult).then_inc(cxr_made, 1)
                dve.wait_ge(cxr_made, k + 1)
                nc.vector.tensor_scalar(SG[k % 2][:, 0:TC], GT[k % 2][:, 0:TC], GAIN[:, 64 + k:65 + k],
                                        MODS[:, 192 + k:193 + k], ALU.mult, ALU.add).then_inc(ch_made, 1)
                if k >= 1:
                    ctx_lo(k - 1)
            ctx_lo(KD - 1)
            split_lo(at(U_LR + 1))
            dve.wait_ge(pe_done, U_LR + 1)
            lb = U_LR % 2
            nc.vector.tensor_copy(LRT[0:2 * RANK, 0:T], BANK[2 * lb][0:2 * RANK, :])
            nc.vector.tensor_copy(LRT[0:2 * RANK, T:TA], BANK[4 + lb][0:2 * RANK, 0:TC]).then_inc(evac_done, 1)

            bx = B[:, 0:T].rearrange("p (c t) -> p c t", c=NC_)
            t2x = T2[:, 0:T].rearrange("p (c t) -> p c t", c=NC_)
            am = AM[:].rearrange("p (c t) -> p c t", c=NC_)

            def gla_dir(hd, d, pb):
                zd = hd.times(2) + (d + 1)
                dve.wait_ge(z_out, zd.v)
                nc.vector.scalar_tensor_tensor(T2[:], T1[:], -1.0, T1[:], ALU.mult, ALU.min).then_inc(z_min, 1)
                dve.wait_ge(z_ln, zd.v)
                nc.vector.scalar_tensor_tensor(T1[:], T1[:], 0.0, T2[:], ALU.min, ALU.subtract).then_inc(g_made, 1)
                dve.wait_ge(g_made, zd.v)
                if d == 0:
                    nc.vector.tensor_tensor_scan(B[:, 0:T], KEEP[:], T1[:, 0:T], 0.0, ALU.mult, ALU.add)
                    nc.vector.tensor_tensor_scan(B[:, T:TA], KEEP[:, 0:TC], T1[:, T:TA], 0.0, ALU.min, ALU.add).then_inc(b_made, 1)
                else:
                    nc.vector.tensor_tensor_scan(B[:, T - 1::-1], KEEP[:], T1[:, T - 1::-1], 0.0, ALU.mult, ALU.add)
                    nc.vector.tensor_tensor_scan(B[:, TA - 1:T - 1:-1], KEEP[:, 0:TC], T1[:, TA - 1:T - 1:-1], 0.0, ALU.min, ALU.add).then_inc(b_made, 1)
                dve.wait_ge(b_made, zd.v)
                end = CH - 1 if d == 0 else 0
                nc.vector.tensor_tensor(t2x, bx[:, :, end:end + 1].broadcast_to([P, NC_, CH]), bx, ALU.subtract)
                end = TA - 1 if d == 0 else T
                nc.vector.tensor_tensor(T2[:, T:TA], B[:, end:end + 1].broadcast_to([P, TC]), B[:, T:TA], ALU.subtract).then_inc(kd_arg, 1)
                dve.wait_ge(eb_made, zd.v)
                nc.vector.tensor_tensor(QB[d][:], QT[:], T1[:, 0:T], ALU.mult).then_inc(qb_made, 1)
                dve.wait_ge(kd_e, zd.v)
                nc.vector.tensor_tensor(T2[:], KT[:], T2[:], ALU.mult).then_inc(kd_made, 1)

                def level_d(n):
                    sz = LEVELS[n]
                    blk = lambda t: t.rearrange("p (n r) -> p n r", r=2 * sz)
                    mid = sz - 1 if d == 0 else sz
                    b = blk(B[:, 0:T])
                    if 7 * d + n >= 2:
                        dve.wait_ge(lv_k, (hd.times(14) + (7 * d + n - 1)).v)
                    nc.vector.tensor_tensor(blk(EL[(7 * d + n) % 2][:]), b, b[:, :, mid:mid + 1].broadcast_to([P, T // (2 * sz), 2 * sz]),
                                            ALU.subtract).then_inc(lv_d, 1)

                def level_wait(n):
                    dve.wait_ge(lv_mm, (hd.times(14) + (7 * d + n + 1)).v)
                    if 7 * d + n >= 1:
                        dve.wait_ge(lv_cp, (hd.times(14) + (7 * d + n)).v)

                def level_copy(n):
                    nc.vector.copy_predicated(am, MASKS[:, 7 * d + n:7 * d + n + 1, :].broadcast_to([P, NC_, P]),
                                              BANK[6 + (7 * d + n) % 2].rearrange("p (c t) -> p c t", c=NC_)).then_inc(lv_cp, 1)

                level_d(0)
                dve.wait_ge(sp_made, zd.v)
                order = [0, 1, 2, 3] if d == 0 else [3, 2, 1, 0]
                s0 = hd.times(8) + 4 * d
                for n, c in enumerate(order):
                    if n == 0:
                        nc.vector.tensor_copy(ST[d][:, c, :], PS[:, pb * T + 3 * DV:pb * T + 4 * DV]).then_inc(st_made, 1)
                    else:
                        dve.wait_ge(st_made, (s0 + n).v)
                        before = order[n - 1]
                        col = before * CH + (CH - 1 if d == 0 else 0)
                        nc.vector.scalar_tensor_tensor(ST[d][:, c, :], ST[d][:, before, :], T1[:, col:col + 1],
                                                       PS[:, pb * T + (n - 1) * DV:pb * T + n * DV], ALU.mult, ALU.add).then_inc(st_made, 1)
                if d == 0:
                    dve.wait_ge(dg_mm, (hd + 1).v)
                    ident = IDENT[:].rearrange("p (a t) -> p a t", a=1).broadcast_to([P, NC_, P])
                    bank = BANK[4 + pb // 2].rearrange("p (c t) -> p c t", c=NC_)
                    nc.vector.scalar_tensor_tensor(am, bank, 2.0, ident, ALU.mult, ALU.mult).then_inc(dg_made, 1)
                    dve.wait_ge(dg_made, (hd + 1).v)
                for n in range(len(LEVELS)):
                    lv = hd.times(14) + (7 * d + n + 1)
                    slot = (7 * d + n) % 2
                    if n + 1 < len(LEVELS):
                        level_d(n + 1)
                    dve.wait_ge(lv_e, lv.v)
                    nc.vector.tensor_tensor(QL[slot][:], QT[:], EL[slot][:], ALU.mult).then_inc(lv_q, 1)
                    if n >= 1:
                        level_wait(n - 1)
                    nc.vector.tensor_tensor(KL[slot][:], KT[:, 0:T], EL[slot][:], ALU.mult).then_inc(lv_k, 1)
                    if n >= 1:
                        level_copy(n - 1)
                level_wait(len(LEVELS) - 1)
                nc.vector.memset(STAT[:, 62:63], 0.0)
                level_copy(len(LEVELS) - 1)

            dve.wait_ge(tab2_landed, 32)
            with dve.Fori(0, GH_ // 2) as i:
                for s in range(2):
                    hd, u = At(s, i, 2), At(U_G + 3 * s, i, 6)
                    pa, pb = 2 * (s % 2), 2 * ((s + 1) % 2)
                    split_lo(u + 1)
                    dve.wait_ge(pe_done, (u + 1).v)
                    nc.vector.tensor_copy(KT[:, 0:T], BANK[pa])
                    nc.vector.tensor_copy(KT[:, T:TA], BANK[4 + pa // 2][:, 0:TC])
                    nc.vector.tensor_scalar(QT[:], BANK[pa + 1], DK ** -0.5, None, ALU.mult).then_inc(evac_done, 1)
                    split_lo(u + 2)
                    dve.wait_ge(pe_done, (u + 2).v)
                    for n, b in enumerate((pb, pb + 1, 4 + pb // 2)):
                        last = nc.vector.tensor_copy(V[:, 2 * n:2 * n + 2, :].rearrange("p a e -> p (a e)"), BANK[b])
                    last.then_inc(evac_done, 1)
                    dve.wait_ge(evac_done, (u + 2).v)
                    gla_dir(hd, 0, pb)
                    split_lo(u + 3)
                    dve.wait_ge(pe_done, (u + 3).v)
                    nc.vector.tensor_copy(SG[0][:], BANK[pa])
                    nc.vector.tensor_copy(SG[1][:], BANK[pa + 1]).then_inc(evac_done, 1)
                    gla_dir(hd, 1, pb)
                    dve.wait_ge(o_rt, (hd + 1).v)
                    nc.vector.reciprocal(STAT[:, 4:8], STAT[:, 0:4]).then_inc(o_rs, 1)
                    dve.wait_ge(o_rs, (hd + 1).v)
                    for c in range(4):
                        last = nc.vector.tensor_scalar(DIAG[:, c, :], IDENT[:], STAT[:, 4 + c:5 + c], None, ALU.mult)
                    last.then_inc(o_diag, 1)
                    dve.wait_ge(o_rb, (hd + 1).v)
                    dve.wait_ge(sg_made, (hd.times(2) + 2).v)
                    for e in range(2):
                        nc.vector.tensor_tensor(KL[e][:], KL[e][:], BANK[7], ALU.mult).then_inc(o_xr, 1)
                    for e in range(2):
                        dve.wait_ge(o_xr, (hd.times(2) + (e + 1)).v)
                        o = O_T[:, bass.ds((hd.times(2) + e).v, 1), :].rearrange("p a t -> p (a t)")
                        nc.vector.scalar_tensor_tensor(o, KL[e][:], vec("gla_norm_2", e), SG[e][:], ALU.mult, ALU.mult).then_inc(o_done, 1)
            split_lo(at(U_K + 1))
            dve.wait_ge(pe_done, U_K + 1)
            assert U_K % 2 == 0
            for h in range(NKV):
                nc.vector.tensor_copy(K_RAW[:, h, 0:T], BANK[h])
            nc.vector.tensor_copy(K_RAW[:, :, T:TA], BANK[4].rearrange("p (h t) -> p h t", h=2)).then_inc(k_raw, 1)
            dve.wait_ge(k_raw, 1)
            nc.vector.tensor_copy(STAT[:, 63:64], EPS_C[:]).then_inc(evac_done, 1)
            dve.wait_ge(pe_done, U_V + 1)
            for n, b in enumerate((2, 3, 5)):
                last = nc.vector.tensor_copy(VA[:, 2 * n:2 * n + 2, :].rearrange("p a e -> p (a e)"), BANK[b])
            last.then_inc(evac_done, 1)
            dve.wait_ge(k_rt, 1)
            nc.vector.reciprocal(STAT[:, 12:24], STAT[:, 0:12]).then_inc(k_rs, 1)
            dve.wait_ge(k_rs, 1)
            for n in range(12):
                last = nc.vector.tensor_scalar(DIAG_K[:, n, :], IDENT[:], STAT[:, 12 + n:13 + n], None, ALU.mult)
            last.then_inc(k_diag, 1)
            dve.wait_ge(k_rb, 1)
            for h in range(NKV):
                nc.vector.scalar_tensor_tensor(K_X[:, h, 0:T], K_RAW[:, h, 0:T], vec("k_norm_2"), BANK[6 + h], ALU.mult, ALU.mult)
                nc.vector.scalar_tensor_tensor(KR[:, h, T:TA], K_RAW[:, h, T:TA], vec("k_norm_2"),
                                               BANK[0][:, TC * h:TC * (h + 1)], ALU.mult, ALU.mult).then_inc(k_x, 1)
            dve.wait_ge(tab3_landed, 48)
            dve.wait_ge(k_rot, 1)
            for h in range(NKV):
                nc.vector.tensor_tensor(KR[:, h, 0:T], K_X[:, h, 0:T], COS[:], ALU.mult).then_inc(k_cos, 1)
                nc.vector.tensor_tensor(TQ[h][:], BANK[6 + h], SIN[:], ALU.mult).then_inc(k_sin, 1)
                dve.wait_ge(k_sin, h + 1)
                nc.vector.tensor_tensor(KR[:, h, 0:T], KR[:, h, 0:T], TQ[h][:], ALU.add).then_inc(k_made, 1)
            split_lo(at(U_V + 1))
            with dve.Fori(0, NKV) as kv:
                for ui in range(2):
                    qi, u = At(ui, kv, 2), At(U_Q + ui, kv, 2)
                    pb = 2 * u.slot
                    if ui == 0:
                        nc.vector.tensor_copy(VS[:], VA[:, :, bass.ds(At(0, kv, HD).v, HD)]).then_inc(vs_made, 1)
                    split_lo(u + 1)
                    dve.wait_ge(pe_done, (u + 1).v)
                    dve.wait_ge(q_sq, (qi.times(2) + 2).v)
                    nc.vector.tensor_scalar(QX[0][:], BANK[pb], vec("q_norm_2"), None, ALU.mult)
                    nc.vector.tensor_scalar(QX[1][:], BANK[pb + 1], vec("q_norm_2"), None, ALU.mult).then_inc(evac_done, 1)
                    dve.wait_ge(q_rt, (qi + 1).v)
                    nc.vector.reciprocal(STAT[:, 8:16], STAT[:, 0:8]).then_inc(q_rs, 1)
                    dve.wait_ge(q_rs, (qi + 1).v)
                    nc.vector.tensor_scalar(STAT[:, 16:24], STAT[:, 8:16], HD ** -0.5, None, ALU.mult)
                    nc.vector.tensor_scalar(STAT[:, 24:32], STAT[:, 8:16], -HD ** -0.5, None, ALU.mult).then_inc(q_sc, 1)
                    dve.wait_ge(q_sc, (qi + 1).v)
                    for m in range(2):
                        nc.vector.tensor_tensor(QR[m][:], QX[m][:], COS[:], ALU.mult).then_inc(q_cos, 1)
                        nc.vector.tensor_tensor(TQ[m][:], BANK[4 + m], SIN[:], ALU.mult).then_inc(q_sin, 1)
                        dve.wait_ge(q_sin, (qi.times(2) + (m + 1)).v)
                        nc.vector.tensor_tensor(QR[m][:], QR[m][:], TQ[m][:], ALU.add).then_inc(q_made, 1)
                    for m in range(2):
                        a = At(2 * ui + m, kv, 4)

                        def bias(c):
                            n = a.times(4) + (c + 1)
                            dve.wait_ge(sc_made, n.v)
                            nc.vector.tensor_reduce(STAT[:, 32 + c % 2:33 + c % 2], WIDE[4 + 2 * (c % 2)], AX.X, ALU.max).then_inc(mx_made, 1)
                            dve.wait_ge(mx_made, n.v)
                            nc.vector.tensor_tensor(STAT[:, 34 + c % 2:35 + c % 2], STAT[:, 32 + c % 2:33 + c % 2],
                                                    STAT[:, 24 + 4 * m + c:25 + 4 * m + c], ALU.mult).then_inc(nb_made, 1)

                        def normalise(c):
                            n = a.times(4) + (c + 1)
                            dve.wait_ge(p_exp, n.v)
                            nc.vector.reciprocal(STAT[:, 38 + c % 2:39 + c % 2], STAT[:, 36 + c % 2:37 + c % 2]).then_inc(p_rr, 1)
                            dve.wait_ge(p_rr, n.v)
                            nc.vector.tensor_scalar(PP[c % 2][:], PP[c % 2][:], STAT[:, 38 + c % 2:39 + c % 2], None, ALU.mult).then_inc(p_norm, 1)

                        bias(0)
                        for c in range(1, 4):
                            bias(c)
                            normalise(c - 1)
                        normalise(3)
                        dve.wait_ge(pv_made, (a + 1).v)
                        at_tile = AT_T[:, bass.ds(a.v, 1), :].rearrange("p a t -> p (a t)")
                        nc.vector.tensor_copy(at_tile, BANK[4]).then_inc(at_made, 1)
            for k in range(KD):
                dve.wait_ge(a_hi_made, k + 1)
                nc.vector.tensor_tensor(A_LO[:, k, :], AT_T[:, k, :], A_HI[:, k, :].bitcast(F32), ALU.subtract).then_inc(a_ready, 1)
            dve.wait_ge(a_ready, KD)
            for k in range(KD):
                dve.wait_ge(a_hi_made, KD + k + 1)
                nc.vector.tensor_tensor(L_LO[:, k, :], O_T[:, k, :], L_HI[:, k, :].bitcast(F32), ALU.subtract).then_inc(a_ready, 1)
            with dve.Fori(0, KD) as i:
                u = At(U_D, i, 2)
                m = At(0, i, 1)
                y = Y[:, bass.ds(m.v, 1), :].rearrange("p a t -> p (a t)")
                split_lo(u + 1)
                dve.wait_ge(evac_done, (u + 1).v)
                split_lo(u + 2)
                dve.wait_ge(pe_done, (u + 2).v)
                nc.vector.tensor_tensor(y, SGB[0][:], BANK[2], ALU.mult).then_inc(y_a, 1)
                nc.vector.tensor_tensor(SGB[1][:], SGB[1][:], BANK[3], ALU.mult).then_inc(y_g, 1)
                dve.wait_ge(y_g, (m + 1).v)
                nc.vector.tensor_tensor(y, y, SGB[1][:], ALU.add).then_inc(evac_done, 1)
            for k in range(KD):
                dve.wait_ge(y_hi_made, k + 1)
                nc.vector.tensor_tensor(H_LO[:, k, 0:T], Y[:, k, :], H_HI[:, k, 0:T].bitcast(F32), ALU.subtract).then_inc(y_ready, 1)

            def out_pair(j):
                u = j + U_WO
                split_lo(u + 1)
                dve.wait_ge(pe_done, (u + 1).v)
                for a in range(2):
                    last = add_branch(j.times(2) + a, BANK[2 * u.slot + a], 6)
                last.then_inc(evac_done, 1)

            each(dve, 4, 0, 2, out_pair)
            norm_split(8, 7)

            def quarter(q, last_one=False):
                for j in range(4):
                    u = q.times(8) + (U_MLP + j)
                    split_lo(u + 1)
                    for m in range(2):
                        t = 2 * j + m
                        n = q.times(8) + (t + 1)
                        dve.wait_ge(relu_made, n.v)
                        mul = nc.vector.tensor_tensor(GT[m][:], SA[m][:], BANK[2 * u.slot + m], ALU.mult)
                        if m == 1:
                            mul.then_inc(evac_done, 1)
                            dve.wait_ge(evac_done, (u + 1).v)
                        else:
                            mul.then_inc(y_a, 1)
                            dve.wait_ge(y_a, (q.times(4) + (KD + j + 1)).v)
                        nc.vector.tensor_copy(G_HI[:, t, :], GT[m][:]).then_inc(m_hi_made, 1)
                        dve.wait_ge(m_hi_made, n.v)
                        nc.vector.tensor_tensor(G_LO[:, t, :], GT[m][:], G_HI[:, t, :].bitcast(F32), ALU.subtract).then_inc(m_ready, 1)
                for j in range(4):
                    u = q.times(8) + (U_MLP + 4 + j)
                    if not (last_one and j == 3):
                        split_lo(u + 1)
                    dve.wait_ge(pe_done, (u + 1).v)
                    for m in range(2):
                        last = add_branch(at(2 * j + m), BANK[2 * u.slot + m], 7)
                    last.then_inc(evac_done, 1)

            with dve.Fori(0, 3) as i:
                quarter(At(0, i, 1))
            quarter(at(3), True)

        @block.tensor
        def _(pe):
            def products(u, kt, tiles, rhs_hi, rhs_lo, ready=None, banks=None, cols=T, bank_cols=0, first=True):
                if first:
                    pe.wait_ge(lo_done, (u + 1).v)
                    wait(pe, evac_done, u - 1)
                banks = banks or [BANK[2 * u.slot + m] for m in range(tiles)]
                n = kt * tiles * P
                hi = W_HI[u.slot][:, 0:n].rearrange("p (k m) -> p k m", k=kt)
                lo = W_LO[u.slot][:, 0:n].rearrange("p (k m) -> p k m", k=kt)
                for k in range(kt):
                    if ready:
                        ready(k)
                    for m in range(tiles):
                        dst = banks[m][:, bank_cols:bank_cols + cols]
                        c = slice(m * P, (m + 1) * P)
                        pe.matmul(dst, hi[:, k, c], rhs_hi(k), start=(k == 0), stop=False)
                        pe.matmul(dst, hi[:, k, c], rhs_lo(k), start=False, stop=False)
                        last = pe.matmul(dst, lo[:, k, c], rhs_hi(k), start=False, stop=(k == kt - 1))
                return last

            def h_part(b, a=0, n=T):
                return lambda k: b[:, k, a:a + n]

            def mod_sums(g):
                for h in range(2):
                    pe.wait_ge(ada_used[h], 8 * g + 8)
                wait(pe, mod_read, at(MOD_READ.get(g - 1, 0)))
                for t in range(24):
                    last = pe.matmul(BANK[7][:, t:t + 1], ACC[:, t * P:(t + 1) * P], ONES[:, 0:1], start=True, stop=True)
                if g == 6:
                    for t in range(16):
                        last = pe.matmul(BANK[7][:, 24 + t:25 + t], ACC_C[:, t * P:(t + 1) * P], ONES[:, 0:1], start=True, stop=True)
                last.then_inc(mod_summed, 1)

            def norm(r):
                pe.wait_ge(sq_summed, KD * (r + 1))
                for c in range(4):
                    last = pe.matmul(BANK[6][:, c:c + 1], SSQ[:, c * P:(c + 1) * P], ONES_D[:, 0:1], start=True, stop=True)
                last.then_inc(ms_made, 1)
                pe.wait_ge(diag_made, 4 * (r + 1))
                for c in range(4):
                    last = pe.matmul(BANK[5][:, c * P:(c + 1) * P], ONES[:], DIAG[:, c, :], start=True, stop=True)
                last.then_inc(rb_made, 1)

            def ffn(f):
                for half in range(2):
                    g = FFN_GROUPS[f][half]
                    base = U_FFN[f] + half * (IN_UNITS + OUT_UNITS)
                    q0 = (2 * f + half) * FH
                    pe.wait_ge(lo_done, base + 1)
                    if half == 0:
                        pe.wait_ge(h_ready, H_BASE[FFN_NORM[f]] + 1)

                    def in_unit(j):
                        ready = None
                        if half == 0 and j.base == 0 :
                            ready = lambda k: pe.wait_ge(h_ready, H_BASE[FFN_NORM[f]] + k + 1)
                        products(j + base, KD, 2, h_part(H_HI), h_part(H_LO), ready).then_inc(pe_done, 1)

                    each(pe, IN_UNITS, 0 if base else 2, 1, in_unit)

                    def out_unit(m):
                        ready = (lambda k: pe.wait_ge(g_ready, q0 + k + 1)) if m.base == 0 else None
                        products(m + (base + IN_UNITS), FH, 1, h_part(G_HI), h_part(G_LO), ready).then_inc(pe_done, 1)
                        if g is not None and m.i is None and m.base == 6:
                            mod_sums(g)

                    each(pe, OUT_UNITS, 2, 2, out_unit)

            pe.wait_ge(tab_landed, 16)
            pe.wait_ge(vec_landed, 16 * N_VEC_DMAS)
            for t in range(NVT):
                n = min(P, NVEC - t * P)
                last = pe.transpose(BANK[6][:, t * P:t * P + n], V_ROWS[0:n, t, :], IDENT[0:n, 0:n])
            last.then_inc(vec_turned, 1)
            pe.wait_ge(in_landed, 16)
            for k in range(KD):
                wait(pe, x_made, at(k - 3))
                for c in range(4):
                    last = pe.transpose(BANK[k % 4][:, c * P:(c + 1) * P], X_ROWS[:, c, k * P:(k + 1) * P], IDENT[:])
                last.then_inc(x_turned, 1)
            pe.wait_ge(const_ready, 3)
            pe.wait_ge(vec_ready, 1)
            norm(0)
            mod_sums(0)
            ffn(0)
            norm(1)
            pe.wait_ge(lo_done, U_POOL + 1)
            hi = W_HI[U_POOL % 2][:].rearrange("p (g k m) -> p g k m", g=4, k=2)
            lo = W_LO[U_POOL % 2][:].rearrange("p (g k m) -> p g k m", g=4, k=2)
            for gi in range(4):
                pe.wait_ge(p_ready, 2 * gi + 2)
                if gi >= 2:
                    pe.wait_ge(pool_added, gi - 1)
                for m in range(2):
                    dst = BANK[2 * (gi % 2) + m][:]
                    for k in range(2):
                        kk, cc = 2 * gi + k, slice(m * P, (m + 1) * P)
                        pe.matmul(dst, hi[:, gi, k, cc], H_HI[:, kk, 0:T], start=(k == 0), stop=False)
                        pe.matmul(dst, hi[:, gi, k, cc], H_LO[:, kk, 0:T], start=False, stop=False)
                        last = pe.matmul(dst, lo[:, gi, k, cc], H_HI[:, kk, 0:T], start=False, stop=(k == 1))
                last.then_inc(pool_mm if gi < 3 else pe_done, 1)
            norm(2)
            ffn(1)
            norm(3)
            ffn(2)
            norm(4)

            def cv_unit(j):
                ready = (lambda k: pe.wait_ge(h_ready, H_BASE[4] + k + 1)) if j.base == 0 else None
                products(j + U_CONV, KD, 2, h_part(H_HI), h_part(H_LO), ready).then_inc(pe_done, 1)

            each(pe, 8, 0, 0, cv_unit)
            each(pe, 4, 0, 0, lambda j: products(j + (U_CONV + 8), KD, 2, h_part(H_HI), h_part(H_LO)).then_inc(pe_done, 1))

            def out_pair(j):
                ready = (lambda k: pe.wait_ge(z_ready, k + 1)) if j.base == 0 else None
                products(j + (U_CONV + 12), KD, 2, h_part(Z_HI), h_part(Z_LO), ready).then_inc(pe_done, 1)

            each(pe, 4, 0, 2, out_pair)
            norm(5)
            ffn(3)
            norm(6)
            norm(7)
            pe.wait_ge(c_landed, 16)
            for k in range(KD):
                for c in range(2):
                    last = pe.transpose(BANK[k // 2][:, TC * (k % 2) + c * P:TC * (k % 2) + (c + 1) * P], C_ROWS[:, c, k * P:(k + 1) * P], IDENT[:])
                last.then_inc(c_turned, 1)
            pe.wait_ge(csq_summed, KD)
            for c in range(2):
                last = pe.matmul(BANK[7][:, c:c + 1], SSQ[:, c * P:(c + 1) * P], ONES_D[:, 0:1], start=True, stop=True)
            last.then_inc(cms_made, 1)
            pe.wait_ge(cdiag_made, 2)
            for c in range(2):
                last = pe.matmul(BANK[6][:, c * P:(c + 1) * P], ONES[:], DIAG[:, c, :], start=True, stop=True)
            last.then_inc(crb_made, 1)
            pe.wait_ge(h_ready, H_BASE[7] + 2 * KD)

            def exact(dst, a_hi, a_lo, b_hi, b_lo, first, last):
                pe.matmul(dst, a_hi, b_hi, start=first, stop=False)
                pe.matmul(dst, a_hi, b_lo, start=False, stop=False)
                return pe.matmul(dst, a_lo, b_hi, start=False, stop=last)

            def ctx_products(u, cols, width, dst):
                hi = W_HI[u.slot][:, 0:KD * width].rearrange("p (k m) -> p k m", k=KD)
                lo = W_LO[u.slot][:, 0:KD * width].rearrange("p (k m) -> p k m", k=KD)
                for k in range(KD):
                    last = exact(dst, hi[:, k, cols], lo[:, k, cols], H_HI[:, k, T:TA], H_LO[:, k, T:TA], k == 0, k == KD - 1)
                return last

            def token_products(u, banks):
                pe.wait_ge(lo_done, (u + 1).v)
                wait(pe, evac_done, u - 1)
                hi = W_HI[u.slot][:].rearrange("p (k m) -> p k m", k=KD)
                lo = W_LO[u.slot][:].rearrange("p (k m) -> p k m", k=KD)
                for t in range(TA // P):
                    dst = banks[t // 2][:, DV * (t % 2):DV * (t % 2 + 1)]
                    for k in range(KD):
                        last = exact(dst, H_HI[:, k, t * P:(t + 1) * P], H_LO[:, k, t * P:(t + 1) * P], hi[:, k, :], lo[:, k, :], k == 0, k == KD - 1)
                return last

            u = at(U_LR)
            r = slice(0, 2 * RANK)
            pe.wait_ge(lo_done, U_LR + 1)
            pe.wait_ge(evac_done, U_LR)
            hi = W_HI[u.slot][:, 0:KD * 2 * RANK].rearrange("p (k m) -> p k m", k=KD)
            lo = W_LO[u.slot][:, 0:KD * 2 * RANK].rearrange("p (k m) -> p k m", k=KD)
            for dst, a, b in ((BANK[2 * u.slot][r, :], 0, T), (BANK[4 + u.slot][r, 0:TC], T, TA)):
                for k in range(KD):
                    last = exact(dst, hi[:, k, :], lo[:, k, :], H_HI[:, k, a:b], H_LO[:, k, a:b], k == 0, k == KD - 1)
            last.then_inc(pe_done, 1)

            with pe.Fori(0, GH_ // 2) as i:
                for s in range(2):
                    hd, u = At(s, i, 2), At(U_G + 3 * s, i, 6)
                    pa, pb = 2 * (s % 2), 2 * ((s + 1) % 2)
                    products(u, KD, 2, h_part(H_HI), h_part(H_LO))
                    ctx_products(u, slice(0, P), 2 * P, BANK[4 + pa // 2][:, 0:TC]).then_inc(pe_done, 1)
                    token_products(u + 1, [BANK[pb], BANK[pb + 1], BANK[4 + pb // 2]]).then_inc(pe_done, 1)

                    def gate_z(d):
                        for a, b in ((0, T), (T, TA)):
                            last = pe.matmul(PS[:, 6 * T + a:6 * T + b], W_GK[0:2 * RANK, d, :], LRT[0:2 * RANK, a:b], start=True, stop=True)
                        last.then_inc(z_made, 1)

                    def states(d):
                        zd = hd.times(2) + (d + 1)
                        pe.wait_ge(kd_made, zd.v)
                        for t in range(TA // P):
                            last = pe.transpose(PS[:, 6 * T + t * P:6 * T + (t + 1) * P], T2[:, t * P:(t + 1) * P], IDENT[:])
                        last.then_inc(kdt_t, 1)
                        pe.wait_ge(kdt_made, zd.v)
                        if d == 1:
                            pe.wait_ge(st_made, (hd.times(8) + 4).v)
                        for n, c in enumerate((0, 1, 2) if d == 0 else (3, 2, 1)):
                            pe.matmul(PS[:, pb * T + n * DV:pb * T + (n + 1) * DV], KDT[:, c, :], V[:, c, :], start=True, stop=True)
                        for t in (4, 5):
                            last = pe.matmul(PS[:, pb * T + 3 * DV:pb * T + 4 * DV], KDT[:, t, :], V[:, t, :], start=(t == 4), stop=(t == 5))
                        last.then_inc(sp_made, 1)

                    def levels(d):
                        for n in range(len(LEVELS)):
                            slot = (7 * d + n) % 2
                            lv = hd.times(14) + (7 * d + n + 1)
                            pe.wait_ge(lv_q, lv.v)
                            pe.wait_ge(lv_k, lv.v)
                            if 7 * d + n >= 2:
                                pe.wait_ge(lv_cp, (lv - 2).v)
                            for c in range(NC_):
                                cc = slice(c * CH, (c + 1) * CH)
                                last = pe.matmul(BANK[6 + slot][:, cc], KL[slot][:, cc], QL[slot][:, cc], start=True, stop=True)
                            last.then_inc(lv_mm, 1)

                    pe.wait_ge(evac_done, (u + 1).v)
                    pe.wait_ge(wgk_landed, (hd.times(32) + 32).v)
                    gate_z(0)
                    pe.wait_ge(evac_done, (u + 2).v)
                    for c in range(NC_):
                        cc = slice(c * CH, (c + 1) * CH)
                        last = pe.matmul(BANK[4 + pb // 2][:, cc], KT[:, cc], QT[:, cc], start=True, stop=True)
                    last.then_inc(dg_mm, 1)
                    states(0)
                    products(u + 2, KD, 2, h_part(H_HI), h_part(H_LO)).then_inc(pe_done, 1)
                    levels(0)
                    pe.wait_ge(lv_cp, (hd.times(14) + 7).v)
                    gate_z(1)
                    states(1)
                    levels(1)
                    pe.wait_ge(st_made, (hd.times(8) + 8).v)
                    pe.wait_ge(lv_cp, (hd.times(14) + 14).v)
                    for e in range(2):
                        ee = slice(e * P, (e + 1) * P)
                        for c in range(NC_):
                            cc = slice(c * CH, (c + 1) * CH)
                            dst = BANK[pb + e][:, cc]
                            pe.matmul(dst, V[:, c, ee], AM[:, cc], start=True, stop=False)
                            pe.matmul(dst, ST[0][:, c, ee], QB[0][:, cc], start=False, stop=False)
                            last = pe.matmul(dst, ST[1][:, c, ee], QB[1][:, cc], start=False, stop=True)
                    last.then_inc(o_mm, 1)
                    pe.wait_ge(o_sq, (hd.times(2) + 2).v)
                    for c in range(NC_):
                        for e in range(2):
                            last = pe.matmul(BANK[6][:, c:c + 1], QL[e][:, c * CH:(c + 1) * CH], ONES_D[:, 1:2], start=(e == 0), stop=(e == 1))
                    last.then_inc(o_ms, 1)
                    pe.wait_ge(o_diag, (hd + 1).v)
                    for c in range(NC_):
                        last = pe.matmul(BANK[7][:, c * P:(c + 1) * P], ONES[:], DIAG[:, c, :], start=True, stop=True)
                    last.then_inc(o_rb, 1)
            u = at(U_K)
            products(u, KD, 2, h_part(H_HI), h_part(H_LO))
            for h in range(NKV):
                last = ctx_products(u, slice(h * P, (h + 1) * P), 2 * P, BANK[4][:, TC * h:TC * (h + 1)])
            last.then_inc(pe_done, 1)
            token_products(at(U_V), [BANK[2], BANK[3], BANK[5]]).then_inc(pe_done, 1)
            pe.wait_ge(k_sq, 2)
            pe.wait_ge(o_done, 2 * GH_)
            for h in range(NKV):
                for t in range(6):
                    last = pe.matmul(BANK[6][:, 6 * h + t:6 * h + t + 1], K_SQ[:, h, t * P:(t + 1) * P], ONES_HD[:, 0:1], start=True, stop=True)
            last.then_inc(k_ms, 1)
            pe.wait_ge(k_diag, 1)
            for h in range(NKV):
                for t in range(6):
                    dst = BANK[6 + h][:, t * P:(t + 1) * P] if t < 4 else BANK[0][:, TC * h + (t - 4) * P:TC * h + (t - 3) * P]
                    last = pe.matmul(dst, ONES[:], DIAG_K[:, 6 * h + t, :], start=True, stop=True)
            last.then_inc(k_rb, 1)
            pe.wait_ge(k_x, 2)
            pe.wait_ge(tab3_landed, 48)
            for h in range(NKV):
                last = pe.matmul(BANK[6 + h], PERM[:], K_X[:, h, 0:T], start=True, stop=True)
            last.then_inc(k_rot, 1)
            pe.wait_ge(k_made, 2)
            with pe.Fori(0, NKV) as kv:
                for ui in range(2):
                    qi, u = At(ui, kv, 2), At(U_Q + ui, kv, 2)
                    pe.wait_ge(vs_made, At(1, kv, 1).v)
                    if ui == 1:
                        pe.wait_ge(at_made, At(2, kv, 4).v)
                    products(u, KD, 2, h_part(H_HI), h_part(H_LO)).then_inc(pe_done, 1)
                    pe.wait_ge(q_sq, (qi.times(2) + 2).v)
                    for m in range(2):
                        for c in range(4):
                            last = pe.matmul(BANK[6][:, 4 * m + c:4 * m + c + 1], Q_SQ[m][:, c * P:(c + 1) * P], ONES_HD[:, 0:1], start=True, stop=True)
                    pe.wait_ge(evac_done, (u + 1).v)
                    for m in range(2):
                        last = pe.matmul(BANK[4 + m], PERM[:], QX[m][:], start=True, stop=True)
                    last.then_inc(q_rot, 1)
                    for m in range(2):
                        a = At(2 * ui + m, kv, 4)

                        def scores(c):
                            n = a.times(4) + c
                            if c >= 2 or m == 1:
                                pe.wait_ge(p_exp, (n - 1).v)
                            if c == 0:
                                pe.wait_ge(q_made, (qi.times(2) + 2).v)
                                if m == 1:
                                    pe.wait_ge(at_made, a.v)
                            q = QR[m][:, c * P:(c + 1) * P]
                            for x0, x1 in ((0, T), (T, TA)):
                                keys = KR[:, bass.ds(At(0, kv, 1).v, 1), x0:x1].rearrange("p a t -> p (a t)")
                                last = pe.matmul(WIDE[4 + 2 * (c % 2)][:, x0:x1], q, keys, start=True, stop=True)
                            last.then_inc(sc_made, 1)

                        def turn(c):
                            n = a.times(4) + c
                            pe.wait_ge(p_norm, (n + 1).v)
                            if c >= 2 or m == 1:
                                pe.wait_ge(pt_made, (n - 1).v)
                            for t in range(6):
                                last = pe.transpose(WIDE[2 * (c % 2)][:, t * P:(t + 1) * P], PP[c % 2][:, t * P:(t + 1) * P], IDENT[:])
                            last.then_inc(p_t, 1)

                        scores(0)
                        for c in range(1, 4):
                            scores(c)
                            turn(c - 1)
                        turn(3)
                        pe.wait_ge(pt_made, (a.times(4) + 4).v)
                        for t in range(6):
                            last = pe.matmul(BANK[4], VS[:, t, :], PT[:, t, :], start=(t == 0), stop=(t == 5))
                        last.then_inc(pv_made, 1)
            pe.wait_ge(at_made, NQ)
            with pe.Fori(0, KD) as i:
                u = At(U_D, i, 2)
                products(u, KD, 2, h_part(H_HI), h_part(H_LO)).then_inc(pe_done, 1)
                u = u + 1
                pe.wait_ge(lo_done, (u + 1).v)
                pe.wait_ge(evac_done, (u - 1).v)
                hi = W_HI[u.slot][:].rearrange("p (k m) -> p k m", k=KD)
                lo = W_LO[u.slot][:].rearrange("p (k m) -> p k m", k=KD)
                for m, (x_hi, x_lo) in enumerate(((A_HI, A_LO), (L_HI, L_LO))):
                    mm = slice(m * P, (m + 1) * P)
                    for k in range(KD):
                        pe.wait_ge(a_ready, KD * m + k + 1)
                        last = exact(BANK[2 + m], hi[:, k, mm], lo[:, k, mm], x_hi[:, k, :], x_lo[:, k, :], k == 0, k == KD - 1)
                last.then_inc(pe_done, 1)

            def out_pair(j):
                ready = (lambda k: pe.wait_ge(y_ready, k + 1)) if j.base == 0 else None
                products(j + U_WO, KD, 2, h_part(H_HI), h_part(H_LO), ready).then_inc(pe_done, 1)

            each(pe, 4, 0, 2, out_pair)
            norm(8)

            def quarter(q):
                for j in range(4):
                    ready = (lambda k: pe.wait_ge(h_ready, H_BASE[8] + k + 1)) if j == 0 else None
                    products(q.times(8) + (U_MLP + j), KD, 2, h_part(H_HI), h_part(H_LO), ready).then_inc(pe_done, 1)
                for j in range(4):
                    ready = (lambda k: pe.wait_ge(m_ready, (q.times(8) + (k + 1)).v)) if j == 0 else None
                    products(q.times(8) + (U_MLP + 4 + j), KD, 2, h_part(G_HI), h_part(G_LO), ready).then_inc(pe_done, 1)

            with pe.Fori(0, 3) as i:
                quarter(At(0, i, 1))
            quarter(at(3))
            pe.wait_ge(evac_done, N_UNITS)
            for c in range(4):
                wait(pe, out_made, at(c - 1))
                for f in range(KD):
                    last = pe.transpose(PS[:, 2 * T * (c % 2) + f * P:2 * T * (c % 2) + (f + 1) * P], X[:, f, c * P:(c + 1) * P], IDENT[:])
                last.then_inc(row_t, 1)


INPUTS = ("x", "c", "ada_w", "ada_b", "norm_g", "ffn_w_in", "ffn_w_out", "pool_w", "pool_scale",
          "conv_w_in", "conv_w", "conv_w_out", "final_g", "c_2", "ctx_2", "c_ctx_2", "w_ada_2",
          "b_ada_2", "norm1_2", "w_in_2", "q_norm_2", "k_norm_2", "w_gk_fwd_2", "b_gk_fwd_2",
          "w_gk_bwd_2", "b_gk_bwd_2", "gla_norm_2", "w_br_attn_2", "w_br_gla_2", "w_out_2",
          "norm2_2", "w_mlp1_2", "w_mlp2_2")


def kernel(**inputs):
    from concourse import bacc
    from concourse.bass_utils import run_bass_kernel_spmd

    nc = bacc.Bacc("TRN2", target_bir_lowering=False, num_devices=1)
    arrays, args = {}, {}
    for name, a in list((n, inputs[n]) for n in INPUTS) + list(host_tables().items()):
        a = np.ascontiguousarray(a)
        arrays[f"in_{name}"] = a
        args[name] = nc.dram_tensor(f"in_{name}", a.shape, mybir.dt.from_np(a.dtype), kind="ExternalInput").ap()
    out = nc.dram_tensor("out_0", (1, T, D), F32, kind="ExternalOutput").ap()
    build(nc, args, out[0])
    got = run_bass_kernel_spmd(nc, [arrays], core_ids=[0])
    return got.results[0]["out_0"]
```

```python
from contextlib import ExitStack

import numpy as np

import concourse.bass as bass
from concourse import mybir

P = 128
D = 1024
KD = D // P
T = 512
TC = 256
TA = T + TC
F = 2816
FH = F // P // 2
EPS = 1e-6
POOL_WINDOWS = (2, 4, 8, 16)
CONV_WIDTH = 3
HD = 128
NQ = 8
NKV = 2
GH_ = 4
DK = 128
DV = 256
RANK = 16
CH = 128
NC_ = T // CH
GRID_W = 64
F2 = 4096
LEVELS = (1, 2, 4, 8, 16, 32, 64)

ALU = mybir.AluOpType
ACT = mybir.ActivationFunctionType
F32 = mybir.dt.float32
F32R = mybir.dt.float32r
I32 = mybir.dt.int32
AX = mybir.AxisListType

IN_SIZES = (NKV * HD, NKV * HD, GH_ * DK, GH_ * DV, RANK, RANK, NQ * HD, GH_ * DK, GH_ * DV, D, D)
(C_AK, C_AV, C_GK, C_GV, C_LR, _, C_AQ, C_GQ, C_GO, C_GA, C_GG) = (
    int(x) for x in np.cumsum((0,) + IN_SIZES)[:-1])

VEC_ROWS = {}
_at = 0
for _name, _rows in (("c", 8), ("c_2", 8), ("c_ctx_2", 8), ("ada_b", 144), ("norm_g", 48),
                     ("pool_scale", 8), ("conv_w", 24), ("final_g", 8), ("b_ada_2", 48),
                     ("norm1_2", 8), ("norm2_2", 8), ("q_norm_2", 1), ("k_norm_2", 1),
                     ("b_gk_fwd_2", 4), ("b_gk_bwd_2", 4), ("gla_norm_2", 2)):
    VEC_ROWS[_name] = (_at, _rows)
    _at += _rows
NVEC = _at
NVT = -(-NVEC // P)
N_VEC_DMAS = sum((a + n - 1) // P - a // P + 1 for a, n in VEC_ROWS.values())

IN_UNITS = FH
OUT_UNITS = KD
FFN_UNITS = 2 * (IN_UNITS + OUT_UNITS)
U_FFN = [0, FFN_UNITS + 1, 2 * FFN_UNITS + 1, 3 * FFN_UNITS + 1 + 16]
U_POOL = FFN_UNITS
U_CONV = 3 * FFN_UNITS + 1
U_B2 = 4 * FFN_UNITS + 1 + 16
U_LR = U_B2
U_G = U_LR + 1
U_K, U_V, U_Q = U_G + 3 * GH_, U_G + 3 * GH_ + 1, U_G + 3 * GH_ + 2
U_D = U_Q + NQ // 2
U_WO = U_D + 16
U_MLP = U_WO + 4
N_UNITS = U_MLP + 32
FULL = 2048
OUT_SIZE = FH * P


def unit_size(n):
    for u in U_FFN:
        for h in range(2):
            o = u + h * (IN_UNITS + OUT_UNITS) + IN_UNITS
            if o <= n < o + OUT_UNITS:
                return OUT_SIZE
    return KD * 2 * RANK if n == U_LR else FULL


def host_tables():
    ident = np.eye(P, dtype=np.float32)
    half = HD // 2
    freqs = (10000.0 ** (-np.arange(0, half, 2, dtype=np.float32) / half)).astype(np.float32)
    t = np.arange(T)
    ang = np.stack([(t // GRID_W)[:, None].astype(np.float32) * freqs,
                    (t % GRID_W)[:, None].astype(np.float32) * freqs], axis=1)
    cos = np.zeros((HD, T), np.float32)
    sin = np.zeros((HD, T), np.float32)
    perm = np.zeros((HD, HD), np.float32)
    for d in range(HD):
        ax, ab, f = d // 64, (d // 32) % 2, d % 32
        cos[d] = np.cos(ang[:, ax, f])
        sin[d] = np.sin(ang[:, ax, f]) * (1 if ab else -1)
        perm[d, d ^ 32] = 1
    masks = np.zeros((P, len(LEVELS), P), np.int32)
    j, i = np.arange(P)[:, None], np.arange(P)[None, :]
    for n, s in enumerate(LEVELS):
        masks[:, n] = (j // (2 * s) == i // (2 * s)) & (j // s != i // s)
    keep = np.ones((P, T), np.float32)
    keep[:, ::CH] = 0
    pos = np.arange(16, dtype=np.float32) + 1
    edge = np.stack([np.where(pos < w, np.float32(w) / pos, 1) for w in POOL_WINDOWS])
    edge = np.broadcast_to(edge.astype(np.float32), (P, 4, 16))
    return {"t_ident": ident, "t_perm": perm, "t_cos": cos, "t_sin": sin, "t_masks": masks,
            "t_keep": keep, "t_edge": np.ascontiguousarray(edge)}


class At:

    def __init__(self, base, i=None, stride=0):
        self.base, self.i, self.stride = base, i, stride

    def __add__(self, n):
        return At(self.base + n, self.i, self.stride)

    def __sub__(self, n):
        return At(self.base - n, self.i, self.stride)

    @property
    def v(self):
        return self.base if self.i is None else self.i * self.stride + self.base

    def times(self, n):
        return At(self.base * n, self.i, self.stride * n)

    def half(self):
        return At(self.base // 2, self.i, self.stride // 2)

    @property
    def slot(self):
        return self.base % 2


def wait(eng, sem, at):
    assert at.base > 0 or at.i is None
    if at.base > 0:
        eng.wait_ge(sem, at.v)


def at(n):
    return At(n)


def spans(count, pre, post):
    out = [(n, 0) for n in range(pre)]
    pairs = (count - pre - post) // 2
    out.append((pre, pairs))
    out += [(n, 0) for n in range(pre + 2 * pairs, count)]
    return out


def each(eng, count, pre, post, step):
    for n, pairs in spans(count, pre, post):
        if pairs:
            with eng.Fori(0, pairs) as i:
                for s in range(2):
                    step(At(n + s, i, 2))
        else:
            step(At(n))


def build(nc, ins, out):
    ctx_ = ExitStack()
    with ctx_:
        def sb(name, shape, dt=F32):
            return ctx_.enter_context(nc.sbuf_tensor(name, shape, dt))

        def psum(name, shape):
            return ctx_.enter_context(nc.psum_tensor(name, shape, F32))

        def sem(name):
            return ctx_.enter_context(nc.semaphore(name))

        W_RAW = [sb(f"w_raw{s}", [P, FULL]) for s in range(2)]
        W_HI = [sb(f"w_hi{s}", [P, FULL], F32R) for s in range(2)]
        W_LO = [sb(f"w_lo{s}", [P, FULL], F32R) for s in range(2)]
        X = sb("x_res", [P, KD, T])
        H_HI = sb("h_hi", [P, KD, TA], F32R)
        H_LO = sb("h_lo", [P, KD, TA], F32R)
        IDENT = sb("ident", [P, P])
        ONES_D = sb("ones_d", [P, 2])
        ONES = sb("ones", [P, P])
        ONES_HD = sb("ones_hd", [P, 1])
        EPS_C = sb("eps_c", [P, 1])
        VECS = sb("vecs", [P, NVT * P])
        COND = sb("cond", [P, 24])
        MODS = sb("mods", [P, 8 * 24 + 16])
        GAIN = sb("gain", [P, 9 * KD])
        GATE = sb("gate", [P, 8 * KD])
        RSTD4 = sb("rstd4", [P, 8])
        DIAG = sb("diag", [P, 4, P])
        SSQ = sb("ssq", [P, T])
        FLEX_KB = 86
        FLEX = sb("flex", [P, FLEX_KB * 256])
        FLEX0 = nc.sbuf_base - FLEX_KB * 1024

        def view(name, kb, shape, dt=F32):
            return nc.alloc_sbuf_tensor_at(name, shape, dt, offset=FLEX0 + int(kb * 1024))

        G_HI = view("g_hi", 0, [P, FH, T], F32R)
        G_LO = view("g_lo", 22, [P, FH, T], F32R)
        ADA = [view(f"ada{h}", 44 + 6 * h, [P, 1536]) for h in range(2)]
        ADA_FIRST = ADA + [view(f"ada_first{n}", 20 + 6 * n, [P, 1536]) for n in range(4)]
        ACC = view("ada_acc", 56, [P, 3 * D])
        SA = [view(f"silu_a{s}", 68 + 2 * s, [P, T]) for s in range(2)]
        GT = [view(f"g_t{s}", 72 + 2 * s, [P, T]) for s in range(2)]
        ACC_C = view("ada_acc_ctx", 76, [P, 2 * D])
        X_ROWS = view("x_rows", 0, [P, 4, D])
        V_ROWS = view("vec_rows", 16, [P, NVT, P])
        PH = view("pool_h", 0, [P, KD, T])
        PS_A = view("pool_a", 16, [P, 2, T])
        PS_B = view("pool_b", 20, [P, 2, T])
        EDGE = view("pool_edge", 24, [P, 4, 16])
        U_T = [view(f"conv_u{s}", 32 + 3 * s, [P, T + 2]) for s in range(2)]
        C_T = [view(f"conv_c{s}", 38 + 2 * s, [P, T]) for s in range(2)]
        CV = view("conv_out", 16, [P, KD, T])
        Z_HI = view("z_hi", 0, [P, KD, T], F32R)
        Z_LO = view("z_lo", 16, [P, KD, T], F32R)

        C_ROWS = view("ctx_rows", 0, [P, 2, D])
        C_X = view("ctx_t", 8, [P, KD, TC])
        O_T = view("gla_out", 0, [P, KD, T])
        MASKS = view("masks", 16, [P, len(LEVELS), P], I32)
        KEEP = view("keep", 19.5, [P, T])
        W_GK = view("w_gk", 21.5, [P, 2, P])
        LRT = view("low_rank", 23, [P, TA])
        KQ = view("gla_kq", 26, [P, 2, TA])
        KT, QT = KQ[:, 0, :], KQ[:, 1, 0:T]
        V = view("gla_v", 32, [P, TA // P, DV])
        BB = view("gla_b", 38, [P, 2 * TA + 4])
        B = [BB[:, d * TA:(d + 1) * TA] for d in range(2)]
        T1 = view("gla_t1", 44.25, [P, TA])
        T2 = view("gla_t2", 47.25, [P, TA])
        SG = [view(f"gla_sg{n}", 44.25 + 2 * n, [P, T]) for n in range(2)]
        QB = [view(f"gla_qb{d}", 50.25 + 2 * d, [P, T]) for d in range(2)]
        KDT = view("gla_kdt", 54.25, [P, TA // P, P])
        ST = [view(f"gla_state{d}", 57.25 + 4 * d, [P, NC_, DV]) for d in range(2)]
        AM = view("gla_a", 65.25, [P, T])
        KQL = [view(f"gla_kql{n}", 67.5 + 4 * n, [P, 2, T]) for n in range(2)]
        EL = [view(f"gla_el{n}", 75.5 + 4 * n, [P, 2, T]) for n in range(2)]
        O_SQ = [KQL[0][:, n, :] for n in range(2)]
        O_N = [KQL[1][:, n, :] for n in range(2)]
        AT_T = view("attn_out", 16, [P, KD, T])
        KR = view("attn_k", 32, [P, NKV, TA])
        K_LO = view("attn_k_lo", 32, [P, NKV, TA], F32R)
        K_HI = view("attn_k_hi", 80, [P, NKV, TA], F32R)
        VA = view("attn_v", 38, [P, TA // P, NKV * HD])
        K_RAW = view("attn_k_raw", 44, [P, NKV, TA])
        K_X = view("attn_k_x", 50, [P, NKV, TA])
        K_SQ = view("attn_k_sq", 56, [P, NKV, TA])
        DIAG_K = view("attn_diag", 66, [P, 12, P])
        PT = view("attn_pt", 44, [P, TA // P, T])
        PP = [view(f"attn_p{n}", 56 + 3 * n, [P, TA]) for n in range(2)]
        QX = [view(f"attn_qx{n}", 62 + 2 * n, [P, T]) for n in range(2)]
        Q_SQ = [view(f"attn_qsq{n}", 66 + 2 * n, [P, T]) for n in range(2)]
        Q_HI = [view(f"attn_q_hi{n}", 66 + 2 * n, [P, T], F32R) for n in range(2)]
        VS = view("attn_vs", 70, [P, TA // P, HD])
        COS = view("cos", 74, [P, T])
        SIN = view("sin", 76, [P, T])
        PERM = view("perm", 78, [P, P])
        TQ = [view(f"attn_tq{n}", 2 * n - 4, [P, T]) for n in range(2)]
        Q_LO = [view(f"attn_q_lo{n}", 2 * n - 4, [P, T], F32R) for n in range(2)]
        A_HI = view("a_hi", 32, [P, KD, T], F32R)
        A_LO = view("a_lo", 48, [P, KD, T], F32R)
        L_HI = view("l_hi", 64, [P, KD, T], F32R)
        L_LO = view("l_lo", 16, [P, KD, T], F32R)
        Y = view("merged", 0, [P, KD, T])
        SGB = [view(f"branch_gate{n}", 80 + 2 * n, [P, T]) for n in range(2)]
        STAT = sb("stat", [P, 64])

        PS = psum("ps", [P, 8 * T])
        BANK = [PS[:, b * T:(b + 1) * T] for b in range(8)]
        WIDE = {b: PS[:, b * T:b * T + TA] for b in (0, 2, 4, 6)}

        landed = [sem(f"w_landed{s}") for s in range(2)]
        hi_done = sem("hi_done")
        lo_done = sem("lo_done")
        pe_done = sem("pe_done")
        evac_done = sem("evac_done")
        silu_made = sem("silu_made")
        g_hi_made = sem("g_hi_made")
        g_ready = sem("g_ready")
        ada_landed = [sem(f"ada_landed{h}") for h in range(2)]
        first_landed = [sem(f"ada_first_landed{n}") for n in range(6)]
        ada_used = [sem(f"ada_used{h}") for h in range(2)]
        acc_cleared = sem("acc_cleared")
        mod_summed = sem("mod_summed")
        mod_read = sem("mod_read")
        mod_done = sem("mod_done")
        const_ready = sem("const_ready")
        in_landed = sem("in_landed")
        vec_landed = sem("vec_landed")
        tab_landed = sem("tab_landed")
        vec_turned = sem("vec_turned")
        vec_ready = sem("vec_ready")
        cond_ready = sem("cond_ready")
        x_turned = sem("x_turned")
        x_made = sem("x_made")
        sq_made = sem("sq_made")
        sq_summed = sem("sq_summed")
        ms_made = sem("ms_made")
        rt_made = sem("rt_made")
        rs_made = sem("rs_made")
        diag_made = sem("diag_made")
        rb_made = sem("rb_made")
        xr_made = sem("xr_made")
        h_made = sem("h_made")
        h_hi_made = sem("h_hi_made")
        h_ready = sem("h_ready")
        pool_step = sem("pool_step")
        pool_mixed = sem("pool_mixed")
        pool_mm = sem("pool_mm")
        pool_added = sem("pool_added")
        cv_zero = sem("cv_zero")
        p_hi_made = sem("p_hi_made")
        p_ready = sem("p_ready")
        cv_c = sem("cv_c")
        cv_1 = sem("cv_1")
        cv_2 = sem("cv_2")
        cv_3 = sem("cv_3")
        cz_made = sem("cz_made")
        z_hi_made = sem("z_hi_made")
        z_ready = sem("z_ready")
        (c_landed, c_turned, c_made, csq_made, csq_summed, cms_made, crt_made, crs_made, cdiag_made,
         crb_made, cxr_made, ch_made, tab2_landed, wgk_zero, wgk_landed, z_made, z_out, z_min,
         z_exp, z_ln, g_made, b_made, kd_arg, kd_e, eb_made, kd_made, qb_made, kdt_t, kdt_made,
         sp_made, st_made, lv_d, lv_e, lv_k, lv_mm, lv_cp, dg_mm, dg_made, o_mm, o_cp, o_sq, o_ms,
         o_rt, o_rs, o_diag, o_rb, o_xr, o_done, tab3_landed, k_raw, k_sq, k_ms, k_rt, k_rs, k_diag,
         k_rb, k_x, k_rot, k_cos, k_sin, k_made, vs_made, q_sq, q_rot, q_rt, q_rs, q_sc, q_cos,
         q_sin, q_made, k_hi_made, k_ready, q_sum, q_hi_made, sc_made, mx_made, nb_made, p_exp,
         p_rr, p_norm, p_t, pt_made, pv_made, at_made, a_hi_made, a_ready, sig_made, y_a, y_g,
         y_hi_made, y_ready, relu_made, m_hi_made, m_ready, row_t) = (
         sem(n) for n in """
            c_landed c_turned c_made csq_made csq_summed cms_made crt_made crs_made
            cdiag_made crb_made cxr_made ch_made tab2_landed wgk_zero wgk_landed z_made
            z_out z_min z_exp z_ln g_made b_made kd_arg kd_e eb_made kd_made qb_made kdt_t
            kdt_made sp_made st_made lv_d lv_e lv_k lv_mm lv_cp dg_mm dg_made o_mm o_cp o_sq
            o_ms o_rt o_rs o_diag o_rb o_xr o_done tab3_landed k_raw k_sq k_ms k_rt k_rs
            k_diag k_rb k_x k_rot k_cos k_sin k_made vs_made q_sq q_rot q_rt q_rs q_sc q_cos
            q_sin q_made k_hi_made k_ready q_sum q_hi_made sc_made mx_made nb_made p_exp
            p_rr p_norm p_t pt_made pv_made at_made a_hi_made a_ready sig_made y_a y_g
            y_hi_made y_ready relu_made m_hi_made m_ready row_t
            """.split())
        out_made = sem("out_made")
        out_sem = sem("out_written")

        def vec(name, n=0):
            return VECS[:, VEC_ROWS[name][0] + n:VEC_ROWS[name][0] + n + 1]

        def vecs(name, a, b):
            return VECS[:, VEC_ROWS[name][0] + a:VEC_ROWS[name][0] + b]

        def ada_view(g):
            w = ins["ada_w"][g // 3] if g < 6 else ins["w_ada_2"][0]
            return w.rearrange("(k p) m -> p k m", p=P), 3 * D * (g % 3)

        FFN_GROUPS = [(1, 2), (3, 4), (5, 6), (7, None)]
        FFN_NORM = [0, 2, 3, 5]
        FFN_NEXT = [1, 3, 4, 6]
        EARLY = {OUT_UNITS - 2: range(5), OUT_UNITS - 1: (5, 6)}
        H_BASE = {0: 0, 2: 8, 3: 16, 4: 24, 5: 32, 7: 40, 8: 56}
        MOD_READ = {g: g + 1 for g in range(6)} | {6: 8, 7: 9}
        MOD_DONE = {g: 2 * g + 2 for g in range(6)} | {6: 15, 7: 17}

        block = ctx_.enter_context(nc.Block())

        @block.sync
        def _(sp):
            sp.dma_start(X_ROWS[:], ins["x"][0].rearrange("(c p) d -> p c d", p=P)).then_inc(in_landed, 16)
            for name, (row, rows) in VEC_ROWS.items():
                flat = ins[name]
                while len(flat.shape) > 1:
                    flat = flat.rearrange("a b c -> (a b) c") if len(flat.shape) == 3 else flat.rearrange("a b -> (a b)")
                src = flat.rearrange("(r q) -> r q", q=P)
                done = 0
                while done < rows:
                    r = row + done
                    n = min(rows - done, P - r % P)
                    sp.dma_start(V_ROWS[r % P:r % P + n, r // P, :], src[done:done + n, :]).then_inc(vec_landed, 16)
                    done += n
            sp.dma_start(IDENT[:], ins["t_ident"]).then_inc(tab_landed, 16)

            def unit(u, kt, width, *src):
                wait(sp, lo_done, u - 1)
                dst = W_RAW[u.slot][:, 0:kt * width * len(src)]
                if len(src) == 2:
                    dst = dst.rearrange("p (k g m) -> p k g m", k=kt, g=2)
                    for g in range(2):
                        sp.dma_start(dst[:, :, g, :], src[g]).then_inc(landed[u.slot], 16)
                else:
                    dst = dst.rearrange("p (k m) -> p k m", k=kt)
                    for rows in (slice(0, kt // 2), slice(kt // 2, kt)):
                        sp.dma_start(dst[:, rows, :], src[0][:, rows, :]).then_inc(landed[u.slot], 16)

            def ffn(f):
                layer, s = f // 2, f % 2
                w_in = ins["ffn_w_in"][layer, s].rearrange("(k p) (g m) -> p k g m", p=P, g=2)
                w_out = ins["ffn_w_out"][layer, s].rearrange("(k p) m -> p k m", p=P)
                for half in range(2):
                    base = U_FFN[f] + half * (IN_UNITS + OUT_UNITS)

                    def in_unit(j):
                        if j.base >= 2 or base > 0:
                            c = (j + half * FH).times(P).v
                            unit(j + base, KD, P, w_in[:, :, 0, bass.ds(c, P)], w_in[:, :, 1, bass.ds(c, P)])

                    each(sp, IN_UNITS, 2, 1, in_unit)

                    def out_unit(m):
                        unit(m + (base + IN_UNITS), FH, P,
                             w_out[:, half * FH:(half + 1) * FH, bass.ds(m.times(P).v, P)])

                    each(sp, OUT_UNITS, 2, 2, out_unit)

            w, _ = ada_view(0)
            for n in range(2 * KD):
                k, h = n // 2, n % 2
                if n >= 6:
                    sp.wait_ge(ada_used[h], k - 2)
                sp.dma_start(ADA_FIRST[n % 6][:], w[:, k, 1536 * h:1536 * (h + 1)]).then_inc(first_landed[n % 6], 16)
            w_in0 = ins["ffn_w_in"][0, 0].rearrange("(k p) (g m) -> p k g m", p=P, g=2)
            unit(at(0), KD, P, w_in0[:, :, 0, 0:P], w_in0[:, :, 1, 0:P])
            unit(at(1), KD, P, w_in0[:, :, 0, P:2 * P], w_in0[:, :, 1, P:2 * P])
            ffn(0)
            unit(at(U_POOL), KD, 2 * P, ins["pool_w"][0].rearrange("g (k p) m -> p (g k) m", p=P))
            sp.wait_ge(evac_done, U_POOL)
            sp.dma_start(EDGE[:], ins["t_edge"]).then_inc(tab_landed, 16)
            ffn(1)
            ffn(2)
            w_cin = ins["conv_w_in"][0].rearrange("(k p) (g m) -> p k g m", p=P, g=3)
            w_cout = ins["conv_w_out"][0].rearrange("(k p) m -> p k m", p=P)
            each(sp, 8, 0, 0, lambda j: unit(
                j + U_CONV, KD, P, w_cin[:, :, 1, bass.ds(j.times(P).v, P)], w_cin[:, :, 2, bass.ds(j.times(P).v, P)]))
            each(sp, 4, 0, 0, lambda j: unit(
                j + (U_CONV + 8), KD, 2 * P, w_cin[:, :, 0, bass.ds(j.times(2 * P).v, 2 * P)]))
            each(sp, 4, 0, 2, lambda j: unit(
                j + (U_CONV + 12), KD, 2 * P, w_cout[:, :, bass.ds(j.times(2 * P).v, 2 * P)]))
            ffn(3)
            w2 = ins["w_in_2"][0].rearrange("(k p) m -> p k m", p=P)
            unit(at(U_LR), KD, 2 * RANK, w2[:, :, C_LR:C_LR + 2 * RANK])
            sp.wait_ge(evac_done, U_LR)
            sp.dma_start(C_ROWS[:], ins["ctx_2"][0].rearrange("(c p) d -> p c d", p=P)).then_inc(c_landed, 16)
            sp.dma_start(MASKS[:], ins["t_masks"]).then_inc(tab2_landed, 16)
            sp.dma_start(KEEP[:], ins["t_keep"]).then_inc(tab2_landed, 16)
            with sp.Fori(1, GH_ // 2 + 1) as i:
                for s in range(2):
                    hd, u = At(s - 2, i, 2), At(U_G + 3 * s - 6, i, 6)
                    unit(u, KD, P, w2[:, :, bass.ds((hd.times(DK) + C_GK).v, DK)],
                         w2[:, :, bass.ds((hd.times(DK) + C_GQ).v, DK)])
                    unit(u + 1, KD, DV, w2[:, :, bass.ds((hd.times(DV) + C_GV).v, DV)])
                    if s == 0:
                        sp.wait_ge(wgk_zero, 1)
                    head_cols = bass.ds(hd.times(DK).v, DK)
                    sp.wait_ge(pe_done, u.v)
                    sp.dma_start(W_GK[0:RANK, 0, :], ins["w_gk_fwd_2"][0][:, head_cols]).then_inc(wgk_landed, 16)
                    sp.dma_start(W_GK[RANK:2 * RANK, 1, :], ins["w_gk_bwd_2"][0][:, head_cols]).then_inc(wgk_landed, 16)
                    unit(u + 2, KD, DV, w2[:, :, bass.ds((hd.times(DV) + C_GO).v, DV)])
            unit(at(U_K), KD, 2 * P, w2[:, :, C_AK:C_AK + 2 * P])
            unit(at(U_V), KD, 2 * P, w2[:, :, C_AV:C_AV + 2 * P])
            sp.wait_ge(o_done, 2 * GH_)
            sp.dma_start(COS[:], ins["t_cos"]).then_inc(tab3_landed, 16)
            sp.dma_start(SIN[:], ins["t_sin"]).then_inc(tab3_landed, 16)
            sp.dma_start(PERM[:], ins["t_perm"]).then_inc(tab3_landed, 16)
            each(sp, NQ // 2, 0, 0, lambda j: unit(j + U_Q, KD, 2 * P, w2[:, :, bass.ds((j.times(2 * P) + C_AQ).v, 2 * P)]))
            w_bra = ins["w_br_attn_2"][0].rearrange("(k p) m -> p k m", p=P)
            w_brg = ins["w_br_gla_2"][0].rearrange("(k p) m -> p k m", p=P)
            with sp.Fori(1, KD + 1) as i:
                col = lambda c0: bass.ds(At(c0 - P, i, P).v, P)
                unit(At(U_D - 2, i, 2), KD, P, w2[:, :, col(C_GA)], w2[:, :, col(C_GG)])
                unit(At(U_D - 1, i, 2), KD, P, w_bra[:, :, col(0)], w_brg[:, :, col(0)])
            w_o = ins["w_out_2"][0].rearrange("(k p) m -> p k m", p=P)
            each(sp, 4, 0, 2, lambda j: unit(j + U_WO, KD, 2 * P, w_o[:, :, bass.ds(j.times(2 * P).v, 2 * P)]))
            w_m1 = ins["w_mlp1_2"][0].rearrange("(k p) m -> p k m", p=P)
            w_m2 = ins["w_mlp2_2"][0].rearrange("(k p) m -> p k m", p=P)

            def quarter(q):
                for j in range(4):
                    unit(q.times(8) + (U_MLP + j), KD, 2 * P, w_m1[:, :, bass.ds((q.times(D) + 2 * P * j).v, 2 * P)])
                for j in range(4):
                    unit(q.times(8) + (U_MLP + 4 + j), KD, 2 * P,
                         w_m2[:, bass.ds(q.times(KD).v, KD), 2 * P * j:2 * P * (j + 1)])

            with sp.Fori(0, 3) as i:
                quarter(At(0, i, 1))
            quarter(at(3))
            for c in range(4):
                sp.wait_ge(out_made, c + 1)
                sp.dma_start(out[c * P:(c + 1) * P, :], X_ROWS[:, c, :]).then_inc(out_sem, 16)
            sp.wait_ge(out_sem, 64)

        @block.gpsimd
        def _(pool):
            nc.gpsimd.memset(ONES[:], 1.0).then_inc(const_ready, 1)
            nc.gpsimd.memset(ONES_D[:, 0:1], 1.0 / D)
            nc.gpsimd.memset(ONES_D[:, 1:2], 1.0 / DV)
            nc.gpsimd.memset(ONES_HD[:], 1.0 / HD).then_inc(const_ready, 1)
            nc.gpsimd.memset(EPS_C[:], EPS).then_inc(const_ready, 1)
            nc.gpsimd.memset(ACC[:], 0.0).then_inc(acc_cleared, 1)

            def ada(g, k):
                w, col = ada_view(g)
                for h in range(2):
                    wait(pool, ada_used[h], k + 8 * g)
                    pool.dma_start(ADA[h][:], w[:, bass.ds(k.v, 1), col + 1536 * h:col + 1536 * (h + 1)]
                                   .rearrange("p a m -> p (a m)")).then_inc(ada_landed[h], 16)

            for g in range(1, 8):
                pool.wait_ge(mod_summed, g)
                if g == 6:
                    nc.gpsimd.memset(ACC_C[:], 0.0).then_inc(acc_cleared, 1)
                nc.gpsimd.memset(ACC[:], 0.0).then_inc(acc_cleared, 1)
                ada(g, at(0))
                with pool.Fori(0, 7) as i:
                    ada(g, At(1, i, 1))

            pool.wait_ge(evac_done, U_LR)
            nc.gpsimd.memset(W_GK[0:2 * RANK], 0.0).then_inc(wgk_zero, 1)

        @block.scalar
        def _(act):
            def split_hi(u):
                act.wait_ge(landed[u.slot], (u.half().times(32) + 32).v)
                wait(act, pe_done, u - 1)
                n = unit_size(u.base)
                nc.scalar.copy(W_HI[u.slot][:, 0:n], W_RAW[u.slot][:, 0:n]).then_inc(hi_done, 1)

            def squares(r, ready, tiles=range(KD)):
                for k in tiles:
                    ready(k)
                    wait(act, sq_summed, at(KD * r + k - 1))
                    nc.scalar.activation((SA if r == 7 else GT)[k % 2][:], X[:, k, :], ACT.Square).then_inc(sq_made, 1)

            def root(r):
                act.wait_ge(ms_made, r + 1)
                nc.scalar.activation(RSTD4[:, 4:8], BANK[6][:, 0:4], ACT.Sqrt, bias=EPS_C[:]).then_inc(rt_made, 1)

            def h_hi(r, g):
                for k in range(KD):
                    act.wait_ge(xr_made, KD * r + k + 1)
                    if k >= 2:
                        act.wait_ge(h_ready, H_BASE[r] + k - 1)
                    nc.scalar.activation(SA[k % 2][:], GT[k % 2][:], ACT.Identity,
                                         bias=MODS[:, 24 * g + k:24 * g + k + 1]).then_inc(h_made, 1)
                    act.wait_ge(h_made, KD * (r - (r > 6)) + k + 1)
                    nc.scalar.copy(H_HI[:, k, 0:T], SA[k % 2][:]).then_inc(h_hi_made, 1)

            def after_ffn(f):
                return lambda k: act.wait_ge(evac_done, U_FFN[f] + FFN_UNITS - OUT_UNITS + k + 1)

            def ffn(f):
                for half in range(2):
                    base = U_FFN[f] + half * (IN_UNITS + OUT_UNITS)

                    def in_unit(j):
                        u = j + base
                        if half or j.i is not None or j.base:
                            split_hi(u + 1)
                        act.wait_ge(pe_done, (u + 1).v)
                        wait(act, evac_done, u - 1)
                        nc.scalar.activation(SA[u.slot][:], BANK[2 * u.slot][:], ACT.Silu).then_inc(silu_made, 1)

                    def out_unit(m):
                        split_hi(m + (base + IN_UNITS + 1))
                        if half and m.i is None and m.base >= OUT_UNITS - 2:
                            squares(FFN_NEXT[f], after_ffn(f), EARLY[m.base])

                    each(act, IN_UNITS, 2, 1, in_unit)
                    each(act, OUT_UNITS, 2, 2, out_unit)
                squares(FFN_NEXT[f], after_ffn(f), (KD - 1,))

            act.wait_ge(vec_ready, 1)
            nc.scalar.activation(COND[:], VECS[:, 0:24], ACT.Silu).then_inc(cond_ready, 1)
            for k in range(KD):
                act.wait_ge(x_turned, k + 1)
                nc.scalar.copy(X[:, k, :], BANK[k % 4][:]).then_inc(x_made, 1)
            act.wait_ge(const_ready, 3)
            squares(0, lambda k: act.wait_ge(x_made, k + 1))
            split_hi(at(0))
            split_hi(at(1))
            root(0)
            h_hi(0, 0)
            ffn(0)
            split_hi(at(U_POOL + 1))
            root(1)
            for k in range(KD):
                act.wait_ge(pool_mixed, k + 1)
                nc.scalar.copy(H_HI[:, k, 0:T], PH[:, k, :]).then_inc(p_hi_made, 1)
            squares(2, lambda k: act.wait_ge(pool_added, k // 2 + 1) if k < 6 else
                    act.wait_ge(evac_done, U_POOL + 1))
            split_hi(at(U_FFN[1] + 1))
            root(2)
            h_hi(2, 2)
            ffn(1)
            split_hi(at(U_FFN[2] + 1))
            root(3)
            h_hi(3, 3)
            ffn(2)
            split_hi(at(U_CONV + 1))
            root(4)
            h_hi(4, 4)

            def cv_unit(j):
                u = j + U_CONV
                if j.i is not None or j.base:
                    split_hi(u + 1)
                act.wait_ge(pe_done, (u + 1).v)
                wait(act, evac_done, u - 1)
                nc.scalar.copy(C_T[u.slot][:], BANK[2 * u.slot][:]).then_inc(cv_c, 1)

            each(act, 8, 2, 0, cv_unit)
            each(act, 4, 0, 0, lambda j: split_hi(j + (U_CONV + 9)))
            each(act, 4, 0, 2, lambda j: split_hi(j + (U_CONV + 13)))
            squares(5, lambda k: act.wait_ge(evac_done, U_CONV + 12 + k // 2 + 1))
            split_hi(at(U_FFN[3] + 1))
            root(5)
            h_hi(5, 5)
            ffn(3)
            root(6)
            squares(7, lambda k: act.wait_ge(xr_made, KD * 6 + k + 1))
            root(7)
            h_hi(7, 6)
            for k in range(KD):
                act.wait_ge(c_turned, 2 * (k // 2) + 2)
                nc.scalar.copy(C_X[:, k, :], BANK[k // 2][:, TC * (k % 2):TC * (k % 2 + 1)]).then_inc(c_made, 1)
            for k in range(KD):
                act.wait_ge(c_made, k + 1)
                wait(act, csq_summed, at(k - 1))
                nc.scalar.activation(SG[k % 2][:, 0:TC], C_X[:, k, :], ACT.Square).then_inc(csq_made, 1)
            act.wait_ge(cms_made, 1)
            nc.scalar.activation(STAT[:, 0:2], BANK[7][:, 0:2], ACT.Sqrt, bias=EPS_C[:]).then_inc(crt_made, 1)
            for k in range(KD):
                act.wait_ge(ch_made, k + 1)
                nc.scalar.copy(H_HI[:, k, T:TA], SG[k % 2][:, 0:TC]).then_inc(h_hi_made, 1)
            split_hi(at(U_LR + 1))

            def gla_levels(hd):
                for n in range(len(LEVELS)):
                    e = EL[n % 2]
                    act.wait_ge(lv_d, (hd.times(len(LEVELS)) + (n + 1)).v)
                    nc.scalar.activation(e[:, 0, :], e[:, 0, :], ACT.Exp, scale=-1.0 / 16)
                    nc.scalar.activation(e[:, 1, :], e[:, 1, :], ACT.Exp, scale=1.0 / 16).then_inc(lv_e, 1)

            with act.Fori(0, GH_ // 2) as i:
                for s in range(2):
                    hd, u = At(s, i, 2), At(U_G + 3 * s, i, 6)
                    split_hi(u + 1)
                    for d in range(2):
                        zd = hd.times(2) + (d + 1)
                        bias = VECS[:, bass.ds((hd + VEC_ROWS[("b_gk_fwd_2", "b_gk_bwd_2")[d]][0]).v, 1)]
                        act.wait_ge(z_made, zd.v)
                        nc.scalar.activation(T1[:], WIDE[6], ACT.Identity, bias=bias).then_inc(z_out, 1)
                        act.wait_ge(z_min, zd.v)
                        nc.scalar.activation(T2[:], T2[:], ACT.Exp).then_inc(z_exp, 1)
                        act.wait_ge(z_exp, zd.v)
                        nc.scalar.activation(T2[:], T2[:], ACT.Ln, bias=1.0).then_inc(z_ln, 1)
                        act.wait_ge(b_made, zd.v)
                        nc.scalar.activation(T1[:, 0:T], B[d][:, 0:T], ACT.Exp, scale=1.0 / 16).then_inc(eb_made, 1)
                        act.wait_ge(kd_arg, zd.v)
                        nc.scalar.activation(T2[:], T2[:], ACT.Exp, scale=1.0 / 16).then_inc(kd_e, 1)
                        if d == 0:
                            split_hi(u + 2)
                        act.wait_ge(kdt_t, zd.v)
                        nc.scalar.copy(KDT[:].rearrange("p c t -> p (c t)"), WIDE[6]).then_inc(kdt_made, 1)
                        if d == 0:
                            split_hi(u + 3)
                    gla_levels(hd)
                    pa, pb = 2 * (s % 2), 2 * ((s + 1) % 2)
                    act.wait_ge(pe_done, (u + 3).v)
                    act.wait_ge(st_made, (hd.times(8) + 8).v)
                    nc.scalar.activation(SG[0][:], BANK[pa], ACT.Silu)
                    nc.scalar.activation(SG[1][:], BANK[pa + 1], ACT.Silu).then_inc(evac_done, 1)
                    act.wait_ge(o_mm, (hd + 1).v)
                    for e in range(2):
                        nc.scalar.copy(O_N[e], BANK[pb + e][:]).then_inc(o_cp, 1)
                    for e in range(2):
                        nc.scalar.activation(O_SQ[e], BANK[pb + e][:], ACT.Square).then_inc(o_sq, 1)
                    act.wait_ge(o_ms, (hd + 1).v)
                    nc.scalar.activation(STAT[:, 0:4], BANK[6][:, 0:4], ACT.Sqrt, bias=EPS_C[:]).then_inc(o_rt, 1)
            split_hi(at(U_K + 1))
            act.wait_ge(k_raw, 1)
            for h in range(NKV):
                nc.scalar.activation(K_SQ[:, h, :], K_RAW[:, h, :], ACT.Square).then_inc(k_sq, 1)
            act.wait_ge(k_ms, 1)
            nc.scalar.activation(STAT[:, 0:12], BANK[6][:, 0:12], ACT.Sqrt, bias=EPS_C[:]).then_inc(k_rt, 1)
            split_hi(at(U_V + 1))
            with act.Fori(0, NKV) as kv:
                for ui in range(2):
                    qi, u = At(ui, kv, 2), At(U_Q + ui, kv, 2)
                    pb = 2 * u.slot
                    act.wait_ge(pe_done, (u + 1).v)
                    if ui == 0:
                        act.wait_ge(vs_made, At(1, kv, 1).v)
                    for m in range(2):
                        if ui == 1:
                            act.wait_ge(at_made, At(2, kv, 4).v)
                        nc.scalar.activation(Q_SQ[m][:], BANK[pb + m][:], ACT.Square).then_inc(q_sq, 1)
                    split_hi(u + 1)
                    act.wait_ge(q_rot, (qi + 1).v)
                    nc.scalar.activation(STAT[:, 0:8], BANK[6][:, 0:8], ACT.Sqrt, bias=EPS_C[:]).then_inc(q_rt, 1)
                    for m in range(2):
                        a = At(2 * ui + m, kv, 4)

                        def exp_p(c):
                            act.wait_ge(nb_made, (a.times(4) + (c + 1)).v)
                            nc.scalar.activation(PP[c % 2][:], WIDE[4 + 2 * (c % 2)], ACT.Exp, bias=STAT[:, 34 + c % 2:35 + c % 2],
                                                 scale=STAT[:, 16 + 4 * m + c:17 + 4 * m + c],
                                                 accum_out=STAT[:, 36 + c % 2:37 + c % 2]).then_inc(p_exp, 1)

                        def copy_pt(c):
                            act.wait_ge(p_t, (a.times(4) + (c + 1)).v)
                            nc.scalar.copy(PT[:, :, c * P:(c + 1) * P],
                                           WIDE[2 * (c % 2)].rearrange("p (k q) -> p k q", k=6)).then_inc(pt_made, 1)

                        exp_p(0)
                        for c in range(1, 4):
                            exp_p(c)
                            copy_pt(c - 1)
                        copy_pt(3)
            act.wait_ge(at_made, NQ)
            for k in range(KD):
                nc.scalar.copy(A_HI[:, k, :], AT_T[:, k, :]).then_inc(a_hi_made, 1)
            for k in range(KD):
                nc.scalar.copy(L_HI[:, k, :], O_T[:, k, :]).then_inc(a_hi_made, 1)
            with act.Fori(0, KD) as i:
                u = At(U_D, i, 2)
                split_hi(u + 1)
                act.wait_ge(pe_done, (u + 1).v)
                act.wait_ge(evac_done, u.v)
                nc.scalar.activation(SGB[0][:], BANK[0][:], ACT.Sigmoid).then_inc(sig_made, 1)
                nc.scalar.activation(SGB[1][:], BANK[1][:], ACT.Sigmoid).then_inc(evac_done, 1)
                split_hi(u + 2)
            act.wait_ge(evac_done, U_WO)
            for k in range(KD):
                nc.scalar.copy(H_HI[:, k, 0:T], Y[:, k, :]).then_inc(y_hi_made, 1)
            each(act, 4, 0, 2, lambda j: split_hi(j + (U_WO + 1)))
            squares(8, lambda k: act.wait_ge(evac_done, U_WO + k // 2 + 1))
            root(8)
            h_hi(8, 7)

            def quarter(q, last=False):
                for j in range(4):
                    u = q.times(8) + (U_MLP + j)
                    split_hi(u + 1)
                    act.wait_ge(pe_done, (u + 1).v)
                    act.wait_ge(evac_done, u.v)
                    for m in range(2):
                        nc.scalar.activation(SA[m][:], BANK[2 * u.slot + m][:], ACT.Relu).then_inc(relu_made, 1)
                for j in range(4):
                    if not (last and j == 3):
                        split_hi(q.times(8) + (U_MLP + 5 + j))

            with act.Fori(0, 3) as i:
                quarter(At(0, i, 1))
            quarter(at(3), True)
            for c in range(4):
                act.wait_ge(row_t, c + 1)
                nc.scalar.copy(X_ROWS[:, c, :], PS[:, 2 * T * (c % 2):2 * T * (c % 2 + 1)]).then_inc(out_made, 1)

        @block.vector
        def _(dve):
            def split_lo(u):
                dve.wait_ge(hi_done, (u + 1).v)
                n = unit_size(u.base)
                nc.vector.tensor_tensor(W_LO[u.slot][:, 0:n], W_RAW[u.slot][:, 0:n],
                                        W_HI[u.slot][:, 0:n].bitcast(F32), ALU.subtract).then_inc(lo_done, 1)

            def ada(g, k):
                for h in range(2):
                    dve.wait_ge(ada_landed[h], ((k + (8 * g - 7)).times(16)).v)
                    if h == 0 and k.base == 0:
                        dve.wait_ge(acc_cleared, g + 1 + (g >= 6))
                    wait(dve, ada_used[h], k + 8 * g)
                    acc = ACC[:, 1536 * h:1536 * (h + 1)]
                    cond = 0 if g < 6 else 8
                    if g == 6:
                        n = 1536 if h == 0 else 512
                        acc_c = ACC_C[:, 1536 * h:1536 * h + n]
                        nc.vector.scalar_tensor_tensor(acc_c, ADA[h][:, 0:n], COND[:, bass.ds((k + 16).v, 1)],
                                                       acc_c, ALU.mult, ALU.add)
                    nc.vector.scalar_tensor_tensor(acc, ADA[h][:], COND[:, bass.ds((k + cond).v, 1)],
                                                   acc, ALU.mult, ALU.add).then_inc(ada_used[h], 1)

            def modulation(g):
                bias = vecs("ada_b", 24 * g, 24 * g + 24) if g < 6 else vecs("b_ada_2", 24 * (g - 6), 24 * (g - 6) + 24)
                gain = vecs("norm_g", 8 * g, 8 * g + 8) if g < 6 else vecs(("norm1_2", "norm2_2")[g - 6], 0, 8)
                dve.wait_ge(mod_summed, g + 1)
                m = MODS[:, 24 * g:24 * g + 24]
                nc.vector.tensor_tensor(m, BANK[7][:, 0:24], bias, ALU.add).then_inc(mod_read, 1)
                if g == 6:
                    nc.vector.tensor_tensor(MODS[:, 192:208], BANK[7][:, 24:40], bias[:, 0:16], ALU.add).then_inc(mod_read, 1)
                dve.wait_ge(mod_read, MOD_READ[g])
                nc.vector.scalar_tensor_tensor(GAIN[:, 8 * g:8 * g + 8], m[:, 8:16], 1.0, gain, ALU.add, ALU.mult).then_inc(mod_done, 1)
                gate = GATE[:, 8 * g:8 * g + 8]
                if g in FFN_NORM:
                    nc.vector.tensor_scalar(gate, m[:, 16:24], 0.5, None, ALU.mult).then_inc(mod_done, 1)
                elif g == 1:
                    nc.vector.tensor_tensor(gate, m[:, 16:24], vecs("pool_scale", 0, 8), ALU.mult).then_inc(mod_done, 1)
                else:
                    nc.vector.tensor_copy(gate, m[:, 16:24]).then_inc(mod_done, 1)
                if g == 6:
                    nc.vector.scalar_tensor_tensor(GAIN[:, 64:72], MODS[:, 200:208], 1.0, gain, ALU.add, ALU.mult).then_inc(mod_done, 1)

            def square_sums(r, tiles=range(KD)):
                sq = SA if r == 7 else GT
                for k in tiles:
                    dve.wait_ge(sq_made, KD * r + k + 1)
                    if k == 0:
                        nc.vector.tensor_copy(SSQ[:], sq[0][:]).then_inc(sq_summed, 1)
                    else:
                        dve.wait_ge(sq_summed, KD * r + k)
                        nc.vector.tensor_tensor(SSQ[:], SSQ[:], sq[k % 2][:], ALU.add).then_inc(sq_summed, 1)

            def rstd_diag(r):
                dve.wait_ge(rt_made, r + 1)
                nc.vector.reciprocal(RSTD4[:, 0:4], RSTD4[:, 4:8]).then_inc(rs_made, 1)
                dve.wait_ge(rs_made, r + 1)
                for c in range(4):
                    nc.vector.tensor_scalar(DIAG[:, c, :], IDENT[:], RSTD4[:, c:c + 1], None, ALU.mult).then_inc(diag_made, 1)

            def normed(r, k, dst, gain):
                if k == 0:
                    dve.wait_ge(rb_made, r + 1)
                nc.vector.scalar_tensor_tensor(dst, X[:, k, :], gain, BANK[5][:], ALU.mult, ALU.mult).then_inc(xr_made, 1)

            def norm_split(r, g, ahead=None, tiles=range(KD)):
                def lo(k):
                    dve.wait_ge(h_hi_made, H_BASE[r] + k + 1)
                    nc.vector.tensor_tensor(H_LO[:, k, 0:T], SA[k % 2][:], H_HI[:, k, 0:T].bitcast(F32),
                                            ALU.subtract).then_inc(h_ready, 1)
                square_sums(r, tiles)
                if ahead is not None:
                    split_lo(at(ahead))
                rstd_diag(r)
                dve.wait_ge(mod_done, MOD_DONE[g])
                for k in range(KD):
                    normed(r, k, GT[k % 2][:], GAIN[:, 8 * g + k:8 * g + k + 1])
                    if k >= 1:
                        lo(k - 1)
                lo(KD - 1)

            def add_branch(m, bank, gate):
                mm = bass.ds(m.v, 1)
                x = X[:, mm, :].rearrange("p a t -> p (a t)")
                return nc.vector.scalar_tensor_tensor(x, bank[:], GATE[:, bass.ds((m + 8 * gate).v, 1)], x, ALU.mult, ALU.add)

            def ffn(f):
                for half in range(2):
                    g = FFN_GROUPS[f][half]
                    base = U_FFN[f] + half * (IN_UNITS + OUT_UNITS)
                    q0 = (2 * f + half) * FH

                    def in_unit(j):
                        u, q = j + base, j + q0
                        if half or j.i is not None or j.base:
                            split_lo(u + 1)
                        if g is not None and j.i is not None:
                            ada(g, j - 2)
                        dve.wait_ge(silu_made, (q + 1).v)
                        nc.vector.tensor_tensor(GT[u.slot][:], SA[u.slot][:], BANK[2 * u.slot + 1][:], ALU.mult).then_inc(evac_done, 1)
                        dve.wait_ge(evac_done, (u + 1).v)
                        tile = lambda b: b[:, bass.ds(j.v, 1), :].rearrange("p a t -> p (a t)")
                        nc.vector.tensor_copy(tile(G_HI), GT[u.slot][:]).then_inc(g_hi_made, 1)
                        dve.wait_ge(g_hi_made, (q + 1).v)
                        nc.vector.tensor_tensor(tile(G_LO), GT[u.slot][:], tile(G_HI).bitcast(F32), ALU.subtract).then_inc(g_ready, 1)

                    each(dve, IN_UNITS, 2, 1, in_unit)

                    def out_unit(m):
                        u = m + (base + IN_UNITS)
                        split_lo(u + 1)
                        if half and m.i is None and m.base >= OUT_UNITS - 2:
                            square_sums(FFN_NEXT[f], EARLY[m.base])
                        dve.wait_ge(pe_done, (u + 1).v)
                        add_branch(m, BANK[2 * u.slot], FFN_NORM[f]).then_inc(evac_done, 1)
                        if g is not None and m.i is None and m.base == 1:
                            modulation(g)

                    each(dve, OUT_UNITS, 2, 2, out_unit)

            dve.wait_ge(vec_turned, 1)
            nc.vector.tensor_copy(VECS[:, 0:NVEC], BANK[6][:, 0:NVEC]).then_inc(vec_ready, 1)
            square_sums(0)
            dve.wait_ge(cond_ready, 1)
            dve.wait_ge(acc_cleared, 1)
            for n in range(2 * KD):
                k, h = n // 2, n % 2
                dve.wait_ge(first_landed[n % 6], 16 * (n // 6 + 1))
                wait(dve, ada_used[h], at(k))
                acc = ACC[:, 1536 * h:1536 * (h + 1)]
                nc.vector.scalar_tensor_tensor(acc, ADA_FIRST[n % 6][:], COND[:, k:k + 1], acc, ALU.mult, ALU.add).then_inc(ada_used[h], 1)
            split_lo(at(0))
            split_lo(at(1))
            modulation(0)

            norm_split(0, 0, None, ())
            ffn(0)
            square_sums(1, (KD - 1,))
            split_lo(at(U_POOL + 1))
            rstd_diag(1)
            dve.wait_ge(mod_done, MOD_DONE[1])
            for k in range(KD):
                normed(1, k, PH[:, k, :], GAIN[:, 8 + k:9 + k])
                dve.wait_ge(xr_made, KD + k + 1)
                nc.vector.tensor_scalar(PH[:, k, :], PH[:, k, :], MODS[:, 24 + k:25 + k], None, ALU.add).then_inc(h_made, 1)
            dve.wait_ge(tab_landed, 32)
            steps = 0
            for gi, w in enumerate(POOL_WINDOWS):
                h = PH[:, 2 * gi:2 * gi + 2, :]
                dve.wait_ge(h_made, KD + 2 * gi + 2)
                src, dst, s = h, PS_A, 1
                while s < w:
                    nc.vector.tensor_tensor(dst[:, :, s:T], src[:, :, s:T], src[:, :, 0:T - s], ALU.add)
                    nc.vector.tensor_copy(dst[:, :, 0:s], src[:, :, 0:s]).then_inc(pool_step, 1)
                    steps += 1
                    dve.wait_ge(pool_step, steps)
                    src, dst = dst, (PS_B if dst is PS_A else PS_A)
                    s *= 2
                for a in range(2):
                    nc.vector.tensor_tensor(src[:, a, 0:w], src[:, a, 0:w], EDGE[:, gi, 0:w], ALU.mult).then_inc(pool_step, 1)
                steps += 2
                dve.wait_ge(pool_step, steps)
                for a in range(2):
                    nc.vector.scalar_tensor_tensor(PH[:, 2 * gi + a, :], src[:, a, :], 1.0 / w, PH[:, 2 * gi + a, :],
                                                   ALU.mult, ALU.subtract).then_inc(pool_mixed, 1)
                for k in (2 * gi, 2 * gi + 1):
                    dve.wait_ge(p_hi_made, k + 1)
                    nc.vector.tensor_tensor(H_LO[:, k, 0:T], PH[:, k, :], H_HI[:, k, 0:T].bitcast(F32),
                                            ALU.subtract).then_inc(p_ready, 1)
            for gi in range(4):
                if gi < 3:
                    dve.wait_ge(pool_mm, gi + 1)
                else:
                    dve.wait_ge(pe_done, U_POOL + 1)
                for a in range(2):
                    last = add_branch(at(2 * gi + a), BANK[2 * (gi % 2) + a], 1)
                last.then_inc(pool_added if gi < 3 else evac_done, 1)
            norm_split(2, 2, U_FFN[1] + 1)
            ffn(1)
            norm_split(3, 3, U_FFN[2] + 1, (KD - 1,))
            ffn(2)
            norm_split(4, 4, U_CONV + 1, (KD - 1,))
            for s in range(2):
                nc.vector.memset(U_T[s][:, 0:2], 0.0).then_inc(cv_zero, 1)

            def cv_unit(j):
                u = j + U_CONV
                uu = U_T[u.slot]
                if j.i is not None or j.base:
                    split_lo(u + 1)
                dve.wait_ge(cv_c, (j + 1).v)
                dve.wait_ge(cv_zero, 2)
                nc.vector.tensor_tensor(uu[:, 2:T + 2], C_T[u.slot][:], BANK[2 * u.slot + 1][:], ALU.mult).then_inc(evac_done, 1)
                dve.wait_ge(evac_done, (u + 1).v)
                cv = CV[:, bass.ds(j.v, 1), :].rearrange("p a t -> p (a t)")
                tap = lambda n: VECS[:, bass.ds((j + (VEC_ROWS["conv_w"][0] + 8 * n)).v, 1)]
                nc.vector.tensor_scalar(cv, uu[:, 0:T], tap(0), None, ALU.mult).then_inc(cv_1, 1)
                dve.wait_ge(cv_1, (j + 1).v)
                nc.vector.scalar_tensor_tensor(cv, uu[:, 1:T + 1], tap(1), cv, ALU.mult, ALU.add).then_inc(cv_2, 1)
                dve.wait_ge(cv_2, (j + 1).v)
                nc.vector.scalar_tensor_tensor(cv, uu[:, 2:T + 2], tap(2), cv, ALU.mult, ALU.add).then_inc(cv_3, 1)

            each(dve, 8, 2, 0, cv_unit)
            dve.wait_ge(cv_3, 8)

            def b_unit(j):
                u = j + (U_CONV + 8)
                split_lo(u + 1)
                dve.wait_ge(pe_done, (u + 1).v)
                for a in range(2):
                    m = j.times(2) + a
                    tile = lambda b: b[:, bass.ds(m.v, 1), :].rearrange("p a t -> p (a t)")
                    mul = nc.vector.tensor_tensor(GT[a][:], BANK[2 * u.slot + a][:], tile(CV), ALU.mult)
                    mul.then_inc(cz_made, 1)
                    dve.wait_ge(cz_made, (m + 1).v)
                    if a == 1:
                        nc.vector.tensor_copy(tile(Z_HI), GT[a][:]).then_inc(evac_done, 1)
                        dve.wait_ge(evac_done, (u + 1).v)
                    else:
                        nc.vector.tensor_copy(tile(Z_HI), GT[a][:]).then_inc(z_hi_made, 1)
                        dve.wait_ge(z_hi_made, (j + 1).v)
                    nc.vector.tensor_tensor(tile(Z_LO), GT[a][:], tile(Z_HI).bitcast(F32), ALU.subtract).then_inc(z_ready, 1)

            each(dve, 4, 0, 0, b_unit)

            def out_pair(j):
                u = j + (U_CONV + 12)
                split_lo(u + 1)
                if j.i is None and j.base == 3:
                    square_sums(5, range(6))
                dve.wait_ge(pe_done, (u + 1).v)
                for a in range(2):
                    last = add_branch(j.times(2) + a, BANK[2 * u.slot + a], 4)
                last.then_inc(evac_done, 1)

            each(dve, 4, 0, 2, out_pair)
            norm_split(5, 5, U_FFN[3] + 1, (6, 7))
            ffn(3)
            square_sums(6, (KD - 1,))
            rstd_diag(6)
            for k in range(KD):
                normed(6, k, X[:, k, :], vec("final_g", k))
            norm_split(7, 6)
            for k in range(KD):
                dve.wait_ge(csq_made, k + 1)
                if k == 0:
                    nc.vector.tensor_copy(SSQ[:, 0:TC], SG[0][:, 0:TC]).then_inc(csq_summed, 1)
                else:
                    dve.wait_ge(csq_summed, k)
                    nc.vector.tensor_tensor(SSQ[:, 0:TC], SSQ[:, 0:TC], SG[k % 2][:, 0:TC], ALU.add).then_inc(csq_summed, 1)
            dve.wait_ge(crt_made, 1)
            nc.vector.reciprocal(STAT[:, 2:4], STAT[:, 0:2]).then_inc(crs_made, 1)
            dve.wait_ge(crs_made, 1)
            for c in range(2):
                nc.vector.tensor_scalar(DIAG[:, c, :], IDENT[:], STAT[:, 2 + c:3 + c], None, ALU.mult).then_inc(cdiag_made, 1)
            dve.wait_ge(crb_made, 1)

            def ctx_lo(k):
                dve.wait_ge(h_hi_made, H_BASE[7] + KD + k + 1)
                nc.vector.tensor_tensor(H_LO[:, k, T:TA], SG[k % 2][:, 0:TC], H_HI[:, k, T:TA].bitcast(F32),
                                        ALU.subtract).then_inc(h_ready, 1)

            for k in range(KD):
                nc.vector.tensor_tensor(GT[k % 2][:, 0:TC], C_X[:, k, :], BANK[6][:, 0:TC], ALU.mult).then_inc(cxr_made, 1)
                dve.wait_ge(cxr_made, k + 1)
                nc.vector.tensor_scalar(SG[k % 2][:, 0:TC], GT[k % 2][:, 0:TC], GAIN[:, 64 + k:65 + k],
                                        MODS[:, 192 + k:193 + k], ALU.mult, ALU.add).then_inc(ch_made, 1)
                if k >= 1:
                    ctx_lo(k - 1)
            ctx_lo(KD - 1)
            split_lo(at(U_LR + 1))
            dve.wait_ge(pe_done, U_LR + 1)
            lb = U_LR % 2
            nc.vector.tensor_copy(LRT[0:2 * RANK, 0:T], BANK[2 * lb][0:2 * RANK, :])
            nc.vector.tensor_copy(LRT[0:2 * RANK, T:TA], BANK[4 + lb][0:2 * RANK, 0:TC]).then_inc(evac_done, 1)

            t2x = T2[:, 0:T].rearrange("p (c t) -> p c t", c=NC_)
            am = AM[:].rearrange("p (c t) -> p c t", c=NC_)

            def decays(hd, d):
                zd = hd.times(2) + (d + 1)
                b = B[d]
                bx = b[:, 0:T].rearrange("p (c t) -> p c t", c=NC_)
                dve.wait_ge(z_out, zd.v)
                nc.vector.scalar_tensor_tensor(T2[:], T1[:], -1.0, T1[:], ALU.mult, ALU.min).then_inc(z_min, 1)
                dve.wait_ge(z_ln, zd.v)
                nc.vector.scalar_tensor_tensor(T1[:], T1[:], 0.0, T2[:], ALU.min, ALU.subtract).then_inc(g_made, 1)
                dve.wait_ge(g_made, zd.v)
                if d == 0:
                    nc.vector.tensor_tensor_scan(b[:, 0:T], KEEP[:], T1[:, 0:T], 0.0, ALU.mult, ALU.add)
                    nc.vector.tensor_tensor_scan(b[:, T:TA], KEEP[:, 0:TC], T1[:, T:TA], 0.0, ALU.min, ALU.add).then_inc(b_made, 1)
                else:
                    nc.vector.tensor_tensor_scan(b[:, T - 1::-1], KEEP[:], T1[:, T - 1::-1], 0.0, ALU.mult, ALU.add)
                    nc.vector.tensor_tensor_scan(b[:, TA - 1:T - 1:-1], KEEP[:, 0:TC], T1[:, TA - 1:T - 1:-1], 0.0, ALU.min, ALU.add).then_inc(b_made, 1)
                dve.wait_ge(b_made, zd.v)
                end = CH - 1 if d == 0 else 0
                nc.vector.tensor_tensor(t2x, bx[:, :, end:end + 1].broadcast_to([P, NC_, CH]), bx, ALU.subtract)
                end = TA - 1 if d == 0 else T
                nc.vector.tensor_tensor(T2[:, T:TA], b[:, end:end + 1].broadcast_to([P, TC]), b[:, T:TA], ALU.subtract).then_inc(kd_arg, 1)
                dve.wait_ge(eb_made, zd.v)
                nc.vector.tensor_tensor(QB[d][:], QT, T1[:, 0:T], ALU.mult).then_inc(qb_made, 1)
                dve.wait_ge(kd_e, zd.v)
                nc.vector.tensor_tensor(T2[:], KT, T2[:], ALU.mult).then_inc(kd_made, 1)

            def states(hd, d, pb):
                dve.wait_ge(sp_made, (hd.times(2) + (d + 1)).v)
                order = [0, 1, 2, 3] if d == 0 else [3, 2, 1, 0]
                s0 = hd.times(8) + 4 * d
                for n, c in enumerate(order):
                    if n == 0:
                        nc.vector.tensor_copy(ST[d][:, c, :], PS[:, pb * T + 3 * DV:pb * T + 4 * DV]).then_inc(st_made, 1)
                    else:
                        dve.wait_ge(st_made, (s0 + n).v)
                        before = order[n - 1]
                        col = before * CH + (CH - 1 if d == 0 else 0)
                        nc.vector.scalar_tensor_tensor(ST[d][:, c, :], ST[d][:, before, :], T1[:, col:col + 1],
                                                       PS[:, pb * T + (n - 1) * DV:pb * T + n * DV], ALU.mult, ALU.add).then_inc(st_made, 1)

            def levels(hd):
                lv0 = hd.times(len(LEVELS))

                def level_d(n):
                    sz = LEVELS[n]
                    nb = T // (2 * sz)
                    mid = BB[:, 0:2 * TA + 2].rearrange("p (d x) -> p d x", d=2)[:, :, 0:T] \
                        .rearrange("p d (n r) -> p d n r", r=2 * sz)[:, :, :, sz - 1:sz].broadcast_to([P, 2, nb, sz])
                    b = BB[:, 0:2 * TA].rearrange("p (d x) -> p d x", d=2)[:, :, 0:T].rearrange("p d (n r) -> p d n r", r=2 * sz)
                    e = EL[n % 2]
                    e_kq = e[:].rearrange("p d (n r) -> p d n r", r=2 * sz)
                    e_qk = e[:, ::-1, :].rearrange("p d (n r) -> p d n r", r=2 * sz)
                    if n >= 2:
                        dve.wait_ge(lv_k, (lv0 + (n - 1)).v)
                    nc.vector.tensor_tensor(e_kq[:, :, :, 0:sz], b[:, :, :, 0:sz], mid, ALU.subtract)
                    nc.vector.tensor_tensor(e_qk[:, :, :, sz:2 * sz], b[:, :, :, sz:2 * sz], mid, ALU.subtract).then_inc(lv_d, 1)

                def level_copy(n):
                    dve.wait_ge(lv_mm, (lv0 + (n + 1)).v)
                    if n >= 1:
                        dve.wait_ge(lv_cp, (lv0 + n).v)
                    nc.vector.memset(STAT[:, 62:63], 0.0)
                    nc.vector.copy_predicated(am, MASKS[:, n:n + 1, :].broadcast_to([P, NC_, P]),
                                              BANK[6 + n % 2].rearrange("p (c t) -> p c t", c=NC_)).then_inc(lv_cp, 1)

                level_d(0)
                for n in range(len(LEVELS)):
                    if n + 1 < len(LEVELS):
                        level_d(n + 1)
                    dve.wait_ge(lv_e, (lv0 + (n + 1)).v)
                    nc.vector.tensor_tensor(KQL[n % 2][:], KQ[:, :, 0:T], EL[n % 2][:], ALU.mult).then_inc(lv_k, 1)
                    if n >= 1:
                        level_copy(n - 1)
                level_copy(len(LEVELS) - 1)

            dve.wait_ge(tab2_landed, 32)
            with dve.Fori(0, GH_ // 2) as i:
                for s in range(2):
                    hd, u = At(s, i, 2), At(U_G + 3 * s, i, 6)
                    pa, pb = 2 * (s % 2), 2 * ((s + 1) % 2)
                    split_lo(u + 1)
                    dve.wait_ge(pe_done, (u + 1).v)
                    nc.vector.tensor_copy(KT[:, 0:T], BANK[pa])
                    nc.vector.tensor_copy(KT[:, T:TA], BANK[4 + pa // 2][:, 0:TC])
                    nc.vector.tensor_scalar(QT, BANK[pa + 1], DK ** -0.5, None, ALU.mult).then_inc(evac_done, 1)
                    dve.wait_ge(evac_done, (u + 1).v)
                    decays(hd, 0)
                    split_lo(u + 2)
                    dve.wait_ge(pe_done, (u + 2).v)
                    for n, b in enumerate((pb, pb + 1, 4 + pb // 2)):
                        last = nc.vector.tensor_copy(V[:, 2 * n:2 * n + 2, :].rearrange("p a e -> p (a e)"), BANK[b])
                    last.then_inc(evac_done, 1)
                    states(hd, 0, pb)
                    dve.wait_ge(dg_mm, (hd + 1).v)
                    ident = IDENT[:].rearrange("p (a t) -> p a t", a=1).broadcast_to([P, NC_, P])
                    bank = BANK[4 + pb // 2].rearrange("p (c t) -> p c t", c=NC_)
                    nc.vector.scalar_tensor_tensor(am, bank, 2.0, ident, ALU.mult, ALU.mult).then_inc(dg_made, 1)
                    decays(hd, 1)
                    split_lo(u + 3)
                    states(hd, 1, pb)
                    dve.wait_ge(dg_made, (hd + 1).v)
                    levels(hd)
                    dve.wait_ge(o_rt, (hd + 1).v)
                    nc.vector.reciprocal(STAT[:, 4:8], STAT[:, 0:4]).then_inc(o_rs, 1)
                    dve.wait_ge(o_rs, (hd + 1).v)
                    for c in range(4):
                        last = nc.vector.tensor_scalar(DIAG[:, c, :], IDENT[:], STAT[:, 4 + c:5 + c], None, ALU.mult)
                    last.then_inc(o_diag, 1)
                    dve.wait_ge(o_rb, (hd + 1).v)
                    dve.wait_ge(evac_done, (u + 3).v)
                    for e in range(2):
                        nc.vector.tensor_tensor(O_N[e], O_N[e], BANK[7], ALU.mult).then_inc(o_xr, 1)
                    for e in range(2):
                        dve.wait_ge(o_xr, (hd.times(2) + (e + 1)).v)
                        o = O_T[:, bass.ds((hd.times(2) + e).v, 1), :].rearrange("p a t -> p (a t)")
                        nc.vector.scalar_tensor_tensor(o, O_N[e], vec("gla_norm_2", e), SG[e][:], ALU.mult, ALU.mult).then_inc(o_done, 1)
            split_lo(at(U_K + 1))
            dve.wait_ge(pe_done, U_K + 1)
            assert U_K % 2 == 0
            dve.wait_ge(o_done, 2 * GH_)
            for h in range(NKV):
                nc.vector.tensor_copy(K_RAW[:, h, 0:T], BANK[h])
            nc.vector.tensor_copy(K_RAW[:, :, T:TA], BANK[4].rearrange("p (h t) -> p h t", h=2)).then_inc(k_raw, 1)
            dve.wait_ge(k_raw, 1)
            nc.vector.memset(STAT[:, 63:64], 0.0).then_inc(evac_done, 1)
            dve.wait_ge(pe_done, U_V + 1)
            for n, b in enumerate((2, 3, 5)):
                last = nc.vector.tensor_copy(VA[:, 2 * n:2 * n + 2, :].rearrange("p a e -> p (a e)"), BANK[b])
            last.then_inc(evac_done, 1)
            dve.wait_ge(k_rt, 1)
            nc.vector.reciprocal(STAT[:, 12:24], STAT[:, 0:12]).then_inc(k_rs, 1)
            dve.wait_ge(k_rs, 1)
            for n in range(12):
                last = nc.vector.tensor_scalar(DIAG_K[:, n, :], IDENT[:], STAT[:, 12 + n:13 + n], None, ALU.mult)
            last.then_inc(k_diag, 1)
            dve.wait_ge(k_rb, 1)
            for h in range(NKV):
                nc.vector.scalar_tensor_tensor(K_X[:, h, 0:T], K_RAW[:, h, 0:T], vec("k_norm_2"), BANK[6 + h], ALU.mult, ALU.mult)
                nc.vector.scalar_tensor_tensor(KR[:, h, T:TA], K_RAW[:, h, T:TA], vec("k_norm_2"),
                                               BANK[0][:, TC * h:TC * (h + 1)], ALU.mult, ALU.mult).then_inc(k_x, 1)
            dve.wait_ge(tab3_landed, 48)
            dve.wait_ge(k_rot, 1)
            for h in range(NKV):
                nc.vector.tensor_tensor(KR[:, h, 0:T], K_X[:, h, 0:T], COS[:], ALU.mult).then_inc(k_cos, 1)
                nc.vector.tensor_tensor(TQ[h][:], BANK[6 + h], SIN[:], ALU.mult).then_inc(k_sin, 1)
                dve.wait_ge(k_sin, h + 1)
                nc.vector.tensor_tensor(KR[:, h, 0:T], KR[:, h, 0:T], TQ[h][:], ALU.add).then_inc(k_made, 1)
                dve.wait_ge(k_made, h + 1)
                nc.vector.tensor_copy(K_HI[:, h, :], KR[:, h, :]).then_inc(k_hi_made, 1)
                dve.wait_ge(k_hi_made, h + 1)
                nc.vector.tensor_tensor(K_LO[:, h, :], KR[:, h, :], K_HI[:, h, :].bitcast(F32), ALU.subtract).then_inc(k_ready, 1)
            split_lo(at(U_V + 1))
            with dve.Fori(0, NKV) as kv:
                for ui in range(2):
                    qi, u = At(ui, kv, 2), At(U_Q + ui, kv, 2)
                    pb = 2 * u.slot
                    if ui == 0:
                        nc.vector.tensor_copy(VS[:], VA[:, :, bass.ds(At(0, kv, HD).v, HD)]).then_inc(vs_made, 1)
                    split_lo(u + 1)
                    dve.wait_ge(pe_done, (u + 1).v)
                    dve.wait_ge(q_sq, (qi.times(2) + 2).v)
                    nc.vector.tensor_scalar(QX[0][:], BANK[pb], vec("q_norm_2"), None, ALU.mult)
                    nc.vector.tensor_scalar(QX[1][:], BANK[pb + 1], vec("q_norm_2"), None, ALU.mult).then_inc(evac_done, 1)
                    dve.wait_ge(q_rt, (qi + 1).v)
                    nc.vector.reciprocal(STAT[:, 8:16], STAT[:, 0:8]).then_inc(q_rs, 1)
                    dve.wait_ge(q_rs, (qi + 1).v)
                    nc.vector.tensor_scalar(STAT[:, 16:24], STAT[:, 8:16], HD ** -0.5, None, ALU.mult)
                    nc.vector.tensor_scalar(STAT[:, 24:32], STAT[:, 8:16], -HD ** -0.5, None, ALU.mult).then_inc(q_sc, 1)
                    dve.wait_ge(q_sc, (qi + 1).v)
                    for m in range(2):
                        qm = (qi.times(2) + (m + 1)).v
                        nc.vector.tensor_tensor(QX[m][:], QX[m][:], COS[:], ALU.mult).then_inc(q_cos, 1)
                        nc.vector.tensor_tensor(TQ[m][:], BANK[4 + m], SIN[:], ALU.mult).then_inc(q_sin, 1)
                        dve.wait_ge(q_sin, qm)
                        nc.vector.tensor_tensor(QX[m][:], QX[m][:], TQ[m][:], ALU.add).then_inc(q_sum, 1)
                        dve.wait_ge(q_sum, qm)
                        nc.vector.tensor_copy(Q_HI[m][:], QX[m][:]).then_inc(q_hi_made, 1)
                        dve.wait_ge(q_hi_made, qm)
                        nc.vector.tensor_tensor(Q_LO[m][:], QX[m][:], Q_HI[m][:].bitcast(F32), ALU.subtract).then_inc(q_made, 1)
                    for m in range(2):
                        a = At(2 * ui + m, kv, 4)

                        def bias(c):
                            n = a.times(4) + (c + 1)
                            dve.wait_ge(sc_made, n.v)
                            nc.vector.tensor_reduce(STAT[:, 32 + c % 2:33 + c % 2], WIDE[4 + 2 * (c % 2)], AX.X, ALU.max).then_inc(mx_made, 1)
                            dve.wait_ge(mx_made, n.v)
                            nc.vector.tensor_tensor(STAT[:, 34 + c % 2:35 + c % 2], STAT[:, 32 + c % 2:33 + c % 2],
                                                    STAT[:, 24 + 4 * m + c:25 + 4 * m + c], ALU.mult).then_inc(nb_made, 1)

                        def normalise(c):
                            n = a.times(4) + (c + 1)
                            dve.wait_ge(p_exp, n.v)
                            nc.vector.reciprocal(STAT[:, 38 + c % 2:39 + c % 2], STAT[:, 36 + c % 2:37 + c % 2]).then_inc(p_rr, 1)
                            dve.wait_ge(p_rr, n.v)
                            nc.vector.tensor_scalar(PP[c % 2][:], PP[c % 2][:], STAT[:, 38 + c % 2:39 + c % 2], None, ALU.mult).then_inc(p_norm, 1)

                        bias(0)
                        for c in range(1, 4):
                            bias(c)
                            normalise(c - 1)
                        normalise(3)
                        dve.wait_ge(pv_made, (a + 1).v)
                        at_tile = AT_T[:, bass.ds(a.v, 1), :].rearrange("p a t -> p (a t)")
                        nc.vector.tensor_copy(at_tile, BANK[4]).then_inc(at_made, 1)
            for k in range(KD):
                dve.wait_ge(a_hi_made, k + 1)
                nc.vector.tensor_tensor(A_LO[:, k, :], AT_T[:, k, :], A_HI[:, k, :].bitcast(F32), ALU.subtract).then_inc(a_ready, 1)
            dve.wait_ge(a_ready, KD)
            for k in range(KD):
                dve.wait_ge(a_hi_made, KD + k + 1)
                nc.vector.tensor_tensor(L_LO[:, k, :], O_T[:, k, :], L_HI[:, k, :].bitcast(F32), ALU.subtract).then_inc(a_ready, 1)
            with dve.Fori(0, KD) as i:
                u = At(U_D, i, 2)
                m = At(0, i, 1)
                y = Y[:, bass.ds(m.v, 1), :].rearrange("p a t -> p (a t)")
                split_lo(u + 1)
                dve.wait_ge(evac_done, (u + 1).v)
                split_lo(u + 2)
                dve.wait_ge(pe_done, (u + 2).v)
                nc.vector.tensor_tensor(y, SGB[0][:], BANK[2], ALU.mult).then_inc(y_a, 1)
                nc.vector.tensor_tensor(SGB[1][:], SGB[1][:], BANK[3], ALU.mult).then_inc(y_g, 1)
                dve.wait_ge(y_g, (m + 1).v)
                nc.vector.tensor_tensor(y, y, SGB[1][:], ALU.add).then_inc(evac_done, 1)
            for k in range(KD):
                dve.wait_ge(y_hi_made, k + 1)
                nc.vector.tensor_tensor(H_LO[:, k, 0:T], Y[:, k, :], H_HI[:, k, 0:T].bitcast(F32), ALU.subtract).then_inc(y_ready, 1)

            def out_pair(j):
                u = j + U_WO
                split_lo(u + 1)
                if j.i is None and j.base == 3:
                    square_sums(8, range(6))
                dve.wait_ge(pe_done, (u + 1).v)
                for a in range(2):
                    last = add_branch(j.times(2) + a, BANK[2 * u.slot + a], 6)
                last.then_inc(evac_done, 1)

            each(dve, 4, 0, 2, out_pair)
            norm_split(8, 7, None, (6, 7))

            def quarter(q, last_one=False):
                for j in range(4):
                    u = q.times(8) + (U_MLP + j)
                    split_lo(u + 1)
                    for m in range(2):
                        t = 2 * j + m
                        n = q.times(8) + (t + 1)
                        dve.wait_ge(relu_made, n.v)
                        mul = nc.vector.tensor_tensor(GT[m][:], SA[m][:], BANK[2 * u.slot + m], ALU.mult)
                        if m == 1:
                            mul.then_inc(evac_done, 1)
                            dve.wait_ge(evac_done, (u + 1).v)
                        else:
                            mul.then_inc(y_a, 1)
                            dve.wait_ge(y_a, (q.times(4) + (KD + j + 1)).v)
                        nc.vector.tensor_copy(G_HI[:, t, :], GT[m][:]).then_inc(m_hi_made, 1)
                        dve.wait_ge(m_hi_made, n.v)
                        nc.vector.tensor_tensor(G_LO[:, t, :], GT[m][:], G_HI[:, t, :].bitcast(F32), ALU.subtract).then_inc(m_ready, 1)
                for j in range(4):
                    u = q.times(8) + (U_MLP + 4 + j)
                    if not (last_one and j == 3):
                        split_lo(u + 1)
                    dve.wait_ge(pe_done, (u + 1).v)
                    for m in range(2):
                        last = add_branch(at(2 * j + m), BANK[2 * u.slot + m], 7)
                    last.then_inc(evac_done, 1)

            with dve.Fori(0, 3) as i:
                quarter(At(0, i, 1))
            quarter(at(3), True)

        @block.tensor
        def _(pe):
            def products(u, kt, tiles, rhs_hi, rhs_lo, ready=None, banks=None, cols=T, bank_cols=0, first=True):
                if first:
                    pe.wait_ge(lo_done, (u + 1).v)
                    wait(pe, evac_done, u - 1)
                banks = banks or [BANK[2 * u.slot + m] for m in range(tiles)]
                n = kt * tiles * P
                hi = W_HI[u.slot][:, 0:n].rearrange("p (k m) -> p k m", k=kt)
                lo = W_LO[u.slot][:, 0:n].rearrange("p (k m) -> p k m", k=kt)
                for k in range(kt):
                    if ready:
                        ready(k)
                    for m in range(tiles):
                        dst = banks[m][:, bank_cols:bank_cols + cols]
                        c = slice(m * P, (m + 1) * P)
                        pe.matmul(dst, hi[:, k, c], rhs_hi(k), start=(k == 0), stop=False)
                        pe.matmul(dst, hi[:, k, c], rhs_lo(k), start=False, stop=False)
                        last = pe.matmul(dst, lo[:, k, c], rhs_hi(k), start=False, stop=(k == kt - 1))
                return last

            def h_part(b, a=0, n=T):
                return lambda k: b[:, k, a:a + n]

            def mod_sums(g):
                for h in range(2):
                    pe.wait_ge(ada_used[h], 8 * g + 8)
                wait(pe, mod_read, at(MOD_READ.get(g - 1, 0)))
                for t in range(24):
                    last = pe.matmul(BANK[7][:, t:t + 1], ACC[:, t * P:(t + 1) * P], ONES[:, 0:1], start=True, stop=True)
                if g == 6:
                    for t in range(16):
                        last = pe.matmul(BANK[7][:, 24 + t:25 + t], ACC_C[:, t * P:(t + 1) * P], ONES[:, 0:1], start=True, stop=True)
                last.then_inc(mod_summed, 1)

            def norm(r):
                pe.wait_ge(sq_summed, KD * (r + 1))
                for c in range(4):
                    last = pe.matmul(BANK[6][:, c:c + 1], SSQ[:, c * P:(c + 1) * P], ONES_D[:, 0:1], start=True, stop=True)
                last.then_inc(ms_made, 1)
                pe.wait_ge(diag_made, 4 * (r + 1))
                pe.matmul(BANK[5][:], ONES[:], DIAG[:].rearrange("p c t -> p (c t)"), start=True, stop=True).then_inc(rb_made, 1)

            def ffn(f):
                for half in range(2):
                    g = FFN_GROUPS[f][half]
                    base = U_FFN[f] + half * (IN_UNITS + OUT_UNITS)
                    q0 = (2 * f + half) * FH
                    pe.wait_ge(lo_done, base + 1)
                    if half == 0:
                        pe.wait_ge(h_ready, H_BASE[FFN_NORM[f]] + 1)

                    def in_unit(j):
                        ready = None
                        if half == 0 and j.base == 0 :
                            ready = lambda k: pe.wait_ge(h_ready, H_BASE[FFN_NORM[f]] + k + 1)
                        products(j + base, KD, 2, h_part(H_HI), h_part(H_LO), ready).then_inc(pe_done, 1)

                    each(pe, IN_UNITS, 2, 1, in_unit)

                    def out_unit(m):
                        ready = (lambda k: pe.wait_ge(g_ready, q0 + k + 1)) if m.base == 0 else None
                        products(m + (base + IN_UNITS), FH, 1, h_part(G_HI), h_part(G_LO), ready).then_inc(pe_done, 1)
                        if g is not None and m.i is None and m.base == 1:
                            mod_sums(g)

                    each(pe, OUT_UNITS, 2, 2, out_unit)

            pe.wait_ge(tab_landed, 16)
            pe.wait_ge(vec_landed, 16 * N_VEC_DMAS)
            for t in range(NVT):
                n = min(P, NVEC - t * P)
                last = pe.transpose(BANK[6][:, t * P:t * P + n], V_ROWS[0:n, t, :], IDENT[0:n, 0:n])
            last.then_inc(vec_turned, 1)
            pe.wait_ge(in_landed, 16)
            for k in range(KD):
                wait(pe, x_made, at(k - 3))
                for c in range(4):
                    last = pe.transpose(BANK[k % 4][:, c * P:(c + 1) * P], X_ROWS[:, c, k * P:(k + 1) * P], IDENT[:])
                last.then_inc(x_turned, 1)
            pe.wait_ge(const_ready, 3)
            pe.wait_ge(vec_ready, 1)
            mod_sums(0)
            norm(0)
            ffn(0)
            norm(1)
            pe.wait_ge(lo_done, U_POOL + 1)
            hi = W_HI[U_POOL % 2][:].rearrange("p (g k m) -> p g k m", g=4, k=2)
            lo = W_LO[U_POOL % 2][:].rearrange("p (g k m) -> p g k m", g=4, k=2)
            for gi in range(4):
                pe.wait_ge(p_ready, 2 * gi + 2)
                if gi >= 2:
                    pe.wait_ge(pool_added, gi - 1)
                for m in range(2):
                    dst = BANK[2 * (gi % 2) + m][:]
                    for k in range(2):
                        kk, cc = 2 * gi + k, slice(m * P, (m + 1) * P)
                        pe.matmul(dst, hi[:, gi, k, cc], H_HI[:, kk, 0:T], start=(k == 0), stop=False)
                        pe.matmul(dst, hi[:, gi, k, cc], H_LO[:, kk, 0:T], start=False, stop=False)
                        last = pe.matmul(dst, lo[:, gi, k, cc], H_HI[:, kk, 0:T], start=False, stop=(k == 1))
                last.then_inc(pool_mm if gi < 3 else pe_done, 1)
            norm(2)
            ffn(1)
            norm(3)
            ffn(2)
            norm(4)

            def cv_unit(j):
                ready = (lambda k: pe.wait_ge(h_ready, H_BASE[4] + k + 1)) if j.base == 0 else None
                products(j + U_CONV, KD, 2, h_part(H_HI), h_part(H_LO), ready).then_inc(pe_done, 1)

            each(pe, 8, 2, 0, cv_unit)
            each(pe, 4, 0, 0, lambda j: products(j + (U_CONV + 8), KD, 2, h_part(H_HI), h_part(H_LO)).then_inc(pe_done, 1))

            def out_pair(j):
                ready = (lambda k: pe.wait_ge(z_ready, k + 1)) if j.base == 0 else None
                products(j + (U_CONV + 12), KD, 2, h_part(Z_HI), h_part(Z_LO), ready).then_inc(pe_done, 1)

            each(pe, 4, 0, 2, out_pair)
            norm(5)
            ffn(3)
            norm(6)
            norm(7)
            pe.wait_ge(c_landed, 16)
            for k in range(KD):
                for c in range(2):
                    last = pe.transpose(BANK[k // 2][:, TC * (k % 2) + c * P:TC * (k % 2) + (c + 1) * P], C_ROWS[:, c, k * P:(k + 1) * P], IDENT[:])
                last.then_inc(c_turned, 1)
            pe.wait_ge(csq_summed, KD)
            for c in range(2):
                last = pe.matmul(BANK[7][:, c:c + 1], SSQ[:, c * P:(c + 1) * P], ONES_D[:, 0:1], start=True, stop=True)
            last.then_inc(cms_made, 1)
            pe.wait_ge(cdiag_made, 2)
            for c in range(2):
                last = pe.matmul(BANK[6][:, c * P:(c + 1) * P], ONES[:], DIAG[:, c, :], start=True, stop=True)
            last.then_inc(crb_made, 1)
            pe.wait_ge(h_ready, H_BASE[7] + 2 * KD)

            def exact(dst, a_hi, a_lo, b_hi, b_lo, first, last):
                pe.matmul(dst, a_hi, b_hi, start=first, stop=False)
                pe.matmul(dst, a_hi, b_lo, start=False, stop=False)
                return pe.matmul(dst, a_lo, b_hi, start=False, stop=last)

            def ctx_products(u, cols, width, dst):
                hi = W_HI[u.slot][:, 0:KD * width].rearrange("p (k m) -> p k m", k=KD)
                lo = W_LO[u.slot][:, 0:KD * width].rearrange("p (k m) -> p k m", k=KD)
                for k in range(KD):
                    last = exact(dst, hi[:, k, cols], lo[:, k, cols], H_HI[:, k, T:TA], H_LO[:, k, T:TA], k == 0, k == KD - 1)
                return last

            def token_products(u, banks):
                pe.wait_ge(lo_done, (u + 1).v)
                wait(pe, evac_done, u - 1)
                hi = W_HI[u.slot][:].rearrange("p (k m) -> p k m", k=KD)
                lo = W_LO[u.slot][:].rearrange("p (k m) -> p k m", k=KD)
                for t in range(TA // P):
                    dst = banks[t // 2][:, DV * (t % 2):DV * (t % 2 + 1)]
                    for k in range(KD):
                        last = exact(dst, H_HI[:, k, t * P:(t + 1) * P], H_LO[:, k, t * P:(t + 1) * P], hi[:, k, :], lo[:, k, :], k == 0, k == KD - 1)
                return last

            u = at(U_LR)
            r = slice(0, 2 * RANK)
            pe.wait_ge(lo_done, U_LR + 1)
            pe.wait_ge(evac_done, U_LR)
            hi = W_HI[u.slot][:, 0:KD * 2 * RANK].rearrange("p (k m) -> p k m", k=KD)
            lo = W_LO[u.slot][:, 0:KD * 2 * RANK].rearrange("p (k m) -> p k m", k=KD)
            for dst, a, b in ((BANK[2 * u.slot][r, :], 0, T), (BANK[4 + u.slot][r, 0:TC], T, TA)):
                for k in range(KD):
                    last = exact(dst, hi[:, k, :], lo[:, k, :], H_HI[:, k, a:b], H_LO[:, k, a:b], k == 0, k == KD - 1)
            last.then_inc(pe_done, 1)

            with pe.Fori(0, GH_ // 2) as i:
                for s in range(2):
                    hd, u = At(s, i, 2), At(U_G + 3 * s, i, 6)
                    pa, pb = 2 * (s % 2), 2 * ((s + 1) % 2)
                    products(u, KD, 2, h_part(H_HI), h_part(H_LO))
                    ctx_products(u, slice(0, P), 2 * P, BANK[4 + pa // 2][:, 0:TC]).then_inc(pe_done, 1)

                    def gate_z(d):
                        for a, b in ((0, T), (T, TA)):
                            last = pe.matmul(PS[:, 6 * T + a:6 * T + b], W_GK[0:2 * RANK, d, :], LRT[0:2 * RANK, a:b], start=True, stop=True)
                        last.then_inc(z_made, 1)

                    def states(d):
                        zd = hd.times(2) + (d + 1)
                        pe.wait_ge(kd_made, zd.v)
                        for t in range(TA // P):
                            last = pe.transpose(PS[:, 6 * T + t * P:6 * T + (t + 1) * P], T2[:, t * P:(t + 1) * P], IDENT[:])
                        last.then_inc(kdt_t, 1)
                        pe.wait_ge(kdt_made, zd.v)
                        for n, c in enumerate((0, 1, 2) if d == 0 else (3, 2, 1)):
                            pe.matmul(PS[:, pb * T + n * DV:pb * T + (n + 1) * DV], KDT[:, c, :], V[:, c, :], start=True, stop=True)
                        for t in (4, 5):
                            last = pe.matmul(PS[:, pb * T + 3 * DV:pb * T + 4 * DV], KDT[:, t, :], V[:, t, :], start=(t == 4), stop=(t == 5))
                        last.then_inc(sp_made, 1)

                    pe.wait_ge(evac_done, (u + 1).v)
                    pe.wait_ge(wgk_landed, (hd.times(32) + 32).v)
                    gate_z(0)
                    token_products(u + 1, [BANK[pb], BANK[pb + 1], BANK[4 + pb // 2]]).then_inc(pe_done, 1)
                    pe.wait_ge(evac_done, (u + 2).v)
                    for c in range(NC_):
                        cc = slice(c * CH, (c + 1) * CH)
                        last = pe.matmul(BANK[4 + pb // 2][:, cc], KT[:, cc], QT[:, cc], start=True, stop=True)
                    last.then_inc(dg_mm, 1)
                    states(0)
                    pe.wait_ge(st_made, (hd.times(8) + 4).v)
                    gate_z(1)
                    products(u + 2, KD, 2, h_part(H_HI), h_part(H_LO)).then_inc(pe_done, 1)
                    states(1)
                    for n in range(len(LEVELS)):
                        lv = hd.times(len(LEVELS)) + (n + 1)
                        pe.wait_ge(lv_k, lv.v)
                        if n >= 2:
                            pe.wait_ge(lv_cp, (lv - 2).v)
                        for c in range(NC_):
                            cc = slice(c * CH, (c + 1) * CH)
                            last = pe.matmul(BANK[6 + n % 2][:, cc], KQL[n % 2][:, 0, cc], KQL[n % 2][:, 1, cc], start=True, stop=True)
                        last.then_inc(lv_mm, 1)
                    pe.wait_ge(st_made, (hd.times(8) + 8).v)
                    pe.wait_ge(lv_cp, (hd.times(len(LEVELS)) + len(LEVELS)).v)
                    for e in range(2):
                        ee = slice(e * P, (e + 1) * P)
                        for c in range(NC_):
                            cc = slice(c * CH, (c + 1) * CH)
                            dst = BANK[pb + e][:, cc]
                            pe.matmul(dst, V[:, c, ee], AM[:, cc], start=True, stop=False)
                            pe.matmul(dst, ST[0][:, c, ee], QB[0][:, cc], start=False, stop=False)
                            last = pe.matmul(dst, ST[1][:, c, ee], QB[1][:, cc], start=False, stop=True)
                    last.then_inc(o_mm, 1)
                    pe.wait_ge(o_sq, (hd.times(2) + 2).v)
                    for c in range(NC_):
                        for e in range(2):
                            last = pe.matmul(BANK[6][:, c:c + 1], O_SQ[e][:, c * CH:(c + 1) * CH], ONES_D[:, 1:2], start=(e == 0), stop=(e == 1))
                    last.then_inc(o_ms, 1)
                    pe.wait_ge(o_diag, (hd + 1).v)
                    pe.matmul(BANK[7], ONES[:], DIAG[:].rearrange("p c t -> p (c t)"), start=True, stop=True).then_inc(o_rb, 1)
            u = at(U_K)
            products(u, KD, 2, h_part(H_HI), h_part(H_LO))
            for h in range(NKV):
                last = ctx_products(u, slice(h * P, (h + 1) * P), 2 * P, BANK[4][:, TC * h:TC * (h + 1)])
            last.then_inc(pe_done, 1)
            token_products(at(U_V), [BANK[2], BANK[3], BANK[5]]).then_inc(pe_done, 1)
            pe.wait_ge(k_sq, 2)
            pe.wait_ge(o_done, 2 * GH_)
            for h in range(NKV):
                for t in range(6):
                    last = pe.matmul(BANK[6][:, 6 * h + t:6 * h + t + 1], K_SQ[:, h, t * P:(t + 1) * P], ONES_HD[:, 0:1], start=True, stop=True)
            last.then_inc(k_ms, 1)
            pe.wait_ge(k_diag, 1)
            for h in range(NKV):
                for t in range(6):
                    dst = BANK[6 + h][:, t * P:(t + 1) * P] if t < 4 else BANK[0][:, TC * h + (t - 4) * P:TC * h + (t - 3) * P]
                    last = pe.matmul(dst, ONES[:], DIAG_K[:, 6 * h + t, :], start=True, stop=True)
            last.then_inc(k_rb, 1)
            pe.wait_ge(k_x, 2)
            pe.wait_ge(tab3_landed, 48)
            for h in range(NKV):
                last = pe.matmul(BANK[6 + h], PERM[:], K_X[:, h, 0:T], start=True, stop=True)
            last.then_inc(k_rot, 1)
            pe.wait_ge(k_ready, 2)
            with pe.Fori(0, NKV) as kv:
                for ui in range(2):
                    qi, u = At(ui, kv, 2), At(U_Q + ui, kv, 2)
                    pe.wait_ge(vs_made, At(1, kv, 1).v)
                    if ui == 1:
                        pe.wait_ge(at_made, At(2, kv, 4).v)
                    products(u, KD, 2, h_part(H_HI), h_part(H_LO)).then_inc(pe_done, 1)
                    pe.wait_ge(q_sq, (qi.times(2) + 2).v)
                    for m in range(2):
                        for c in range(4):
                            last = pe.matmul(BANK[6][:, 4 * m + c:4 * m + c + 1], Q_SQ[m][:, c * P:(c + 1) * P], ONES_HD[:, 0:1], start=True, stop=True)
                    pe.wait_ge(evac_done, (u + 1).v)
                    for m in range(2):
                        last = pe.matmul(BANK[4 + m], PERM[:], QX[m][:], start=True, stop=True)
                    last.then_inc(q_rot, 1)
                    for m in range(2):
                        a = At(2 * ui + m, kv, 4)

                        def scores(c):
                            n = a.times(4) + c
                            if c >= 2 or m == 1:
                                pe.wait_ge(p_exp, (n - 1).v)
                            if c == 0:
                                pe.wait_ge(q_made, (qi.times(2) + 2).v)
                                if m == 1:
                                    pe.wait_ge(at_made, a.v)
                            cc = slice(c * P, (c + 1) * P)
                            for x0, x1 in ((0, T), (T, TA)):
                                keys = [b[:, bass.ds(At(0, kv, 1).v, 1), x0:x1].rearrange("p a t -> p (a t)") for b in (K_HI, K_LO)]
                                last = exact(WIDE[4 + 2 * (c % 2)][:, x0:x1], Q_HI[m][:, cc], Q_LO[m][:, cc], *keys, True, True)
                            last.then_inc(sc_made, 1)

                        def turn(c):
                            n = a.times(4) + c
                            pe.wait_ge(p_norm, (n + 1).v)
                            if c >= 2 or m == 1:
                                pe.wait_ge(pt_made, (n - 1).v)
                            for t in range(6):
                                last = pe.transpose(WIDE[2 * (c % 2)][:, t * P:(t + 1) * P], PP[c % 2][:, t * P:(t + 1) * P], IDENT[:])
                            last.then_inc(p_t, 1)

                        scores(0)
                        for c in range(1, 4):
                            scores(c)
                            turn(c - 1)
                        turn(3)
                        pe.wait_ge(pt_made, (a.times(4) + 4).v)
                        for t in range(6):
                            last = pe.matmul(BANK[4], VS[:, t, :], PT[:, t, :], start=(t == 0), stop=(t == 5))
                        last.then_inc(pv_made, 1)
            pe.wait_ge(at_made, NQ)
            with pe.Fori(0, KD) as i:
                u = At(U_D, i, 2)
                products(u, KD, 2, h_part(H_HI), h_part(H_LO)).then_inc(pe_done, 1)
                u = u + 1
                pe.wait_ge(lo_done, (u + 1).v)
                pe.wait_ge(evac_done, (u - 1).v)
                hi = W_HI[u.slot][:].rearrange("p (k m) -> p k m", k=KD)
                lo = W_LO[u.slot][:].rearrange("p (k m) -> p k m", k=KD)
                for m, (x_hi, x_lo) in enumerate(((A_HI, A_LO), (L_HI, L_LO))):
                    mm = slice(m * P, (m + 1) * P)
                    for k in range(KD):
                        pe.wait_ge(a_ready, KD * m + k + 1)
                        last = exact(BANK[2 + m], hi[:, k, mm], lo[:, k, mm], x_hi[:, k, :], x_lo[:, k, :], k == 0, k == KD - 1)
                last.then_inc(pe_done, 1)

            def out_pair(j):
                ready = (lambda k: pe.wait_ge(y_ready, k + 1)) if j.base == 0 else None
                products(j + U_WO, KD, 2, h_part(H_HI), h_part(H_LO), ready).then_inc(pe_done, 1)

            each(pe, 4, 0, 2, out_pair)
            norm(8)

            def quarter(q):
                for j in range(4):
                    ready = (lambda k: pe.wait_ge(h_ready, H_BASE[8] + k + 1)) if j == 0 else None
                    products(q.times(8) + (U_MLP + j), KD, 2, h_part(H_HI), h_part(H_LO), ready).then_inc(pe_done, 1)
                for j in range(4):
                    ready = (lambda k: pe.wait_ge(m_ready, (q.times(8) + (k + 1)).v)) if j == 0 else None
                    products(q.times(8) + (U_MLP + 4 + j), KD, 2, h_part(G_HI), h_part(G_LO), ready).then_inc(pe_done, 1)

            with pe.Fori(0, 3) as i:
                quarter(At(0, i, 1))
            quarter(at(3))
            pe.wait_ge(evac_done, N_UNITS)
            for c in range(4):
                wait(pe, out_made, at(c - 1))
                for f in range(KD):
                    last = pe.transpose(PS[:, 2 * T * (c % 2) + f * P:2 * T * (c % 2) + (f + 1) * P], X[:, f, c * P:(c + 1) * P], IDENT[:])
                last.then_inc(row_t, 1)


INPUTS = ("x", "c", "ada_w", "ada_b", "norm_g", "ffn_w_in", "ffn_w_out", "pool_w", "pool_scale",
          "conv_w_in", "conv_w", "conv_w_out", "final_g", "c_2", "ctx_2", "c_ctx_2", "w_ada_2",
          "b_ada_2", "norm1_2", "w_in_2", "q_norm_2", "k_norm_2", "w_gk_fwd_2", "b_gk_fwd_2",
          "w_gk_bwd_2", "b_gk_bwd_2", "gla_norm_2", "w_br_attn_2", "w_br_gla_2", "w_out_2",
          "norm2_2", "w_mlp1_2", "w_mlp2_2")


def kernel(**inputs):
    from concourse import bacc
    from concourse.bass_utils import run_bass_kernel_spmd

    nc = bacc.Bacc("TRN2", target_bir_lowering=False, num_devices=1)
    arrays, args = {}, {}
    for name, a in list((n, inputs[n]) for n in INPUTS) + list(host_tables().items()):
        a = np.ascontiguousarray(a)
        arrays[f"in_{name}"] = a
        args[name] = nc.dram_tensor(f"in_{name}", a.shape, mybir.dt.from_np(a.dtype), kind="ExternalInput").ap()
    out = nc.dram_tensor("out_0", (1, T, D), F32, kind="ExternalOutput").ap()
    build(nc, args, out[0])
    got = run_bass_kernel_spmd(nc, [arrays], core_ids=[0])
    return got.results[0]["out_0"]
```
